# Optimizing a Trainium2 kernel written in Bass

```python
import math
import jax, jax.numpy as jnp
from jax import lax
import numpy as np

D_MODEL = 1024
BATCH = 1
SEQ = 512
DEPTH = 2

CHUNK = 64
Q_BLOCK = 128
N_MIXERS = 2
DIFF_HEADS = 8
DIFF_HEAD_DIM = D_MODEL // (2 * DIFF_HEADS)
SB_HEADS = 16
SB_HEAD_DIM = D_MODEL // SB_HEADS
N_GROUPS = 4
EXPERTS_PER_GROUP = 8
N_EXPERTS = N_GROUPS * EXPERTS_PER_GROUP
TOP_K = 2
EXPERT_HIDDEN = D_MODEL // 2
MOE_BLOCK = 128
RMS_EPS = 1e-6
SUBLN_EPS = 1e-5


def rms_norm(x, g, eps=RMS_EPS):
    xf = x.astype(jnp.float32)
    y = xf * lax.rsqrt(jnp.mean(xf * xf, axis=-1, keepdims=True) + eps)
    return (y * g.astype(jnp.float32)).astype(x.dtype)

def alibi_slopes(n_heads):
    return jnp.exp2(-8.0 * jnp.arange(1, n_heads + 1, dtype=jnp.float32) / n_heads)

def diff_attention(h, w_in, w_out, lq1, lk1, lq2, lk2, subln_g, lambda_init):
    B, S, D = h.shape
    H, d = DIFF_HEADS, DIFF_HEAD_DIM
    q, k, v = jnp.split(h @ w_in, 3, axis=-1)
    q = q.reshape(B, S, H, 2, d)
    k = k.reshape(B, S, H, 2, d)
    v = v.reshape(B, S, H, 2 * d)
    lam = (jnp.exp(jnp.sum(lq1.astype(jnp.float32) * lk1.astype(jnp.float32)))
           - jnp.exp(jnp.sum(lq2.astype(jnp.float32) * lk2.astype(jnp.float32)))
           + lambda_init)
    slopes = alibi_slopes(H)[None, :, None, None, None]
    scale = 1.0 / math.sqrt(d)
    pos = jnp.arange(S, dtype=jnp.int32)
    outs = []
    for i in range(S // Q_BLOCK):
        q0, q1 = i * Q_BLOCK, (i + 1) * Q_BLOCK
        qb, kb, vb = q[:, q0:q1], k[:, :q1], v[:, :q1]
        tq, tk = pos[q0:q1], pos[:q1]
        s = jnp.einsum('bqhmd,bkhmd->bhmqk', qb, kb).astype(jnp.float32) * scale
        dist = jnp.abs(tq[:, None] - tk[None, :]).astype(jnp.float32)
        allowed = (tk[None, :] // CHUNK) <= (tq[:, None] // CHUNK)
        s = jnp.where(allowed, s - slopes * dist, -jnp.inf)
        p = jax.nn.softmax(s, axis=-1)
        a = p[:, :, 0] - lam * p[:, :, 1]
        outs.append(jnp.einsum('bhqk,bkhe->bqhe', a.astype(vb.dtype), vb))
    o = jnp.concatenate(outs, axis=1)
    o = rms_norm(o, subln_g, SUBLN_EPS) * (1.0 - lambda_init)
    return o.reshape(B, S, D) @ w_out

def stick_breaking_attention(h, w_in, w_out):
    B, S, D = h.shape
    H, d = SB_HEADS, SB_HEAD_DIM
    q, k, v = jnp.split(h @ w_in, 3, axis=-1)
    q = q.reshape(B, S, H, d)
    k = k.reshape(B, S, H, d)
    v = v.reshape(B, S, H, d)
    scale = 1.0 / math.sqrt(d)
    pos = jnp.arange(S, dtype=jnp.int32)
    outs = []
    for i in range(S // Q_BLOCK):
        q0, q1 = i * Q_BLOCK, (i + 1) * Q_BLOCK
        qb, kb, vb = q[:, q0:q1], k[:, :q1], v[:, :q1]
        tq, tk = pos[q0:q1], pos[:q1]
        z = jnp.einsum('bqhd,bkhd->bhqk', qb, kb).astype(jnp.float32) * scale
        strict = tk[None, :] < tq[:, None]
        log_fail = jnp.where(strict, jax.nn.log_sigmoid(-z), 0.0)
        between = lax.cumsum(log_fail, axis=log_fail.ndim - 1, reverse=True) - log_fail
        a = jnp.where(strict, jnp.exp(jax.nn.log_sigmoid(z) + between), 0.0)
        outs.append(jnp.einsum('bhqk,bkhd->bqhd', a.astype(vb.dtype), vb))
    o = jnp.concatenate(outs, axis=1)
    return o.reshape(B, S, D) @ w_out

def expert_dispatch(xf, expert_ids, weights, w_gate, w_up, w_down):
    N, D = xf.shape
    NK = expert_ids.shape[0]
    n_slots = NK + N_EXPERTS * MOE_BLOCK
    n_blocks = n_slots // MOE_BLOCK
    token_ids = jnp.arange(NK, dtype=jnp.int32) // TOP_K
    order = jnp.argsort(expert_ids)
    e_sorted = expert_ids[order]
    counts = jnp.zeros((N_EXPERTS,), jnp.int32).at[expert_ids].add(1)
    padded = (counts + MOE_BLOCK - 1) // MOE_BLOCK * MOE_BLOCK
    starts = jnp.cumsum(counts) - counts
    pad_ends = jnp.cumsum(padded)
    pad_starts = pad_ends - padded
    rank = jnp.arange(NK, dtype=jnp.int32) - starts[e_sorted]
    dest = pad_starts[e_sorted] + rank
    slot_tok = jnp.full((n_slots,), N, jnp.int32).at[dest].set(token_ids[order])
    slot_w = jnp.zeros((n_slots,), jnp.float32).at[dest].set(weights[order])
    block_start = jnp.arange(n_blocks, dtype=jnp.int32) * MOE_BLOCK
    block_expert = jnp.minimum(jnp.searchsorted(pad_ends, block_start, side='right'),
                               N_EXPERTS - 1).astype(jnp.int32)
    x_pad = jnp.concatenate([xf, jnp.zeros((1, D), xf.dtype)], axis=0)
    xs = x_pad[slot_tok].reshape(n_blocks, MOE_BLOCK, D)

    def run_block(args):
        xb, e = args
        hid = jax.nn.silu(xb @ w_gate[e]) * (xb @ w_up[e])
        return hid @ w_down[e]

    ys = lax.map(run_block, (xs, block_expert)).reshape(n_slots, D)
    ys = ys * slot_w[:, None].astype(ys.dtype)
    out = jnp.zeros((N + 1, D), ys.dtype).at[slot_tok].add(ys)
    return out[:N]

def hierarchical_moe(h, w_group, b_group, w_expert, b_expert, w_gate, w_up, w_down):
    B, S, D = h.shape
    N = B * S
    xf = h.reshape(N, D)
    rows = jnp.arange(N, dtype=jnp.int32)
    g_logits = (xf @ w_group).astype(jnp.float32) + b_group.astype(jnp.float32)
    g_prob = jax.nn.softmax(g_logits, axis=-1)
    g_idx = jnp.argmax(g_logits, axis=-1).astype(jnp.int32)
    g_w = g_prob[rows, g_idx][:, None]
    e_all = ((xf @ w_expert).astype(jnp.float32).reshape(N, N_GROUPS, EXPERTS_PER_GROUP)
             + b_expert.astype(jnp.float32))
    e_logits = e_all[rows, g_idx]
    top_v, top_i = lax.top_k(e_logits, TOP_K)
    e_w = jax.nn.softmax(top_v, axis=-1)
    weights = (g_w * e_w).reshape(-1)
    expert_ids = (g_idx[:, None] * EXPERTS_PER_GROUP + top_i.astype(jnp.int32)).reshape(-1)
    y = expert_dispatch(xf, expert_ids, weights, w_gate, w_up, w_down)
    return y.reshape(B, S, D)

def first_inputs(seed: int = 0) -> dict:
    key = jax.random.key(seed)
    ks = jax.random.split(key, 24)
    D, F, E = D_MODEL, EXPERT_HIDDEN, N_EXPERTS
    nA = (DEPTH + 1) // 2
    nB = DEPTH // 2
    dA = DIFF_HEAD_DIM
    nrm = jax.random.normal
    f32 = jnp.float32
    inv = D ** -0.5
    return {
        "x": nrm(ks[0], (BATCH, SEQ, D), f32),
        "c": nrm(ks[1], (BATCH, D), f32),
        "norm1_g": 1.0 + 0.02 * nrm(ks[2], (DEPTH, D), f32),
        "norm2_g": 1.0 + 0.02 * nrm(ks[3], (DEPTH, D), f32),
        "ada_w": 0.5 * inv * nrm(ks[4], (DEPTH, D, 6 * D), f32),
        "ada_b": 0.01 * nrm(ks[5], (DEPTH, 6 * D), f32),
        "diff_w_in": inv * nrm(ks[6], (nA, D, 3 * D), f32),
        "diff_w_out": inv * nrm(ks[7], (nA, D, D), f32),
        "diff_lambda_q1": 0.1 * nrm(ks[8], (nA, dA), f32),
        "diff_lambda_k1": 0.1 * nrm(ks[9], (nA, dA), f32),
        "diff_lambda_q2": 0.1 * nrm(ks[10], (nA, dA), f32),
        "diff_lambda_k2": 0.1 * nrm(ks[11], (nA, dA), f32),
        "diff_subln_g": 1.0 + 0.02 * nrm(ks[12], (nA, 2 * dA), f32),
        "sb_w_in": inv * nrm(ks[13], (nB, D, 3 * D), f32),
        "sb_w_out": inv * nrm(ks[14], (nB, D, D), f32),
        "router_group_w": inv * nrm(ks[15], (DEPTH, D, N_GROUPS), f32),
        "router_group_b": 0.01 * nrm(ks[16], (DEPTH, N_GROUPS), f32),
        "router_expert_w": inv * nrm(ks[17], (DEPTH, D, N_GROUPS * EXPERTS_PER_GROUP), f32),
        "router_expert_b": 0.01 * nrm(ks[18], (DEPTH, N_GROUPS, EXPERTS_PER_GROUP), f32),
        "expert_w_gate": inv * nrm(ks[19], (DEPTH, E, D, F), f32),
        "expert_w_up": inv * nrm(ks[20], (DEPTH, E, D, F), f32),
        "expert_w_down": (F ** -0.5) * nrm(ks[21], (DEPTH, E, F, D), f32),
        "final_norm_g": 1.0 + 0.02 * nrm(ks[22], (D,), f32),
    }

def first_block(x, c, norm1_g, norm2_g, ada_w, ada_b, diff_w_in, diff_w_out,
              diff_lambda_q1, diff_lambda_k1, diff_lambda_q2, diff_lambda_k2, diff_subln_g,
              sb_w_in, sb_w_out, router_group_w, router_group_b, router_expert_w,
              router_expert_b, expert_w_gate, expert_w_up, expert_w_down, final_norm_g):
    cond = jax.nn.silu(c)
    for i in range(DEPTH):
        mod = cond @ ada_w[i] + ada_b[i]
        sh1, sc1, g1, sh2, sc2, g2 = jnp.split(mod[:, None, :], 6, axis=-1)
        h = rms_norm(x, norm1_g[i]) * (1.0 + sc1) + sh1
        j = i // N_MIXERS
        if i % N_MIXERS == 0:
            lambda_init = 0.8 - 0.6 * math.exp(-0.3 * i)
            y = diff_attention(h, diff_w_in[j], diff_w_out[j], diff_lambda_q1[j],
                               diff_lambda_k1[j], diff_lambda_q2[j], diff_lambda_k2[j],
                               diff_subln_g[j], lambda_init)
        else:
            y = stick_breaking_attention(h, sb_w_in[j], sb_w_out[j])
        x = x + g1 * y
        h = rms_norm(x, norm2_g[i]) * (1.0 + sc2) + sh2
        y = hierarchical_moe(h, router_group_w[i], router_group_b[i], router_expert_w[i],
                             router_expert_b[i], expert_w_gate[i], expert_w_up[i],
                             expert_w_down[i])
        x = x + g2 * y
    return rms_norm(x, final_norm_g)


MEM_LEN = 256
EPS = 1e-6

GLA_HEADS = 4
GLA_DV = 96
GLA_DK = 48
GLA_QK = GLA_HEADS * GLA_DK
GLA_WIDTH = GLA_HEADS * GLA_DV
GLA_GATE_RANK = 16
GLA_TAU = 16.0
GLA_CHUNK = 64

CONV_WIDTH = 256
CONV_K = 3

MLA_HEADS = 6
MLA_NOPE = 64
MLA_ROPE = 32
MLA_V = 64
MLA_Q_RANK = 256
MLA_KV_RANK = 256
MLA_WIDTH = MLA_HEADS * MLA_V
ROPE_BASE = 10000.0

D_MIX = GLA_WIDTH + CONV_WIDTH + MLA_WIDTH

MEM_HEADS = 4
MEM_HEAD_DIM = 128
MEM_INNER = MEM_HEADS * MEM_HEAD_DIM

IN_SPLITS = (GLA_QK, GLA_QK, GLA_WIDTH, GLA_GATE_RANK, GLA_WIDTH,
             CONV_WIDTH, CONV_WIDTH, CONV_WIDTH, CONV_WIDTH,
             MLA_Q_RANK, MLA_KV_RANK, MLA_ROPE, MLA_WIDTH)
IN_WIDTH = sum(IN_SPLITS)


def _split_points():
    pts, acc = [], 0
    for s in IN_SPLITS[:-1]:
        acc += s
        pts.append(acc)
    return pts

def rms_norm_2(x, g):
    xf = x.astype(jnp.float32)
    y = xf * lax.rsqrt(jnp.mean(xf * xf, axis=-1, keepdims=True) + EPS)
    return (y * g.astype(jnp.float32)).astype(x.dtype)

def rope_tables(positions):
    inv_freq = 1.0 / (ROPE_BASE ** (jnp.arange(0, MLA_ROPE, 2, dtype=jnp.float32) / MLA_ROPE))
    ang = positions.astype(jnp.float32)[..., None] * inv_freq
    return jnp.cos(ang), jnp.sin(ang)

def apply_rope(x, cos, sin):
    half = MLA_ROPE // 2
    xf = x.astype(jnp.float32)
    x1, x2 = xf[..., :half], xf[..., half:]
    c, s = cos[:, :, None, :], sin[:, :, None, :]
    return jnp.concatenate([x1 * c - x2 * s, x2 * c + x1 * s], axis=-1).astype(x.dtype)

def gla_chunked(q, k, v, log_a):
    B, S, H, dk = q.shape
    dv = v.shape[-1]
    C = GLA_CHUNK
    N = S // C

    def chunks(t):
        return t.astype(jnp.float32).reshape(B, N, C, H, t.shape[-1]).transpose(0, 3, 1, 2, 4)

    qf = chunks(q) * (dk ** -0.5)
    kf, vf, la = chunks(k), chunks(v), chunks(log_a)
    b = jnp.cumsum(la, axis=3)
    b_last = b[:, :, :, -1:, :]
    q_dec = qf * jnp.exp(b)
    k_inv = kf * jnp.exp(-b)
    k_end = kf * jnp.exp(b_last - b)
    mask = jnp.tril(jnp.ones((C, C), dtype=bool))
    A = jnp.einsum('bhncd,bhnjd->bhncj', q_dec, k_inv)
    A = jnp.where(mask, A, 0.0)
    o_intra = jnp.einsum('bhncj,bhnjv->bhncv', A, vf)
    U = jnp.einsum('bhncd,bhncv->bhndv', k_end, vf)
    decay = jnp.exp(b_last[:, :, :, 0, :])

    def step(state, inp):
        u, d = inp
        return d[..., None] * state + u, state

    init = jnp.zeros((B, H, dk, dv), jnp.float32)
    _, s_prev = lax.scan(step, init, (U.transpose(2, 0, 1, 3, 4), decay.transpose(2, 0, 1, 3)))
    s_prev = s_prev.transpose(1, 2, 0, 3, 4)
    o_inter = jnp.einsum('bhncd,bhndv->bhncv', q_dec, s_prev)
    o = o_intra + o_inter
    return o.transpose(0, 2, 3, 1, 4).reshape(B, S, H, dv)

def causal_attention_blocks(q, k, v, scale):
    B, S, H, D = q.shape
    Dv = v.shape[-1]
    nb = S // Q_BLOCK
    qb = q.reshape(B, nb, Q_BLOCK, H, D).transpose(1, 0, 2, 3, 4)
    key_pos = jnp.arange(S)

    def one_block(args):
        qblk, start = args
        s = jnp.einsum('bqhd,bkhd->bhqk', qblk, k).astype(jnp.float32) * scale
        qpos = start + jnp.arange(Q_BLOCK)
        allowed = key_pos[None, :] <= qpos[:, None]
        s = jnp.where(allowed, s, -1e30)
        p = jax.nn.softmax(s, axis=-1).astype(v.dtype)
        return jnp.einsum('bhqk,bkhd->bqhd', p, v)

    out = lax.map(one_block, (qb, jnp.arange(nb) * Q_BLOCK))
    return out.transpose(1, 0, 2, 3, 4).reshape(B, S, H, Dv)

def hybrid_mixer(xn, cos, sin, w_in, gla_w_gate, gla_b_gate, gla_norm, conv_w,
                 mla_q_norm, mla_w_uq, mla_kv_norm, mla_w_ukv, w_out):
    B, S, _ = xn.shape
    proj = xn @ w_in
    (gq, gk, gv, glr, ggate, cc, cb, ch, cgate,
     cq, ckv, kr, mgate) = jnp.split(proj, _split_points(), axis=-1)

    z = glr @ gla_w_gate + gla_b_gate
    log_a = (jax.nn.log_sigmoid(z.astype(jnp.float32)) / GLA_TAU).reshape(B, S, GLA_HEADS, GLA_DK)
    o_gla = gla_chunked(gq.reshape(B, S, GLA_HEADS, GLA_DK),
                        gk.reshape(B, S, GLA_HEADS, GLA_DK),
                        gv.reshape(B, S, GLA_HEADS, GLA_DV), log_a)
    o_gla = rms_norm_2(o_gla, gla_norm).astype(xn.dtype).reshape(B, S, GLA_WIDTH)
    o_gla = o_gla * jax.nn.silu(ggate)

    u = cc * ch
    conv = lax.conv_general_dilated(u, conv_w[:, None, :].astype(u.dtype), window_strides=(1,),
                                    padding=[(CONV_K - 1, 0)],
                                    dimension_numbers=('NWC', 'WIO', 'NWC'),
                                    feature_group_count=CONV_WIDTH)
    o_conv = cb * conv * jax.nn.silu(cgate)

    qh = (rms_norm_2(cq, mla_q_norm) @ mla_w_uq).reshape(B, S, MLA_HEADS, MLA_NOPE + MLA_ROPE)
    q_full = jnp.concatenate([qh[..., :MLA_NOPE], apply_rope(qh[..., MLA_NOPE:], cos, sin)], axis=-1)
    kvh = (rms_norm_2(ckv, mla_kv_norm) @ mla_w_ukv).reshape(B, S, MLA_HEADS, MLA_NOPE + MLA_V)
    k_rope = apply_rope(kr.reshape(B, S, 1, MLA_ROPE), cos, sin)
    k_full = jnp.concatenate([kvh[..., :MLA_NOPE],
                              jnp.broadcast_to(k_rope, (B, S, MLA_HEADS, MLA_ROPE))], axis=-1)
    v_mla = kvh[..., MLA_NOPE:]
    o_mla = causal_attention_blocks(q_full, k_full, v_mla, 1.0 / math.sqrt(MLA_NOPE + MLA_ROPE))
    o_mla = o_mla.reshape(B, S, MLA_WIDTH) * jax.nn.silu(mgate)

    return jnp.concatenate([o_gla, o_conv, o_mla], axis=-1) @ w_out

def memory_cross_attention(hn, mem, norm_mem, wq, wk, wv, wo):
    B, S, _ = hn.shape
    M = mem.shape[1]
    memn = rms_norm_2(mem, norm_mem)
    q = (hn @ wq).reshape(B, S, MEM_HEADS, MEM_HEAD_DIM)
    k = (memn @ wk).reshape(B, M, MEM_HEADS, MEM_HEAD_DIM)
    v = (memn @ wv).reshape(B, M, MEM_HEADS, MEM_HEAD_DIM)
    s = jnp.einsum('bshd,bmhd->bhsm', q, k).astype(jnp.float32) / math.sqrt(MEM_HEAD_DIM)
    p = jax.nn.softmax(s, axis=-1).astype(v.dtype)
    o = jnp.einsum('bhsm,bmhd->bshd', p, v).reshape(B, S, MEM_INNER)
    return o @ wo

def second_inputs(seed: int = 0) -> dict:
    key = jax.random.key(seed)
    ks = jax.random.split(key, 24)
    f32 = jnp.float32

    def dense(k, fan_in, fan_out):
        return jax.random.normal(k, (DEPTH, fan_in, fan_out), f32) * (fan_in ** -0.5)

    def gain(k, n):
        return 1.0 + 0.02 * jax.random.normal(k, (DEPTH, n), f32)

    x = jax.random.normal(ks[0], (BATCH, SEQ, D_MODEL), f32)
    mem = jax.random.normal(ks[1], (BATCH, MEM_LEN, D_MODEL), f32)
    offset = jax.random.randint(ks[2], (BATCH, 1), 0, 1024, dtype=jnp.int32)
    positions = jnp.arange(SEQ, dtype=jnp.int32)[None, :] + offset
    return {
        'x': x,
        'mem': mem,
        'positions': positions,
        'norm_mix': gain(ks[3], D_MODEL),
        'w_in': dense(ks[4], D_MODEL, IN_WIDTH),
        'gla_w_gate': dense(ks[5], GLA_GATE_RANK, GLA_QK),
        'gla_b_gate': 0.02 * jax.random.normal(ks[6], (DEPTH, GLA_QK), f32),
        'gla_norm': gain(ks[7], GLA_DV),
        'conv_w': jax.random.normal(ks[8], (DEPTH, CONV_K, CONV_WIDTH), f32) * (CONV_K ** -0.5),
        'mla_q_norm': gain(ks[9], MLA_Q_RANK),
        'mla_w_uq': dense(ks[10], MLA_Q_RANK, MLA_HEADS * (MLA_NOPE + MLA_ROPE)),
        'mla_kv_norm': gain(ks[11], MLA_KV_RANK),
        'mla_w_ukv': dense(ks[12], MLA_KV_RANK, MLA_HEADS * (MLA_NOPE + MLA_V)),
        'w_out': dense(ks[13], D_MIX, D_MODEL),
        'norm_xattn': gain(ks[14], D_MODEL),
        'norm_mem': gain(ks[15], D_MODEL),
        'mem_wq': dense(ks[16], D_MODEL, MEM_INNER),
        'mem_wk': dense(ks[17], D_MODEL, MEM_INNER),
        'mem_wv': dense(ks[18], D_MODEL, MEM_INNER),
        'mem_wo': dense(ks[19], MEM_INNER, D_MODEL),
        'norm_final': 1.0 + 0.02 * jax.random.normal(ks[20], (D_MODEL,), f32),
    }

def second_block(x, mem, positions, norm_mix, w_in, gla_w_gate, gla_b_gate, gla_norm, conv_w,
              mla_q_norm, mla_w_uq, mla_kv_norm, mla_w_ukv, w_out, norm_xattn, norm_mem,
              mem_wq, mem_wk, mem_wv, mem_wo, norm_final):
    cos, sin = rope_tables(positions)
    h = x
    for l in range(DEPTH):
        h = h + hybrid_mixer(rms_norm_2(h, norm_mix[l]), cos, sin, w_in[l], gla_w_gate[l],
                             gla_b_gate[l], gla_norm[l], conv_w[l], mla_q_norm[l], mla_w_uq[l],
                             mla_kv_norm[l], mla_w_ukv[l], w_out[l])
        h = h + memory_cross_attention(rms_norm_2(h, norm_xattn[l]), mem, norm_mem[l],
                                       mem_wq[l], mem_wk[l], mem_wv[l], mem_wo[l])
    return rms_norm_2(h, norm_final)


def setup_inputs(seed=0):
    out = dict(first_inputs(seed))
    for name, value in second_inputs(seed + 1).items():
        if name != "x":
            out[name + "_2"] = value
    return out


def reference(
    x, c, norm1_g, norm2_g, ada_w, ada_b, diff_w_in, diff_w_out, diff_lambda_q1, diff_lambda_k1,
    diff_lambda_q2, diff_lambda_k2, diff_subln_g, sb_w_in, sb_w_out, router_group_w,
    router_group_b, router_expert_w, router_expert_b, expert_w_gate, expert_w_up, expert_w_down,
    final_norm_g, mem_2, positions_2, norm_mix_2, w_in_2, gla_w_gate_2, gla_b_gate_2,
    gla_norm_2, conv_w_2, mla_q_norm_2, mla_w_uq_2, mla_kv_norm_2, mla_w_ukv_2, w_out_2,
    norm_xattn_2, norm_mem_2, mem_wq_2, mem_wk_2, mem_wv_2, mem_wo_2, norm_final_2,
):
    x = first_block(
        x, c, norm1_g, norm2_g, ada_w, ada_b, diff_w_in, diff_w_out, diff_lambda_q1,
        diff_lambda_k1, diff_lambda_q2, diff_lambda_k2, diff_subln_g, sb_w_in, sb_w_out,
        router_group_w, router_group_b, router_expert_w, router_expert_b, expert_w_gate,
        expert_w_up, expert_w_down, final_norm_g,
    )
    return second_block(
        x, mem_2, positions_2, norm_mix_2, w_in_2, gla_w_gate_2, gla_b_gate_2, gla_norm_2,
        conv_w_2, mla_q_norm_2, mla_w_uq_2, mla_kv_norm_2, mla_w_ukv_2, w_out_2, norm_xattn_2,
        norm_mem_2, mem_wq_2, mem_wk_2, mem_wv_2, mem_wo_2, norm_final_2,
    )


_drawn_inputs = setup_inputs


def setup_inputs(seed=0):
    import zlib

    import numpy as np

    out = dict(_drawn_inputs(seed))
    spreads = {}
    factors = {'norm1_g': 3.373,
     'diff_lambda_k1': 8.0,
     'diff_lambda_q2': 8.0,
     'diff_subln_g': 3.934,
     'router_group_b': 5.185,
     'router_expert_b': 3.932,
     'gla_b_gate_2': 8.0,
     'gla_norm_2': 5.772,
     'mla_q_norm_2': 8.0,
     'mla_kv_norm_2': 8.0,
     'norm_xattn_2': 8.0,
     'norm_mem_2': 8.0,
     'norm_final_2': 2.826}
    for name, (base, spread) in spreads.items():
        noise = np.random.default_rng([zlib.crc32(name.encode()), seed]).standard_normal(out[name].shape)
        drawn = base * np.exp(spread * noise) if base else spread * noise
        out[name] = __import__('jax').numpy.asarray(drawn.astype(out[name].dtype))
    for name, factor in factors.items():
        out[name] = (out[name] * factor).astype(out[name].dtype)
    return out
```

```python
import math
from contextlib import ExitStack

import numpy as np

import concourse.bass as bass
from concourse import mybir

F32 = mybir.dt.float32
I32 = mybir.dt.int32
ALU = mybir.AluOpType
ACT = mybir.ActivationFunctionType
AX = mybir.AxisListType.X

P = 128
D = 1024
S = 512
T = S // P
KD = D // P
DEPTH = 2
BANK = 512
BANKS = 8
SLOTS = 4
SLOT = 4096
NEG = -1e30
BIG = float(1 << 20)

DIFF_HEADS = 8
DIFF_LAMBDA_INIT = 0.8 - 0.6 * math.exp(0.0)
SB_HEADS = 16
HD = 64

GROUPS = 4
PER_GROUP = 8
EXPERTS = GROUPS * PER_GROUP
HIDDEN = 512
KH = HIDDEN // P
MAX_BLOCKS = (2 * S + EXPERTS * P) // P
TABLE = MAX_BLOCKS + 1

MEM = 256
MT = MEM // P
GH, GDK, GDV, CHUNK = 4, 48, 96, 64
GQK, GV = GH * GDK, GH * GDV
CW = 256
MH, NOPE, ROPE, MV = 6, 64, 32, 64
MQ = NOPE + ROPE
RANK = 256
XH, XD = 4, 128
IN_SPLITS = (GQK, GQK, GV, 16, GV, CW, CW, CW, CW, RANK, RANK, ROPE, MH * MV)
IN_WIDTH = sum(IN_SPLITS)
IN_AT = [sum(IN_SPLITS[:n]) for n in range(len(IN_SPLITS))]
(C_GQ, C_GK, C_GV, C_GLR, C_GGATE, C_CC, C_CB, C_CH, C_CGATE, C_CQ, C_CKV, C_KR, C_MGATE) = IN_AT
IN_CHUNKS = [(n, min(BANK, IN_WIDTH - n)) for n in range(0, IN_WIDTH, BANK)]


def shape_constants():
    p = np.arange(P)[:, None]
    c = np.arange(P)[None, :]
    same = (p // CHUNK) == (c // CHUNK)
    u = np.arange(S)[None, :] - (S - P)
    parts = {
        "ident": (p == c),
        "alibi": np.where(np.floor_divide(u, CHUNK) <= p // CHUNK, -np.abs(p - u), NEG),
        "before": (p < c),
        "neg_ge": -1.0 * (p >= c),
        "ones": np.ones((P, P)),
        "neg_ones": -np.ones((P, P)),
        "gla_cum": -1.0 / 16 * (same & (p <= c)),
        "gla_last": -1.0 / 16 * same,
        "gla_chunk": -1.0 / 16 * ((p // CHUNK) == np.arange(2)[None, :]),
        "shift1": (c == p + 1),
        "shift2": (c == p + 2),
        "carry1": (p == P - 1) & (c == 0),
        "carry2": (c == p + 2 - P),
        "gla_mask": (same & (p <= c)),
        "causal": np.where(c <= p, 0.0, NEG),
        "iota": np.broadcast_to(c, (P, P)),
        "rev": np.broadcast_to(8.0 - np.arange(8)[None, :], (P, 8)),
        "row_id": (np.arange(T)[None, :, None] * P + np.arange(P)[:, None, None]
                   + S * np.arange(2)[None, None, :] + 1).reshape(P, 2 * T),
        "inv_freq": np.broadcast_to((1.0 / (np.float32(10000.0) ** (np.arange(0, ROPE, 2, dtype=np.float32) / np.float32(ROPE)))).astype(np.float32)[None, :], (P, ROPE // 2)),
        "minus_half": np.full((P, 32), -0.5),
    }
    at, n = {}, 0
    for name, a in parts.items():
        at[name] = (n, a.shape[1])
        n += a.shape[1]
    table = np.concatenate([np.asarray(a, np.float32) for a in parts.values()], axis=1)
    return np.ascontiguousarray(table), at


class Stage:

    def __init__(self, kind, arg, fill, load, turn, residual, scaled, grouped, tiles_before, updates):
        self.kind, self.arg, self.fill, self.load, self.turn, self.residual = kind, arg, fill, load, turn, residual
        self.scaled, self.grouped, self.tiles_before = scaled, grouped, tiles_before
        self.updates = updates


def attention_steps(heads, ahead, per_head):
    steps = heads * T
    order = []
    for s in range(steps + ahead):
        if s < steps:
            if s % T == 0:
                order += [(what, s) for what in per_head]
            order.append(("scores", s))
        if s >= ahead:
            order += [("turned", s - ahead), ("values", s - ahead)]
    return order


def diff_order():
    order = []
    for what, s in attention_steps(DIFF_HEADS, AHEAD, ()):
        order += [("map0", s), ("map1", s)] if what == "scores" else [(what, s)]
    return order


def gla_fill(stage, what, h, part=0):
    first = stage.fill + 16
    if what == "update":
        return first + 4 * h + part - (h > 0)
    if what == "scores":
        return first + 4 * h + 2 - (h > 0)
    return first + 4 * h + 6 - 3 * (h == GH - 1)


ROUNDER = 1.5 * 2.0 ** 23
_T0 = 6.28125
_T1 = float(np.float32(np.floor((2 * math.pi - _T0) * 2 ** 20) / 2 ** 20))
TURN = (_T0, _T1, 2 * math.pi - _T0 - _T1)
PI_BELOW = 3.1415925
AHEAD = 2
N_SMALL = 5 + 4 + 10


def plan_stages():
    kinds = []
    for layer in range(DEPTH):
        kinds += [("mod", layer), ("norm", ("first1", layer)), ("qkv", layer),
                  ("diff" if layer == 0 else "stick", layer)]
        if layer == 0:
            kinds += [("otrans", 0)]
        kinds += [("attn_out", layer), ("norm", ("first2", layer)), ("route", layer), ("experts", layer),
                  ("combine", layer)]
    kinds += [("final", 0)]
    for layer in range(DEPTH):
        kinds += [("norm", ("mix", layer)), ("project", layer), ("latent_up", layer), ("latent", layer),
                  ("gla", layer), ("conv", layer), ("mtrans", layer), ("mix_out", layer),
                  ("norm", ("xattn", layer)), ("xq", layer), ("norm", ("mem", layer)), ("xkv", layer),
                  ("xattn", layer), ("xtrans", layer), ("x_out", layer)]
    kinds += [("final", 1)]
    fills = {
        "mod": 13, "norm": KD, "qkv": 24, "diff": 4 * DIFF_HEADS * T, "stick": 0, "otrans": KD,
        "attn_out": 8, "route": 3, "experts": 0, "combine": 0, "final": 0,
        "project": len(IN_CHUNKS) * T, "latent_up": 4 + 4 * T, "latent": MH * (2 + 3 * T),
        "gla": 8 + GH * 6, "conv": 2, "mtrans": KD, "mix_out": 8,
        "xq": XH, "xkv": XH + MT, "xattn": 3 * XH * T, "xtrans": XH, "x_out": 8,
    }
    readers = {
        "mod": list(range(12)), "qkv": [3, 7, 11, 15, 19, 23], "attn_out": [6, 7],
        "project": [T * j + T - 1 for j in range(len(IN_CHUNKS))], "latent_up": [3 + 2 * T, 3 + 4 * T],
        "mix_out": [6, 7], "xq": [XH - 1], "xkv": [XH - 1, XH + MT - 1], "x_out": [7],
    }
    plan, last_reader, fill, seen, residual, updates, scaled, grouped, tiles = [], [], 0, {}, None, 0, 0, 0, 0
    for kind, arg in kinds:
        plan.append(Stage(kind, arg, fill, len(last_reader), seen.get(kind, 0), residual,
                          scaled, grouped, tiles, updates))
        scaled += kind in ("norm", "final")
        grouped += kind in ("otrans", "latent_up", "gla")
        if kind == "norm":
            tiles += MT if arg[0] == "mem" else T
        seen[kind] = seen.get(kind, 0) + 1
        last_reader += [fill + r for r in readers.get(kind, [])]
        if kind in ("attn_out", "mix_out", "x_out"):
            residual = ("fills", fill)
        if kind in ("combine", "final"):
            updates += T
            residual = ("updates", updates)
        fill += fills[kind]
    return plan, last_reader


def build_program(nc, upto, x, c, norm1_g, norm2_g, ada_w, ada_b, diff_w_in, diff_w_out,
                  diff_lambda_q1, diff_lambda_k1, diff_lambda_q2, diff_lambda_k2, diff_subln_g,
                  sb_w_in, sb_w_out, router_group_w, router_group_b, router_expert_w, router_expert_b,
                  expert_w_gate, expert_w_up, expert_w_down, final_norm_g, mem_2, positions_2,
                  norm_mix_2, w_in_2, gla_w_gate_2, gla_b_gate_2, gla_norm_2, conv_w_2, mla_q_norm_2,
                  mla_w_uq_2, mla_kv_norm_2, mla_w_ukv_2, w_out_2, norm_xattn_2, norm_mem_2,
                  mem_wq_2, mem_wk_2, mem_wv_2, mem_wo_2, norm_final_2, tables, out):
    _, table_at = shape_constants()
    TABLE_WIDTH = tables.shape[1]
    plan, last_reader = plan_stages()
    plan = plan[:upto]
    ctx = ExitStack()
    with ctx:
        def sbuf(name, shape, dtype=F32):
            return ctx.enter_context(nc.sbuf_tensor(name, shape, dtype))

        def semaphore(name):
            return ctx.enter_context(nc.semaphore(name))

        X = sbuf("residual", [P, T, D])
        XN = sbuf("normed_by_token", [P, T, D])
        HT = sbuf("normed_by_feature", [P, KD, S])
        BIGA = sbuf("projections", [P, T * 3136])
        RING = sbuf("weight_ring", [P, SLOTS, SLOT])
        GB = sbuf("gates", [P, 2, D])
        SCR = sbuf("scratch", [P, 6144])
        CON = sbuf("constants", [P, TABLE_WIDTH])
        COLS = sbuf("columns", [P, 4, KD])
        GCOL = sbuf("gain_columns", [P, 10, KD])
        PS = ctx.enter_context(nc.psum_tensor("banks", [P, BANKS, BANK], F32))

        QT = BIGA[:, 0:4096].rearrange("p (c s) -> p c s", c=8)
        KT = BIGA[:, 4096:8192].rearrange("p (c s) -> p c s", c=8)
        V = BIGA[:, 8192:12288].rearrange("p (t n) -> p t n", t=T)
        PR = BIGA[:, 0:T * IN_WIDTH].rearrange("p (t n) -> p t n", t=T)

        def const(name):
            a, n = table_at[name]
            return CON[:, a:a + n]

        ident = const("ident")
        ones = const("ones")

        SUMSQ = sbuf("sum_of_squares", [P, 32])
        RSTD = sbuf("reciprocal_rms", [P, 32])
        MX = sbuf("row_max", [P, 4, 2])
        SUM = sbuf("row_sum", [P, 4, 2])
        RCP = sbuf("row_reciprocal", [P, 4, 2])
        LAMV = sbuf("lambda_vectors", [P, 4, HD])
        LAM = sbuf("lambda", [P, 8])
        SUBG = sbuf("subln_gain", [P, 2])
        CCOL = sbuf("condition", [P, 4, KD])

        RW = sbuf("router_weights", [P, KD, GROUPS + EXPERTS])
        RB = sbuf("router_bias", [P, GROUPS + EXPERTS])
        WTS = sbuf("expert_weights", [P, 2, T])
        TABI = sbuf("slot_table", [P, 2, TABLE], I32)
        CTRL = sbuf("block_experts", [1, MAX_BLOCKS + 8], I32)
        ROWS_IN = sbuf("block_rows_in", [P, 1], I32)
        ROWS_OUT = sbuf("block_rows_out", [P, 1], I32)

        COS = sbuf("rope_cos", [P, T, ROPE // 2])
        SIN = sbuf("rope_sin", [P, T, ROPE // 2])
        POSI = sbuf("positions", [P, T], I32)
        POSF = sbuf("positions_float", [P, T])
        ANGLE = sbuf("rope_steps", [P, 3, T, ROPE // 2])
        SIN_T = [ANGLE[:, n] for n in range(3)]
        GW = LAMV[0:32].rearrange("p a n -> p (a n)")[:, 0:GQK]
        GN = RW[:, :, :].rearrange("p k n -> p (k n)")[:, 0:GDV]
        at = table_at["alibi"][0]
        CWT = CON[:, at:at + 3 * CW].rearrange("p (j n) -> p j n", j=3)
        RG = sbuf("rank_gains", [P, 2, 2])

        xn_d = nc.dram_tensor("xn_rows", [S, D], F32, kind="Internal").ap()
        y_d = nc.dram_tensor("y_rows", [2 * S, D], F32, kind="Internal").ap()

        bank_full = [semaphore(f"bank_full{n}") for n in range(BANKS)]
        bank_drained = [semaphore(f"bank_drained{n}") for n in range(BANKS)]
        slot_loaded = [semaphore(f"slot_loaded{n}") for n in range(SLOTS)]
        inputs_in = semaphore("inputs_in")
        dve_done = semaphore("dve_done")
        act_done = semaphore("act_done")
        pool_done = semaphore("pool_done")

        def full_wait(eng, n):
            eng.wait_ge(bank_full[n % BANKS], n // BANKS + 1)

        def drained_wait(eng, n):
            eng.wait_ge(bank_drained[n % BANKS], n // BANKS + 1)

        def free_wait(eng, n):
            if n >= BANKS:
                eng.wait_ge(bank_drained[n % BANKS], n // BANKS)

        def loaded_wait(eng, u):
            eng.wait_ge(slot_loaded[u % SLOTS], 16 * (u // SLOTS + 1))

        def bank(n):
            return PS[:, n % BANKS, :]

        def slot(u, width, k=KD):
            return RING[:, u % SLOTS, 0:k * width].rearrange("p (k n) -> p k n", k=k)

        def residual_wait(eng, stage, t=None):
            if stage.residual is None:
                return
            how, n = stage.residual
            tiles = range(T) if t is None else [t]
            if how == "updates":
                eng.wait_ge(residual_written, n - T + 1 + tiles[-1])
            else:
                for tile in tiles:
                    drained_wait(eng, n + 2 * tile)
                    drained_wait(eng, n + 2 * tile + 1)


        residual_written = semaphore("residual_written")
        cond_exp = semaphore("cond_exp")
        cond_rows = semaphore("cond_rows")
        ada_bias_in = semaphore("ada_bias_in")
        sumsq_ready = semaphore("sumsq_ready")
        rstd_ready = semaphore("rstd_ready")
        xn_ready = semaphore("xn_ready")
        squares_ready = semaphore("squares_ready")
        group_sums = semaphore("group_sums")
        group_rstd = semaphore("group_rstd")
        group_normed = semaphore("group_normed")
        lambda_sums = semaphore("lambda_sums")
        lambda_exp = semaphore("lambda_exp")
        negmax_ready = semaphore("negmax_ready")
        diff_exp = semaphore("diff_exp")
        diff_ready = semaphore("diff_ready")
        z_full = semaphore("z_full")
        z_clamped = semaphore("z_clamped")
        z_log = semaphore("z_log")
        sp_raw = semaphore("sp_raw")
        sp_ready = semaphore("sp_ready")
        r_full = semaphore("r_full")
        a_raw = semaphore("a_raw")
        a_ready = semaphore("a_ready")
        o_full = semaphore("o_full")
        o_drained = semaphore("o_drained")
        router_in = semaphore("router_in")
        group_shift = semaphore("group_shift")
        group_exp = semaphore("group_exp")
        pair_diff = semaphore("pair_diff")
        pair_exp = semaphore("pair_exp")
        assigned = semaphore("assigned")
        one_hots = semaphore("one_hots")
        blocks_ready = semaphore("blocks_ready")
        xn_stored = semaphore("xn_stored")
        experts_over = semaphore("experts_over")
        rows_back = semaphore("rows_back")
        gain_in = semaphore("gain_in")
        mixer_in = semaphore("mixer_in")
        mixer_up = semaphore("mixer_up")
        soft_in = semaphore("soft_in")
        soft_log = semaphore("soft_log")
        soft_ready = semaphore("soft_ready")
        decays_ready = semaphore("decays_ready")
        decayed = semaphore("decayed")
        gla_clear = semaphore("gla_clear")
        state_ready = semaphore("state_ready")
        gate_exp = semaphore("gate_exp")
        conv_in = semaphore("conv_in")
        mixed = semaphore("mixed")
        angles = semaphore("angles")
        rope_ready = semaphore("rope_ready")
        memory_in = semaphore("memory_in")
        stored = semaphore("stored")

        class Blocks:

            def __init__(self, layer):
                def s(name):
                    return semaphore(f"{name}_{layer}")

                self.loaded = [s(f"part_loaded{n}") for n in range(6)]
                self.used = [s(f"part_used{n}") for n in range(6)]
                self.gathered = s("gathered")
                self.scattered = s("scattered")
                self.y_free = s("y_free")
                self.rows_turned = s("rows_turned")
                self.first_scaled = s("first_scaled")
                self.last_scaled = s("last_scaled")
                self.gate_exp = s("block_gate_exp")
                self.silu_steps = s("silu_steps")
                self.hidden = s("hidden")
                self.hidden_turned = s("hidden_turned")
                self.hidden_ready = s("hidden_ready")
                self.y_left = s("y_left")
                self.y_right = s("y_right")

        blocks = [Blocks(layer) for layer in range(DEPTH)]

        XG = BIGA[:, 0:1024]
        XGT = BIGA[:, 1024:2048].rearrange("p (k n) -> p k n", k=KD)
        HID = BIGA[:, 2048:2560]
        HIDT = BIGA[:, 2560:3072].rearrange("p (k n) -> p k n", k=KH)
        YB = BIGA[:, 3072:4096]
        GE = BIGA[:, 4096:4608]
        GR = BIGA[:, 4608:5120]
        Y2 = BIGA[:, 0:8192].rearrange("p (j t n) -> p j t n", j=2, t=T)
        W_GATE = RING[:, 0, :].rearrange("p (k n) -> p k n", k=KD)
        W_UP = RING[:, 1, :].rearrange("p (k n) -> p k n", k=KD)
        W_DOWN = RING[:, 2, :].rearrange("p (h k n) -> p h k n", h=2, k=KH)
        MODROW = HT[0:1, :, :].rearrange("p (q a) n -> p q (a n)", a=2)
        ADAB = BIGA[0:1, 6144:12288]
        CB = BIGA[:, 0:1024].rearrange("p (k n) -> p k n", k=KD)
        MEMT = BIGA[:, 4096:6144].rearrange("p (t n) -> p t n", t=MT)
        QM = SCR[:, 0:2304].rearrange("p (t h n) -> p t h n", t=T, h=MH)
        KM = SCR[:, 2304:4608].rearrange("p (t h n) -> p t h n", t=T, h=MH)
        VM = SCR[:, 4608:6144].rearrange("p (t h n) -> p t h n", t=T, h=MH)
        XQT = BIGA[:, 0:2048].rearrange("p (h s) -> p h s", h=XH)
        XKT = BIGA[:, 2048:3072].rearrange("p (h s) -> p h s", h=XH)
        XV = BIGA[:, 3072:4096].rearrange("p (t n) -> p t n", t=MT)

        def SA(s):
            return SCR[:, 1024 * (s % 3):1024 * (s % 3 + 1)].rearrange("p (m n) -> p m n", m=2)

        def AT(s):
            return SCR[:, 3072 + BANK * (s % 2):3072 + BANK * (s % 2 + 1)]

        def SP1(stage, s):
            return GB.rearrange("p a n -> p (a n)")[:, BANK * (s % 3):BANK * (s % 3 + 1)]

        def AT1(stage, s):
            return HT[:, s % 2, :] if stage.kind == "latent" else SCR[:, BANK * (s % 2):BANK * (s % 2 + 1)]

        def LQT(h):
            return HT[:, 4 + h % 2, :]

        def LKT(h):
            return HT[:, 6 + h % 2, :]

        SOFT = SCR[:, 0:768].rearrange("p (t n) -> p t n", t=T)
        QD = SCR[:, 768:1536].rearrange("p (t n) -> p t n", t=T)
        KI = SCR[:, 1536:2304].rearrange("p (t n) -> p t n", t=T)
        KE = SCR[:, 2304:3072].rearrange("p (t n) -> p t n", t=T)
        GLT = SCR[:, 3072:3584]
        DEC = SCR[:, 3584:3616]
        GQT = HT[:, 0:4, :]
        GKT = HT[:, 4:8, :]
        CU2 = SCR[:, 0:1024].rearrange("p (t n) -> p t n", t=T)
        CU1 = SCR[:, 1024:2048].rearrange("p (t n) -> p t n", t=T)
        CU0 = SCR[:, 2048:3072].rearrange("p (t n) -> p t n", t=T)

        def GAT(h):
            return SCR[:, 3616 + BANK * (h % 2):3616 + BANK * (h % 2 + 1)].rearrange("p (t n) -> p t n", t=T)

        def GST(h):
            return GB.rearrange("p a n -> p (a n)")[:, 768 * (h % 2):768 * (h % 2 + 1)].rearrange("p (j n) -> p j n", j=8)

        SGATE = SCR[:, 4608:6144].rearrange("p (t n) -> p t n", t=T)
        GATES = ((C_GGATE, GV), (C_CGATE, CW), (C_MGATE, MH * MV))

        def normed_after(stage):
            return T if stage.kind == "otrans" else T * (2 + stage.turn)

        def squares_before(stage):
            return T + 2 * stage.turn + (stage.kind == "gla")

        def soft_base(stage):
            return DIFF_HEADS * T + stage.turn * (MH + XH) * T + (MH * T if stage.kind == "xattn" else 0)

        ROUTE = {}
        at = 0
        for name, dims in (("logits", (T, 36)), ("gmax", (T,)), ("gshift", (T, 4)), ("gexp", (T, 4)), ("gsum", (T,)),
                           ("gweight", (T,)), ("gfirst", (T, 4)), ("gtop", (T,)), ("group", (T, 4)),
                           ("masked", (T, 4, 8)), ("elogits", (T, 8)), ("top1", (T,)), ("first1", (T, 8)), ("mark1", (T,)),
                           ("hot1", (T, 8)), ("rest", (T, 8)), ("top2", (T,)), ("first2", (T, 8)), ("mark2", (T,)),
                           ("hot2", (T, 8)), ("gap", (T,)), ("gapexp", (T,)), ("total", (T,)), ("share", (T,)),
                           ("assign1", (T, 32)), ("assign2", (T, 32)), ("assigned", (T, 32)), ("rank", (T, 32)),
                           ("count", (32,)), ("nblocks", (32,)), ("upto", (32,)), ("first", (32,)), ("over", (T, 32)),
                           ("place", (T, 32)), ("blockof", (T, 32)), ("picked", (T, 32)), ("places_of", (2, T)),
                           ("blocks_of", (2, T)), ("places", (2 * T, P)), ("blocks", (2 * T, TABLE)), ("empty", (TABLE,)),
                           ("target", (TABLE,)), ("source", (TABLE,)), ("past", (MAX_BLOCKS, 32)), ("expert", (MAX_BLOCKS,))):
            size = math.prod(dims)
            v = SCR[:, at:at + size]
            if len(dims) == 2:
                v = v.rearrange("p (a b) -> p a b", a=dims[0])
            if len(dims) == 3:
                v = v.rearrange("p (a b c) -> p a b c", a=dims[0], b=dims[1])
            ROUTE[name] = v
            at += size
        assert at <= 6144

        def RT(name):
            return ROUTE[name]

        def gains(stage):
            which, layer = stage.arg
            if which == "first1":
                return X, T, COLS[:, 1, :], COLS[:, 0, :]
            if which == "first2":
                return X, T, COLS[:, 3, :], COLS[:, 2, :]
            if which == "mem":
                return MEMT, MT, GCOL[:, 8 + layer, :], None
            return X, T, GCOL[:, {"mix": 4, "xattn": 6}[which] + layer, :], None

        def stick_view(g):
            b = 3 * (g % 2)
            return PS[:, b:b + 3, :].rearrange("p b n -> p (b n)")

        STICK_AT = [0, 512, 1024, 896]
        STICK_N = [S - P * kt for kt in range(T)]
        STICK_W = 1280
        E_BUF = [SCR[:, n * STICK_W:(n + 1) * STICK_W] for n in range(2)]
        A_BUF = [SCR[:, (2 + n) * STICK_W:(3 + n) * STICK_W] for n in range(2)]

        def soft_plan(stage):
            if stage.kind == "latent":
                order = attention_steps(MH, AHEAD, ("turn_q", "turn_k"))
                return order, MH, float(MQ) ** -0.5, lambda i: P * (i + 1), MV, GV + CW
            order = attention_steps(XH, AHEAD, ())
            return order, XH, float(XD) ** -0.5, lambda i: MEM, XD, 0

        def by_row(w, n0, n1):
            return w[:, n0:n1].rearrange("(p k) n -> p k n", p=P)

        def by_chunk(w, n0, n1):
            return w[:, n0:n1].rearrange("(k p) n -> p k n", p=P)

        def weight_loads(stage):
            layer = stage.arg
            if stage.kind == "mod":
                return [(BANK, KD, by_row(ada_w[layer], n * BANK, (n + 1) * BANK)) for n in range(12)]
            if stage.kind == "qkv":
                w = diff_w_in[0] if layer == 0 else sb_w_in[0]
                return [(BANK, KD, by_row(w, n * BANK, (n + 1) * BANK)) for n in range(6)]
            if stage.kind == "attn_out":
                w = diff_w_out[0] if layer == 0 else sb_w_out[0]
                return [(BANK, KD, by_chunk(w, n * BANK, (n + 1) * BANK)) for n in range(2)]
            if stage.kind == "project":
                return [(w, KD, by_row(w_in_2[layer], n, n + w)) for n, w in IN_CHUNKS]
            if stage.kind == "latent_up":
                return [(MH * MQ, 2, by_row(mla_w_uq_2[layer], 0, MH * MQ)),
                        (MH * (NOPE + MV), 2, by_row(mla_w_ukv_2[layer], 0, MH * (NOPE + MV)))]
            if stage.kind == "mix_out":
                return [(BANK, KD, by_chunk(w_out_2[layer], n * BANK, (n + 1) * BANK)) for n in range(2)]
            if stage.kind == "xq":
                return [(BANK, KD, by_row(mem_wq_2[layer], 0, BANK))]
            if stage.kind == "xkv":
                return [(BANK, KD, by_row(mem_wk_2[layer], 0, BANK)), (BANK, KD, by_row(mem_wv_2[layer], 0, BANK))]
            if stage.kind == "x_out":
                return [(D, XH, by_chunk(mem_wo_2[layer], 0, D))]
            return []

        block = ctx.enter_context(nc.Block())

        @block.sync
        def _(sp):
            small = [
                (CON[:, :], tables), (X[:, :, :], x[0].rearrange("(t p) n -> p t n", p=P)),
                (CCOL[:, 0, :], c[0].rearrange("(p k) -> p k", p=P)),
                (SUBG[:, 0:1], diff_subln_g[0].rearrange("(p k) -> p k", p=P)),
                (POSI[:, :], positions_2[0].rearrange("(t p) -> p t", p=P)),
            ]
            for n, v in enumerate((diff_lambda_q1, diff_lambda_k1, diff_lambda_q2, diff_lambda_k2)):
                small.append((LAMV[:, n, :], v[0].partition_broadcast(P)))
            for n, g in enumerate((norm1_g, norm2_g, norm_mix_2, norm_xattn_2, norm_mem_2)):
                for layer in range(DEPTH):
                    small.append((GCOL[:, 2 * n + layer, :], g[layer].rearrange("(p k) -> p k", p=P)))
            assert len(small) == N_SMALL
            with nc.allow_non_contiguous_dma(reason="a few positions"):
                for dst, src in small:
                    sp.dma_start(dst, src).then_inc(inputs_in, 16)
            for stage in plan:
                layer = stage.arg
                if stage.kind == "mod":
                    if stage.turn:
                        residual_wait(sp, stage)
                    sp.dma_start(ADAB, ada_b[layer:layer + 1, :]).then_inc(ada_bias_in, 16)
                if stage.kind == "route":
                    if stage.turn:
                        full_wait(sp, plan[[p.kind for p in plan].index("route")].fill)
                        residual_wait(sp, stage)
                    with nc.allow_non_contiguous_dma(reason="narrow router weights"):
                        sp.dma_start(RW[:, :, 0:GROUPS], router_group_w[layer].rearrange("(p k) n -> p k n", p=P)).then_inc(router_in, 16)
                        sp.dma_start(RW[:, :, GROUPS:], router_expert_w[layer].rearrange("(p k) n -> p k n", p=P)).then_inc(router_in, 16)
                    sp.dma_start(RB[:, 0:GROUPS], router_group_b[layer].partition_broadcast(P)).then_inc(router_in, 16)
                    sp.dma_start(RB[:, GROUPS:], router_expert_b[layer].rearrange("g e -> (g e)").partition_broadcast(P)).then_inc(router_in, 16)
                if stage.kind == "final":
                    residual_wait(sp, stage)
                    g = final_norm_g if stage.arg == 0 else norm_final_2
                    sp.dma_start(GB[:, 0, :], g.partition_broadcast(P)).then_inc(gain_in, 16)
                    if stage.arg == 1:
                        for t in range(T):
                            sp.wait_ge(residual_written, stage.updates + t + 1)
                            sp.dma_start(out[0].rearrange("(t p) n -> p t n", p=P)[:, t, :], X[:, t, :]).then_inc(stored, 16)
                        sp.wait_ge(stored, 16 * T)
                if stage.kind == "project":
                    if stage.turn:
                        residual_wait(sp, stage)
                    sp.dma_start(GW[0:16, :], gla_w_gate_2[layer]).then_inc(mixer_in, 16)
                    sp.dma_start(GW[16:17, :], gla_b_gate_2[layer:layer + 1, :]).then_inc(mixer_in, 16)
                    sp.dma_start(GN[:, :], gla_norm_2[layer].partition_broadcast(P)).then_inc(mixer_in, 16)
                    sp.dma_start(CWT[:, :, :], conv_w_2[layer].partition_broadcast(P)).then_inc(mixer_in, 16)
                    sp.dma_start(RG[:, 0, :], mla_q_norm_2[layer].rearrange("(p k) -> p k", p=P)).then_inc(mixer_in, 16)
                    sp.dma_start(RG[:, 1, :], mla_kv_norm_2[layer].rearrange("(p k) -> p k", p=P)).then_inc(mixer_in, 16)
                for n, (width, k, src) in enumerate(weight_loads(stage)):
                    u = stage.load + n
                    if u >= SLOTS:
                        full_wait(sp, last_reader[u - SLOTS])
                    sp.dma_start(slot(u, width, k), src).then_inc(slot_loaded[u % SLOTS], 16)
                if stage.kind == "xq":
                    sp.wait_ge(mixed, 3 * (stage.turn + 1))
                    sp.dma_start(MEMT, mem_2[0].rearrange("(t p) n -> p t n", p=P)).then_inc(memory_in, 16)
                if stage.kind == "experts":
                    s = blocks[layer]
                    for u in range(stage.load - SLOTS, stage.load):
                        full_wait(sp, last_reader[u])
                    sp.wait_ge(blocks_ready, layer + 1)
                    n_blocks = sp.value_load(CTRL[0:1, 0:1], min_val=1, max_val=MAX_BLOCKS)
                    with sp.Fori(0, n_blocks) as b:
                        e = sp.value_load(CTRL[0:1, bass.ds(b + 1, 1)], min_val=0, max_val=EXPERTS - 1)
                        gate = expert_w_gate[layer, bass.ds(e, 1)].rearrange("a (p k) n -> p (a k) n", p=P)
                        up = expert_w_up[layer, bass.ds(e, 1)].rearrange("a (p k) n -> p (a k) n", p=P)
                        down = expert_w_down[layer, bass.ds(e, 1)].rearrange("a (p k) n -> p (a k) n", p=P)
                        half = KD // 2
                        for n, (dst, src) in enumerate((
                                (W_GATE[:, 0:half, :], gate[:, 0:half, :]), (W_GATE[:, half:, :], gate[:, half:, :]),
                                (W_UP[:, 0:half, :], up[:, 0:half, :]), (W_UP[:, half:, :], up[:, half:, :]),
                                (W_DOWN[:, 0], down[:, :, 0:BANK]), (W_DOWN[:, 1], down[:, :, BANK:]))):
                            sp.wait_ge(s.used[n], b + 1)
                            sp.dma_start(dst, src).then_inc(s.loaded[n], 16)
                    sp.wait_ge(experts_over, layer + 1)

        @block.tensor
        def _(pe):
            def product(n, pieces, start=True, width=None):
                for j, (out_ap, lhs, rhs) in enumerate(pieces):
                    last = pe.matmul(out_ap, lhs, rhs, start=start and j == 0, stop=j == len(pieces) - 1)
                return last

            def fill_done(last, n):
                last.then_inc(bank_full[n % BANKS], 1)

            pe.wait_ge(inputs_in, 16 * N_SMALL)
            for stage in plan:
                f0, u0, layer = stage.fill, stage.load, stage.arg

                if stage.kind == "mod":
                    pe.wait_ge(cond_rows, stage.turn + 1)
                    for n in range(12):
                        free_wait(pe, f0 + n)
                        loaded_wait(pe, u0 + n)
                        w = slot(u0 + n, BANK)
                        for k in range(KD):
                            pe.matmul(bank(f0 + n), CB[:, k, :], w[:, k, :], start=k == 0, stop=False)
                        if n == 0:
                            pe.wait_ge(ada_bias_in, 16 * (stage.turn + 1))
                        fill_done(pe.matmul(bank(f0 + n), ones[0:1, :], ADAB[:, n * BANK:(n + 1) * BANK], start=False, stop=True), f0 + n)
                    fc = f0 + 12
                    free_wait(pe, fc)
                    for q, part in enumerate((0, 1, 3, 4)):
                        drained_wait(pe, f0 + 2 * part)
                        drained_wait(pe, f0 + 2 * part + 1)
                        for k in range(KD):
                            last = pe.matmul(bank(fc)[:, q * KD + k:q * KD + k + 1], MODROW[0:1, q, k::KD], ones[0:1, 0:1], start=True, stop=True)
                    fill_done(last, fc)

                if stage.kind == "norm":
                    _, tiles, _, _ = gains(stage)
                    for k in range(KD):
                        n = f0 + k
                        free_wait(pe, n)
                        for t in range(tiles):
                            if k == 0:
                                pe.wait_ge(xn_ready, stage.tiles_before + t + 1)
                            last = pe.transpose(bank(n)[:, t * P:(t + 1) * P], XN[:, t, k::KD], ident)
                        fill_done(last, n)

                if stage.kind in ("qkv", "xq", "xkv"):
                    norm_fill = f0 - KD
                    if stage.kind == "qkv":
                        turned, cols, v_units, v_tiles = 16, S, (4, 5), T
                    elif stage.kind == "xq":
                        turned, cols, v_units, v_tiles = XH, S, (), 0
                    else:
                        turned, cols, v_units, v_tiles = XH, MEM, (1,), MT
                    for j in range(turned):
                        n, u = f0 + j, u0 + j // 4
                        free_wait(pe, n)
                        if j % 4 == 0:
                            loaded_wait(pe, u)
                        w = slot(u, BANK)
                        for k in range(KD):
                            if j == 0:
                                drained_wait(pe, norm_fill + k)
                            last = pe.matmul(bank(n)[:, 0:cols], w[:, k, (j % 4) * P:(j % 4 + 1) * P], HT[:, k, 0:cols], start=k == 0, stop=k == KD - 1)
                        fill_done(last, n)
                    n = f0 + turned
                    for unit in v_units:
                        loaded_wait(pe, u0 + unit)
                        w = slot(u0 + unit, BANK)
                        for t in range(v_tiles):
                            free_wait(pe, n)
                            for k in range(KD):
                                last = pe.matmul(bank(n), HT[:, k, t * P:(t + 1) * P], w[:, k, :], start=k == 0, stop=k == KD - 1)
                            fill_done(last, n)
                            n += 1

                if stage.kind == "diff":
                    for n in range(f0 - BANKS, f0):
                        drained_wait(pe, n)
                    for n, (what, s) in enumerate(diff_order(), f0):
                        h, i = divmod(s, T)
                        rows = slice(i * P, (i + 1) * P)
                        free_wait(pe, n)
                        if what in ("map0", "map1"):
                            m = HD * (what == "map1")
                            last = pe.matmul(bank(n)[:, 0:(i + 1) * P], QT[m:m + HD, h, rows], KT[m:m + HD, h, 0:(i + 1) * P], start=True, stop=True)
                        if what == "turned":
                            pe.wait_ge(diff_ready, s + 1)
                            for kt in range(i + 1):
                                last = pe.transpose(bank(n)[:, kt * P:(kt + 1) * P], SA(s)[:, 0, kt * P:(kt + 1) * P], ident)
                        if what == "values":
                            drained_wait(pe, n - 1)
                            for kt in range(i + 1):
                                last = pe.matmul(bank(n)[:, 0:P], AT(s)[:, kt * P:(kt + 1) * P], V[:, kt, h * P:(h + 1) * P], start=kt == 0, stop=kt == i)
                        fill_done(last, n)

                if stage.kind == "stick":
                    for n in range(f0 - BANKS, f0):
                        drained_wait(pe, n)

                    def head_rows(g):
                        return slice(HD * (g % 2), HD * (g % 2) + HD)

                    def scores(g):
                        if g >= 2:
                            pe.wait_ge(a_raw, g - 1)
                        rows, c, z = head_rows(g), g // 2, stick_view(g)
                        for kt in (0, 1, 3, 2):
                            last = pe.matmul(z[:, STICK_AT[kt]:STICK_AT[kt] + STICK_N[kt]], KT[rows, c, kt * P:(kt + 1) * P],
                                             QT[rows, c, kt * P:], start=kt != 3, stop=True, skip_group_check=True)
                        last.then_inc(z_full, 1)

                    def sums(g):
                        pe.wait_ge(sp_ready, g + 1)
                        z, sp_rows = stick_view(g), E_BUF[g % 2]
                        for kt in range(T):
                            for jt in range(kt, T):
                                at = STICK_AT[kt] + P * (jt - kt)
                                last = pe.matmul(z[:, at:at + STICK_N[jt]], const("neg_ge" if jt == kt else "neg_ones"),
                                                 sp_rows[:, STICK_AT[jt]:STICK_AT[jt] + STICK_N[jt]], start=False, stop=True, skip_group_check=True)
                        last.then_inc(r_full, 1)

                    def values(g):
                        pe.wait_ge(a_ready, g + 1)
                        if g % 2 == 0 and g >= 4:
                            pe.wait_ge(o_drained, g // 2 - 1)
                        rows, a = head_rows(g), A_BUF[g % 2]
                        for kt in range(T):
                            last = pe.matmul(PS[rows, 6 + (g // 2) % 2, kt * P:], V[:, kt, g * HD:(g + 1) * HD],
                                             a[:, STICK_AT[kt]:STICK_AT[kt] + STICK_N[kt]], start=kt == 0, stop=True, skip_group_check=True)
                        last.then_inc(o_full, 1)

                    scores(0)
                    for g in range(SB_HEADS):
                        if g + 1 < SB_HEADS:
                            scores(g + 1)
                        sums(g)
                        if g:
                            values(g - 1)
                    values(SB_HEADS - 1)

                if stage.kind in ("otrans", "mtrans", "xtrans"):
                    if stage.kind == "otrans":
                        pe.wait_ge(group_normed, normed_after(stage))
                    elif stage.kind == "mtrans":
                        pe.wait_ge(mixed, 3 * (stage.turn + 1))
                    else:
                        for n in range(f0 - BANKS, f0):
                            drained_wait(pe, n)
                    for c in range(XH if stage.kind == "xtrans" else KD):
                        n = f0 + c
                        free_wait(pe, n)
                        for t in range(T):
                            last = pe.transpose(bank(n)[:, t * P:(t + 1) * P], XN[:, t, c * P:(c + 1) * P], ident)
                        fill_done(last, n)

                if stage.kind in ("attn_out", "mix_out", "x_out"):
                    chunks = XH if stage.kind == "x_out" else KD
                    w = [slot(u0, D, XH)[:, :, h * BANK:(h + 1) * BANK] if stage.kind == "x_out" else slot(u0 + h, BANK) for h in range(2)]
                    for t in range(T):
                        for half in range(2):
                            n = f0 + 2 * t + half
                            free_wait(pe, n)
                            if t == 0:
                                loaded_wait(pe, u0 + (0 if stage.kind == "x_out" else half))
                            for k in range(chunks):
                                if n == f0:
                                    if stage.kind == "attn_out" and layer == 1:
                                        pe.wait_ge(o_drained, k + 1)
                                    else:
                                        drained_wait(pe, f0 - chunks + k)
                                last = pe.matmul(bank(n), HT[:, k, t * P:(t + 1) * P], w[half][:, k, :], start=k == 0, stop=k == chunks - 1)
                            fill_done(last, n)

                if stage.kind == "route":
                    free_wait(pe, f0)
                    pe.wait_ge(router_in, 64 * (layer + 1))
                    for k in range(KD):
                        drained_wait(pe, f0 - KD + k)
                    for t in range(T):
                        for k in range(KD):
                            last = pe.matmul(bank(f0)[:, t * 36:t * 36 + 36], HT[:, k, t * P:(t + 1) * P], RW[:, k, :], start=k == 0, stop=k == KD - 1)
                    fill_done(last, f0)
                    free_wait(pe, f0 + 1)
                    pe.wait_ge(assigned, layer + 1)
                    a = RT("assigned")
                    for t in range(T):
                        for j in range(t + 1):
                            pe.matmul(bank(f0 + 1)[:, t * EXPERTS:(t + 1) * EXPERTS], const("before") if j == t else ones, a[:, j, :], start=j == 0, stop=j == t)
                    for t in range(T):
                        last = pe.matmul(bank(f0 + 1)[:, T * EXPERTS:(T + 1) * EXPERTS], ones, a[:, t, :], start=t == 0, stop=t == T - 1)
                    fill_done(last, f0 + 1)
                    free_wait(pe, f0 + 2)
                    pe.wait_ge(one_hots, layer + 1)
                    for j in range(2 * T):
                        last = pe.matmul(bank(f0 + 2)[:, 0:TABLE], RT("places")[:, j, :], RT("blocks")[:, j, :], start=j == 0, stop=j == 2 * T - 1)
                    fill_done(last, f0 + 2)

                if stage.kind == "experts":
                    s = blocks[layer]

                    def rows_by_feature():
                        for k in range(KD):
                            last = pe.transpose(PS[:, k // 4, (k % 4) * P:(k % 4 + 1) * P], XG[:, k::KD], ident)
                        last.then_inc(s.rows_turned, 1)

                    for n in range(max(0, f0 - BANKS), f0):
                        drained_wait(pe, n)
                    pe.wait_ge(blocks_ready, layer + 1)
                    n_blocks = pe.value_load(CTRL[0:1, 0:1], min_val=1, max_val=MAX_BLOCKS)
                    for used in s.used:
                        pe.sem_inc(used, 1)
                    pe.wait_ge(s.gathered, 16)
                    rows_by_feature()
                    with pe.Fori(0, n_blocks) as b:
                        pe.wait_ge(s.first_scaled, b + 1)
                        pe.wait_ge(s.last_scaled, b + 1)
                        pe.wait_ge(s.hidden, b + 1)
                        for part, (bk, w) in enumerate(((2, W_GATE), (3, W_UP))):
                            for half in range(2):
                                pe.wait_ge(s.loaded[2 * part + half], 16 * b + 16)
                                for k in range(4 * half, 4 * half + 4):
                                    last = pe.matmul(PS[:, bk, :], XGT[:, k, :], w[:, k, :], start=k == 0, stop=k == KD - 1)
                                last.then_inc(s.used[2 * part + half], 1)
                        pe.wait_ge(s.gathered, 16 * b + 32)
                        rows_by_feature()
                        pe.wait_ge(s.hidden, b + 2)
                        for k in range(KH):
                            last = pe.transpose(PS[:, 4, k * P:(k + 1) * P], HID[:, k::KH], ident)
                        last.then_inc(s.hidden_turned, 1)
                        pe.wait_ge(s.hidden_ready, b + 1)
                        for half, read in enumerate((s.y_left, s.y_right)):
                            pe.wait_ge(read, b + 1)
                            pe.wait_ge(s.loaded[4 + half], 16 * b + 16)
                            for k in range(KH):
                                last = pe.matmul(PS[:, 5 + half, :], HIDT[:, k, :], W_DOWN[:, half, k, :], start=k == 0, stop=k == KH - 1)
                            last.then_inc(s.used[4 + half], 1)
                    pe.wait_ge(experts_over, layer + 1)

                if stage.kind == "project":
                    for j, (_, width) in enumerate(IN_CHUNKS):
                        loaded_wait(pe, u0 + j)
                        w = slot(u0 + j, width)
                        for t in range(T):
                            n = f0 + T * j + t
                            free_wait(pe, n)
                            for k in range(KD):
                                if n == f0:
                                    drained_wait(pe, f0 - KD + k)
                                last = pe.matmul(bank(n)[:, 0:width], HT[:, k, t * P:(t + 1) * P], w[:, k, :], start=k == 0, stop=k == KD - 1)
                            fill_done(last, n)

                if stage.kind == "latent_up":
                    pe.wait_ge(group_normed, normed_after(stage))
                    for j in range(4):
                        n = f0 + j
                        at = (C_CQ, C_CKV)[j // 2] + j % 2
                        free_wait(pe, n)
                        for t in range(T):
                            last = pe.transpose(bank(n)[:, t * P:(t + 1) * P], PR[:, t, at:at + RANK - j % 2:2], ident)
                        fill_done(last, n)
                    for j, width in enumerate((MH * MQ, MH * (NOPE + MV))):
                        loaded_wait(pe, u0 + j)
                        w = slot(u0 + j, width, 2)
                        for t in range(T):
                            for half in range(2):
                                n = f0 + 4 + 2 * T * j + 2 * t + half
                                free_wait(pe, n)
                                for k in range(2):
                                    if t == 0 and half == 0:
                                        drained_wait(pe, f0 + 2 * j + k)
                                    last = pe.matmul(bank(n)[:, 0:width // 2], HT[:, 2 * j + k, t * P:(t + 1) * P],
                                                     w[:, k, half * width // 2:(half + 1) * width // 2], start=k == 0, stop=k == 1)
                                fill_done(last, n)

                if stage.kind in ("latent", "xattn"):
                    order, heads, _, span, dv, _ = soft_plan(stage)
                    latent = stage.kind == "latent"
                    for n in range(f0 - BANKS, f0):
                        drained_wait(pe, n)
                    if latent:
                        pe.wait_ge(mixer_up, 2 * (stage.turn + 1))
                    made = {}
                    for n, (what, s) in enumerate(order, f0):
                        h, i = divmod(s, T)
                        made[what, s] = n
                        free_wait(pe, n)
                        if what in ("turn_q", "turn_k"):
                            src = QM if what == "turn_q" else KM
                            for t in range(T):
                                last = pe.transpose(bank(n)[0:MQ, t * P:(t + 1) * P], src[:, t, h, :], ident)
                        if what == "scores":
                            L = span(i)
                            if latent:
                                if i == 0:
                                    drained_wait(pe, made["turn_q", s])
                                    drained_wait(pe, made["turn_k", s])
                                pe.matmul(bank(n)[:, 0:L], LQT(h)[0:MQ, i * P:(i + 1) * P], LKT(h)[0:MQ, 0:L], start=True, stop=False, skip_group_check=True)
                                last = pe.matmul(bank(n)[:, L - P:L], ident, const("causal"), start=False, stop=True, skip_group_check=True)
                            else:
                                last = pe.matmul(bank(n)[:, 0:L], XQT[:, h, i * P:(i + 1) * P], XKT[:, h, :], start=True, stop=True)
                        if what == "turned":
                            drained_wait(pe, made["scores", s])
                            for kt in range(span(i) // P):
                                last = pe.transpose(bank(n)[:, kt * P:(kt + 1) * P], SP1(stage, s)[:, kt * P:(kt + 1) * P], ident)
                        if what == "values":
                            drained_wait(pe, n - 1)
                            for kt in range(span(i) // P):
                                v = VM[:, kt, h, :] if latent else XV[:, kt, h * P:(h + 1) * P]
                                last = pe.matmul(bank(n)[:, 0:dv], AT1(stage, s)[:, kt * P:(kt + 1) * P], v, start=kt == 0, stop=kt == span(i) // P - 1)
                        fill_done(last, n)

                if stage.kind == "gla":
                    f_glr, f_z, f_b, f_last, f_dec = f0, f0 + 1, f0 + 3, f0 + 5, f0 + 7
                    free_wait(pe, f_glr)
                    for t in range(T):
                        last = pe.transpose(bank(f_glr)[0:16, t * P:(t + 1) * P], PR[:, t, C_GLR:C_GLR + 16], ident)
                    fill_done(last, f_glr)
                    drained_wait(pe, f_glr)
                    pe.wait_ge(mixer_in, 96 * (stage.turn + 1))
                    for t in range(T):
                        n = f_z + t // 2
                        if t % 2 == 0:
                            free_wait(pe, n)
                        last = pe.matmul(bank(n)[:, (t % 2) * GQK:(t % 2 + 1) * GQK], GLT[0:17, t * P:(t + 1) * P], GW[0:17, :], start=True, stop=True)
                        if t % 2:
                            fill_done(last, n)
                    pe.wait_ge(soft_ready, 2 * (stage.turn + 1))
                    for first, table in ((f_b, "gla_cum"), (f_last, "gla_last")):
                        for j in range(2):
                            free_wait(pe, first + j)
                            fill_done(pe.matmul(bank(first + j)[:, 0:2 * GQK], const(table), SOFT[:, 2 * j:2 * j + 2, :].rearrange("p t n -> p (t n)"), start=True, stop=True), first + j)
                    free_wait(pe, f_dec)
                    for h in range(GH):
                        for t in range(T):
                            last = pe.matmul(bank(f_dec)[0:GDK, h * 8 + 2 * t:h * 8 + 2 * t + 2], SOFT[:, t, h * GDK:(h + 1) * GDK], const("gla_chunk"), start=True, stop=True)
                    fill_done(last, f_dec)
                    f = f0 + 8
                    pe.wait_ge(decayed, 3 * (stage.turn + 1))
                    for h in range(GH):
                        for src in (QD, KI):
                            free_wait(pe, f)
                            for t in range(T):
                                last = pe.transpose(bank(f)[0:GDK, t * P:(t + 1) * P], src[:, t, h * GDK:(h + 1) * GDK], ident)
                            fill_done(last, f)
                            f += 1

                    def outputs(h, n):
                        free_wait(pe, n)
                        drained_wait(pe, gla_fill(stage, "scores", h))
                        pe.wait_ge(state_ready, GH * stage.turn + h + 1)
                        for t in range(T):
                            cols = slice(t * GDV, (t + 1) * GDV)
                            last = pe.matmul(bank(n)[:, cols], GAT(h)[:, t, :], PR[:, t, C_GV + h * GDV:C_GV + (h + 1) * GDV], start=True, stop=False, skip_group_check=True)
                            for half in range(2):
                                if 2 * t + half:
                                    rows = slice(CHUNK * half, CHUNK * (half + 1))
                                    last = pe.matmul(bank(n)[rows, cols], GQT[0:GDK, h, t * P + CHUNK * half:t * P + CHUNK * (half + 1)],
                                                     GST(h)[0:GDK, 2 * t + half, :], start=False, stop=True, skip_group_check=True)
                        fill_done(last, n)

                    for h in range(GH):
                        for part in range(2):
                            n = gla_fill(stage, "update", h, part)
                            free_wait(pe, n)
                            for j in range(part, 7, 2):
                                rows = slice(CHUNK * part, CHUNK * (part + 1))
                                last = pe.matmul(bank(n)[0:GDK, (j // 2) * GDV:(j // 2 + 1) * GDV], KE[rows, j // 2, h * GDK:(h + 1) * GDK],
                                                 PR[rows, j // 2, C_GV + h * GDV:C_GV + (h + 1) * GDV], start=True, stop=True)
                            fill_done(last, n)
                        n = gla_fill(stage, "scores", h)
                        free_wait(pe, n)
                        drained_wait(pe, f0 + 8 + 2 * h)
                        drained_wait(pe, f0 + 9 + 2 * h)
                        for t in range(T):
                            cols = slice(t * P, (t + 1) * P)
                            last = pe.matmul(bank(n)[:, cols], GKT[0:GDK, h, cols], GQT[0:GDK, h, cols], start=True, stop=True)
                        fill_done(last, n)
                        if h:
                            outputs(h - 1, gla_fill(stage, "outputs", h - 1))
                    outputs(GH - 1, gla_fill(stage, "outputs", GH - 1))

                if stage.kind == "conv":
                    pe.wait_ge(conv_in, stage.turn + 1)
                    for t in range(T):
                        n = f0 + t // 2
                        if t % 2 == 0:
                            free_wait(pe, n)
                        pieces = [("shift1", CU1[:, t, :]), ("shift2", CU0[:, t, :])]
                        if t:
                            pieces += [("carry1", CU1[:, t - 1, :]), ("carry2", CU0[:, t - 1, :])]
                        for j, (table, u) in enumerate(pieces):
                            last = pe.matmul(bank(n)[:, (t % 2) * CW:(t % 2 + 1) * CW], const(table), u, start=j == 0, stop=j == len(pieces) - 1)
                        if t % 2:
                            fill_done(last, n)

        @block.scalar
        def _(act):
            own = [0]

            def settle(instruction):
                own[0] += 1
                instruction.then_inc(act_done, 1)
                act.wait_ge(act_done, own[0])

            def drained(instruction, n):
                instruction.then_inc(bank_drained[n % BANKS], 1)

            act.wait_ge(inputs_in, 16 * N_SMALL)
            act.activation(CCOL[:, 1, :], CCOL[:, 0, :], ACT.Exp, scale=-1.0).then_inc(cond_exp, 1)
            for stage in plan:
                f0, layer = stage.fill, stage.arg

                if stage.kind == "mod":
                    for q, part in enumerate((0, 1, 3, 4)):
                        for half in range(2):
                            n = f0 + 2 * part + half
                            full_wait(act, n)
                            drained(act.copy(MODROW[:, q, half * BANK:(half + 1) * BANK], bank(n)[0:1, :]), n)
                    if stage.turn == 0:
                        act.wait_ge(lambda_sums, 1)
                        act.activation(LAM[:, 2:4], LAM[:, 0:2], ACT.Exp).then_inc(lambda_exp, 1)

                if stage.kind in ("norm", "final"):
                    src, tiles = (X, T) if stage.kind == "final" else gains(stage)[0:2]
                    if src is not X:
                        act.wait_ge(memory_in, 16 * (stage.arg[1] + 1))
                        full_wait(act, f0 - XH - 1)
                    for t in range(tiles):
                        if src is X:
                            residual_wait(act, stage, t)
                        last = act.activation(XN[:, t, :], src[:, t, :], ACT.Square, accum_out=SUMSQ[:, t:t + 1])
                    last.then_inc(sumsq_ready, 1)
                if stage.kind == "norm":
                    _, tiles, gain, shift = gains(stage)
                    if stage.arg[0] == "first2":
                        for t in range(T):
                            act.wait_ge(xn_ready, stage.tiles_before + t + 1)
                            act.dma_start(xn_d[t * P:(t + 1) * P, :], XN[:, t, :]).then_inc(xn_stored, 16)
                    for k in range(0, KD, 2):
                        n = f0 + k
                        full_wait(act, n)
                        bias = 0.0 if shift is None else shift[:, k:k + 1]
                        drained(act.activation(HT[:, k, 0:tiles * P], bank(n)[:, 0:tiles * P], ACT.Identity, bias=bias, scale=gain[:, k:k + 1]), n)

                if stage.kind == "qkv":
                    for j in range(8):
                        full_wait(act, f0 + j)
                        drained(act.mul(QT[:, j, :], bank(f0 + j), HD ** -0.5), f0 + j)
                    for j in range(0, 8, 2):
                        n = f0 + 16 + j
                        full_wait(act, n)
                        drained(act.copy(V[:, j % T, (j // T) * BANK:(j // T + 1) * BANK], bank(n)), n)

                if stage.kind == "diff":
                    made = {what_s: n for n, what_s in enumerate(diff_order(), f0)}
                    steps = DIFF_HEADS * T
                    for r in range(steps + AHEAD + 1):
                        if r < steps:
                            L = P * (r % T + 1)
                            act.wait_ge(negmax_ready, r + 1)
                            for m in range(2):
                                act.activation(SA(r)[:, m, 0:L], SA(r)[:, m, 0:L], ACT.Exp, bias=MX[:, r % 3, m:m + 1],
                                               accum_out=SUM[:, r % 3, m:m + 1]).then_inc(diff_exp, 1)
                        s = r - AHEAD
                        if 0 <= s < steps:
                            L, n = P * (s % T + 1), made["turned", s]
                            full_wait(act, n)
                            if s >= 2:
                                full_wait(act, made["values", s - 2])
                            drained(act.copy(AT(s)[:, 0:L], bank(n)[:, 0:L]), n)
                        s = r - AHEAD - 1
                        if s >= 0:
                            h, i = divmod(s, T)
                            n = made["values", s]
                            full_wait(act, n)
                            drained(act.copy(XN[:, i, h * P:(h + 1) * P], bank(n)[:, 0:P]), n)

                if stage.kind == "stick":
                    def logs(g):
                        act.wait_ge(z_clamped, g + 1)
                        e = E_BUF[g % 2]
                        settle(act.activation(e, e, ACT.Exp))
                        act.activation(e, e, ACT.Ln, bias=1.0).then_inc(z_log, 1)

                    logs(0)
                    for g in range(SB_HEADS):
                        if g + 1 < SB_HEADS:
                            logs(g + 1)
                        act.wait_ge(r_full, g + 1)
                        if g >= 2:
                            act.wait_ge(o_full, g - 1)
                        act.activation(A_BUF[g % 2], stick_view(g)[:, 0:STICK_W], ACT.Exp).then_inc(a_raw, 1)

                if stage.kind == "otrans":
                    for n in range(f0 - BANKS, f0):
                        drained_wait(act, n)
                    for t in range(T):
                        act.activation(HT[:, 2 * t:2 * t + 2, :].rearrange("p a n -> p (a n)"), XN[:, t, :], ACT.Square).then_inc(squares_ready, 1)
                if stage.kind == "latent_up":
                    for n in range(f0 - BANKS, f0):
                        drained_wait(act, n)
                    for j, at in enumerate((C_CQ, C_CKV)):
                        for t in range(T):
                            last = act.activation(SCR[:, (j * T + t) * RANK:(j * T + t + 1) * RANK], PR[:, t, at:at + RANK], ACT.Square, accum_out=SUMSQ[:, j * T + t:j * T + t + 1])
                    last.then_inc(squares_ready, 1)
                    for j in range(2 * T):
                        n = f0 + 4 + 2 * T + j
                        t, h = j // 2, 3 * (j % 2)
                        full_wait(act, n)
                        kv = bank(n)[:, 0:3 * (NOPE + MV)].rearrange("p (h n) -> p h n", h=3)
                        act.copy(KM[:, t, h:h + 3, 0:NOPE], kv[:, :, 0:NOPE])
                        drained(act.copy(VM[:, t, h:h + 3, :], kv[:, :, NOPE:]), n)
                    if stage.turn == 0:
                        act.wait_ge(angles, 1)
                        act.activation(SIN[:, :, :], SIN[:, :, :], ACT.Sin)
                        act.activation(COS[:, :, :], COS[:, :, :], ACT.Sin).then_inc(rope_ready, 1)

                if stage.kind in ("otrans", "mtrans", "xtrans"):
                    for c in range(0, XH if stage.kind == "xtrans" else KD, 2):
                        n = f0 + c
                        full_wait(act, n)
                        scale = SUBG[:, 1:2] if stage.kind == "otrans" else 1.0
                        drained(act.activation(HT[:, c, :], bank(n), ACT.Identity, scale=scale), n)

                if stage.kind == "route":
                    act.wait_ge(group_shift, layer + 1)
                    act.activation(RT("gexp"), RT("gshift"), ACT.Exp).then_inc(group_exp, 1)
                    act.wait_ge(pair_diff, layer + 1)
                    act.activation(RT("gapexp"), RT("gap"), ACT.Exp).then_inc(pair_exp, 1)

                if stage.kind == "experts":
                    s = blocks[layer]
                    gain, shift = COLS[:, 3, :], COLS[:, 2, :]

                    def first_chunks():
                        for k in range(KD // 2):
                            last = act.activation(XGT[:, k, :], PS[:, k // 4, (k % 4) * P:(k % 4 + 1) * P], ACT.Identity, bias=shift[:, k:k + 1], scale=gain[:, k:k + 1])
                        last.then_inc(s.first_scaled, 1)

                    act.wait_ge(blocks_ready, layer + 1)
                    n_blocks = act.value_load(CTRL[0:1, 0:1], min_val=1, max_val=MAX_BLOCKS)
                    act.sem_inc(s.y_left, 1)
                    act.wait_ge(s.rows_turned, 1)
                    first_chunks()
                    with act.Fori(0, n_blocks) as b:
                        act.wait_ge(s.used[1], b + 2)
                        act.activation(GE, PS[:, 2, :], ACT.Exp, scale=-1.0).then_inc(s.gate_exp, 1)
                        act.wait_ge(s.rows_turned, b + 2)
                        first_chunks()
                        act.wait_ge(s.hidden_turned, b + 1)
                        act.copy(HIDT.rearrange("p k n -> p (k n)"), PS[:, 4, :]).then_inc(s.hidden_ready, 1)
                        act.wait_ge(s.used[4], b + 2)
                        act.wait_ge(s.y_free, b + 1)
                        act.copy(YB[:, 0:BANK], PS[:, 5, :]).then_inc(s.y_left, 1)

                if stage.kind == "combine":
                    act.wait_ge(experts_over, layer + 1)
                    for t in range(T):
                        for j in range(2):
                            act.dma_start(Y2[:, j, t, :], y_d[j * S + t * P:j * S + (t + 1) * P, :]).then_inc(rows_back, 16)

                if stage.kind == "project":
                    for j, (at, width) in enumerate(IN_CHUNKS):
                        for t in range(0, T, 2):
                            n = f0 + T * j + t
                            full_wait(act, n)
                            drained(act.copy(PR[:, t, at:at + width], bank(n)[:, 0:width]), n)

                if stage.kind in ("latent", "xattn"):
                    order, heads, scale, span, dv, _ = soft_plan(stage)
                    made = {what_s: n for n, what_s in enumerate(order, f0)}
                    base = soft_base(stage)
                    steps = heads * T
                    for r in range(steps + AHEAD):
                        if r < steps:
                            L, n = span(r % T), made["scores", r]
                            if stage.kind == "latent" and r % T == 0:
                                h = r // T
                                nq = made["turn_q", r]
                                full_wait(act, nq)
                                if h >= 2:
                                    full_wait(act, made["scores", r - T - 1])
                                drained(act.copy(LQT(h)[0:MQ, :], bank(nq)[0:MQ, :]), nq)
                            act.wait_ge(negmax_ready, base + r + 1)
                            if r >= 3:
                                full_wait(act, made["turned", r - 3])
                            drained(act.activation(SP1(stage, r)[:, 0:L], bank(n)[:, 0:L], ACT.Exp, bias=MX[:, r % 4, 0:1], scale=scale,
                                                   accum_out=SUM[:, r % 4, 0:1]), n)
                        s = r - AHEAD
                        if s >= 0:
                            L, n = span(s % T), made["turned", s]
                            full_wait(act, n)
                            if s >= 2:
                                full_wait(act, made["values", s - 2])
                            drained(act.copy(AT1(stage, s)[:, 0:L], bank(n)[:, 0:L]), n)

                if stage.kind == "gla":
                    f_z, f_b, f_last, f_dec = f0 + 1, f0 + 3, f0 + 5, f0 + 7
                    full_wait(act, f0)
                    act.wait_ge(gla_clear, 2 * stage.turn + 1)
                    drained(act.copy(GLT[0:16, :], bank(f0)[0:16, :]), f0)
                    act.wait_ge(soft_in, 2 * (stage.turn + 1))
                    soft = SOFT.rearrange("p t n -> p (t n)")
                    settle(act.activation(soft, soft, ACT.Exp))
                    act.activation(soft, soft, ACT.Ln, bias=1.0).then_inc(soft_log, 1)
                    for j in range(2):
                        n = f_b + j
                        full_wait(act, n)
                        b = bank(n)[:, 0:2 * GQK]
                        act.activation(QD[:, 2 * j:2 * j + 2, :].rearrange("p t n -> p (t n)"), b, ACT.Exp)
                        act.activation(KI[:, 2 * j:2 * j + 2, :].rearrange("p t n -> p (t n)"), b, ACT.Exp, scale=-1.0)
                        drained(act.copy(KE[:, 2 * j:2 * j + 2, :].rearrange("p t n -> p (t n)"), b), n)
                    full_wait(act, f_dec)
                    drained(act.activation(DEC[0:GDK, :], bank(f_dec)[0:GDK, 0:32], ACT.Exp), f_dec)
                    act.wait_ge(decayed, 3 * stage.turn + 1)
                    act.activation(KE.rearrange("p t n -> p (t n)"), KE.rearrange("p t n -> p (t n)"), ACT.Exp).then_inc(decays_ready, 1)
                    for h in range(GH):
                        n = f0 + 8 + 2 * h
                        full_wait(act, n)
                        drained(act.copy(GQT[0:GDK, h, :], bank(n)[0:GDK, :]), n)
                    for h in range(GH):
                        n = gla_fill(stage, "outputs", h)
                        full_wait(act, n)
                        drained(act.copy(XN[:, :, h * GDV:(h + 1) * GDV], bank(n)[:, 0:T * GDV].rearrange("p (t n) -> p t n", t=T)), n)
                    for h in range(GH):
                        drained_wait(act, gla_fill(stage, "outputs", h))
                    act.activation(SCR[:, 0:T * GV].rearrange("p (t n) -> p t n", t=T), XN[:, :, 0:GV], ACT.Square).then_inc(squares_ready, 1)
                    for j, (at, width) in enumerate(GATES):
                        if j:
                            act.wait_ge(mixed, 3 * stage.turn + j)
                        act.activation(SGATE[:, :, 0:width], PR[:, :, at:at + width], ACT.Exp, scale=-1.0).then_inc(gate_exp, 1)


        @block.gpsimd
        def _(pool):
            own = [0]

            def settle(instruction):
                own[0] += 1
                instruction.then_inc(pool_done, 1)
                pool.wait_ge(pool_done, own[0])

            def rstd(n, width, eps, ready):
                settle(pool.tensor_scalar(RSTD[:, 0:n], SUMSQ[:, 0:n], 1.0 / width, eps, ALU.mult, ALU.add))
                pool.tensor_tensor(RSTD[:, 0:n], RSTD[:, 0:n], const("minus_half")[:, 0:n], ALU.pow).then_inc(ready, 1)

            def past_only(buf, done):
                for at in STICK_AT:
                    diagonal = buf[:, at:at + P]
                    last = pool.affine_select(out=diagonal, in_=diagonal, compare_op=ALU.is_gt, fill=0.0, base=0, pattern=[[1, P]], channel_multiplier=-1)
                last.then_inc(done, 1)

            pool.wait_ge(inputs_in, 16 * N_SMALL)
            for stage in plan:
                layer = stage.arg
                if stage.kind in ("norm", "final"):
                    pool.wait_ge(sumsq_ready, stage.scaled + 1)
                    rstd(T if stage.kind == "final" else gains(stage)[1], D, 1e-6, rstd_ready)
                if stage.kind == "otrans":
                    pool.wait_ge(group_sums, 1)
                    rstd(T * DIFF_HEADS, P, 1e-5, group_rstd)
                if stage.kind == "latent_up":
                    pool.wait_ge(squares_ready, squares_before(stage) + 1)
                    rstd(2 * T, RANK, 1e-6, group_rstd)
                if stage.kind == "gla":
                    for n in range(stage.fill - BANKS, stage.fill):
                        drained_wait(pool, n)
                    pool.memset(GLT[0:32, :], 1.0).then_inc(gla_clear, 1)
                    pool.memset(SCR[:, 3616:3616 + 2 * BANK], 0.0).then_inc(gla_clear, 1)
                    pool.wait_ge(group_sums, 2 + stage.turn)
                    rstd(T * GH, GDV, 1e-6, group_rstd)
                if stage.kind == "stick":
                    for g in range(SB_HEADS + 1):
                        if g < SB_HEADS:
                            pool.wait_ge(sp_raw, g + 1)
                            past_only(E_BUF[g % 2], sp_ready)
                        if g:
                            pool.wait_ge(a_raw, g)
                            past_only(A_BUF[(g - 1) % 2], a_ready)
                if stage.kind == "experts":
                    s = blocks[layer]
                    pool.wait_ge(blocks_ready, layer + 1)
                    pool.wait_ge(xn_stored, 16 * T * (layer + 1))
                    n_blocks = pool.value_load(CTRL[0:1, 0:1], min_val=1, max_val=MAX_BLOCKS)
                    settle(pool.memset(XG, 0.0))
                    pool.sem_inc(s.y_free, 1)
                    settle(pool.tensor_copy(ROWS_IN[:, :], TABI[:, 0, 0:1]))
                    pool.indirect_dma_start(out=XG, out_offset=None, in_=xn_d, in_offset=bass.IndirectOffsetOnAxis(ap=ROWS_IN[:, 0:1], axis=0),
                                            bounds_check=S - 1, oob_is_err=False).then_inc(s.gathered, 16)
                    with pool.Fori(0, n_blocks) as b:
                        next_in = TABI[:, 0, bass.ds(b + 1, 1)]
                        this_out = TABI[:, 1, bass.ds(b, 1)]
                        pool.wait_ge(s.rows_turned, b + 1)
                        pool.tensor_copy(ROWS_IN[:, :], next_in)
                        pool.drain()
                        pool.indirect_dma_start(out=XG, out_offset=None, in_=xn_d, in_offset=bass.IndirectOffsetOnAxis(ap=ROWS_IN[:, 0:1], axis=0),
                                                bounds_check=S - 1, oob_is_err=False).then_inc(s.gathered, 16)
                        pool.wait_ge(s.y_left, b + 2)
                        pool.wait_ge(s.y_right, b + 2)
                        pool.tensor_copy(ROWS_OUT[:, :], this_out)
                        pool.drain()
                        pool.indirect_dma_start(out=y_d, out_offset=bass.IndirectOffsetOnAxis(ap=ROWS_OUT[:, 0:1], axis=0), in_=YB, in_offset=None,
                                                bounds_check=2 * S - 1, oob_is_err=False).then_inc(s.scattered, 16)
                        pool.wait_ge(s.scattered, 16 * b + 16)
                        pool.sem_inc(s.y_free, 1)
                    pool.drain().then_inc(experts_over, 1)

        @block.vector
        def _(dve):
            own = [0]

            def settle(instruction):
                own[0] += 1
                instruction.then_inc(dve_done, 1)
                dve.wait_ge(dve_done, own[0])

            def drained(instruction, n):
                instruction.then_inc(bank_drained[n % BANKS], 1)

            def gated(j, stage):
                at, width = GATES[j]
                g = SGATE[:, :, 0:width]
                dve.wait_ge(gate_exp, 3 * stage.turn + j + 1)
                settle(dve.tensor_scalar_add(g, g, 1.0))
                settle(dve.reciprocal(g, g))
                settle(dve.tensor_tensor(g, g, PR[:, :, at:at + width], ALU.mult))
                return g

            dve.wait_ge(inputs_in, 16 * N_SMALL)
            dve.wait_ge(cond_exp, 1)
            settle(dve.tensor_scalar_add(CCOL[:, 2, :], CCOL[:, 1, :], 1.0))
            settle(dve.reciprocal(CCOL[:, 3, :], CCOL[:, 2, :]))
            settle(dve.tensor_tensor(CCOL[:, 2, :], CCOL[:, 3, :], CCOL[:, 0, :], ALU.mult))
            settle(dve.tensor_tensor(LAMV[:, 0, :], LAMV[:, 0, :], LAMV[:, 1, :], ALU.mult))
            settle(dve.tensor_tensor(LAMV[:, 2, :], LAMV[:, 2, :], LAMV[:, 3, :], ALU.mult))
            dve.reduce_sum(LAM[:, 0:1], LAMV[:, 0, :], AX)
            dve.reduce_sum(LAM[:, 1:2], LAMV[:, 2, :], AX).then_inc(lambda_sums, 1)
            settle(dve.tensor_scalar(SUBG[:, 1:2], SUBG[:, 0:1], 1.0 - DIFF_LAMBDA_INIT, None, ALU.mult))

            for stage in plan:
                f0, layer = stage.fill, stage.arg

                if stage.kind == "mod":
                    dve.tensor_copy(CB, CCOL[:, 2, :].unsqueeze(2).to_broadcast([P, KD, P])).then_inc(cond_rows, 1)
                    for which, part in enumerate((2, 5)):
                        for half in range(2):
                            n = f0 + 2 * part + half
                            full_wait(dve, n)
                            drained(dve.tensor_copy(GB[:, which, half * BANK:(half + 1) * BANK], bank(n)), n)
                    fc = f0 + 12
                    full_wait(dve, fc)
                    cols = bank(fc)[:, 0:4 * KD].rearrange("p (q k) -> p q k", q=4)
                    dve.tensor_copy(COLS[:, 0, :], cols[:, 0, :])
                    dve.tensor_copy(COLS[:, 2, :], cols[:, 2, :])
                    dve.scalar_tensor_tensor(COLS[:, 1, :], cols[:, 1, :], 1.0, GCOL[:, layer, :], ALU.add, ALU.mult)
                    drained(dve.scalar_tensor_tensor(COLS[:, 3, :], cols[:, 3, :], 1.0, GCOL[:, 2 + layer, :], ALU.add, ALU.mult), fc)
                    drained_wait(dve, fc)
                    if stage.turn == 0:
                        dve.wait_ge(lambda_exp, 1)
                        settle(dve.tensor_tensor(LAM[:, 4:5], LAM[:, 3:4], LAM[:, 2:3], ALU.subtract))
                        settle(dve.tensor_scalar_add(LAM[:, 5:6], LAM[:, 4:5], -DIFF_LAMBDA_INIT))

                if stage.kind == "norm":
                    src, tiles, gain, shift = gains(stage)
                    dve.wait_ge(rstd_ready, stage.scaled + 1)
                    for t in range(tiles):
                        dve.tensor_scalar(XN[:, t, :], src[:, t, :], RSTD[:, t:t + 1], None, ALU.mult).then_inc(xn_ready, 1)
                    for k in range(1, KD, 2):
                        n = f0 + k
                        full_wait(dve, n)
                        src_ap, dst = bank(n)[:, 0:tiles * P], HT[:, k, 0:tiles * P]
                        if shift is None:
                            drained(dve.tensor_scalar(dst, src_ap, gain[:, k:k + 1], None, ALU.mult), n)
                        else:
                            drained(dve.tensor_scalar(dst, src_ap, gain[:, k:k + 1], shift[:, k:k + 1], ALU.mult, ALU.add), n)

                if stage.kind == "final":
                    dve.wait_ge(rstd_ready, stage.scaled + 1)
                    dve.wait_ge(gain_in, 16 * (stage.turn + 1))
                    for t in range(T):
                        dve.scalar_tensor_tensor(X[:, t, :], X[:, t, :], RSTD[:, t:t + 1], GB[:, 0, :], ALU.mult, ALU.mult).then_inc(residual_written, 1)

                if stage.kind == "qkv":
                    for j in range(8):
                        full_wait(dve, f0 + 8 + j)
                        drained(dve.tensor_copy(KT[:, j, :], bank(f0 + 8 + j)), f0 + 8 + j)
                    for j in range(1, 8, 2):
                        n = f0 + 16 + j
                        full_wait(dve, n)
                        drained(dve.tensor_copy(V[:, j % T, (j // T) * BANK:(j // T + 1) * BANK], bank(n)), n)

                if stage.kind == "diff":
                    made = {what_s: n for n, what_s in enumerate(diff_order(), f0)}
                    steps = DIFF_HEADS * T
                    for r in range(steps + 1):
                        if r < steps:
                            h, i = divmod(r, T)
                            L, slope = P * (i + 1), 2.0 ** (-8.0 * (h + 1) / DIFF_HEADS)
                            if r >= 3:
                                full_wait(dve, made["turned", r - 3])
                            for m in range(2):
                                n = made[f"map{m}", r]
                                full_wait(dve, n)
                                drained(dve.scalar_tensor_tensor(SA(r)[:, m, 0:L], const("alibi")[:, S - L:S], slope, bank(n)[:, 0:L], ALU.mult, ALU.add), n)
                            for m in range(2):
                                drained_wait(dve, made[f"map{m}", r])
                            dve.tensor_reduce(MX[:, r % 3, :], SA(r)[:, :, 0:L], AX, ALU.max, negate=True).then_inc(negmax_ready, 1)
                        s = r - 1
                        if s >= 0:
                            L = P * (s % T + 1)
                            dve.wait_ge(diff_exp, 2 * (s + 1))
                            settle(dve.reciprocal(RCP[:, s % 3, :], SUM[:, s % 3, :]))
                            settle(dve.tensor_tensor(RCP[:, s % 3, 1:2], RCP[:, s % 3, 1:2], LAM[:, 5:6], ALU.mult))
                            settle(dve.tensor_scalar(SA(s)[:, 0, 0:L], SA(s)[:, 0, 0:L], RCP[:, s % 3, 0:1], None, ALU.mult))
                            dve.scalar_tensor_tensor(SA(s)[:, 0, 0:L], SA(s)[:, 1, 0:L], RCP[:, s % 3, 1:2], SA(s)[:, 0, 0:L], ALU.mult, ALU.add).then_inc(diff_ready, 1)

                if stage.kind == "stick":
                    def clamp(g):
                        dve.wait_ge(z_full, g + 1)
                        if g >= 2:
                            dve.wait_ge(r_full, g - 1)
                        dve.tensor_scalar(E_BUF[g % 2], stick_view(g)[:, 0:STICK_W], 30.0, None, ALU.min).then_inc(z_clamped, 1)

                    clamp(0)
                    for g in range(SB_HEADS):
                        if g + 1 < SB_HEADS:
                            clamp(g + 1)
                        dve.wait_ge(z_log, g + 1)
                        dve.tensor_tensor(E_BUF[g % 2], E_BUF[g % 2], stick_view(g)[:, 0:STICK_W], ALU.max).then_inc(sp_raw, 1)
                        if g % 2 and g >= 3:
                            c = g // 2 - 1
                            dve.wait_ge(o_full, 2 * c + 2)
                            dve.tensor_copy(HT[:, c, :], PS[:, 6 + c % 2, :]).then_inc(o_drained, 1)
                    c = SB_HEADS // 2 - 1
                    dve.wait_ge(o_full, SB_HEADS)
                    dve.tensor_copy(HT[:, c, :], PS[:, 6 + c % 2, :]).then_inc(o_drained, 1)

                if stage.kind == "otrans":
                    for t in range(T):
                        dve.wait_ge(squares_ready, t + 1)
                        last = dve.reduce_sum(SUMSQ[:, t * DIFF_HEADS:(t + 1) * DIFF_HEADS], HT[:, 2 * t:2 * t + 2, :].rearrange("p a (h n) -> p (a h) n", h=4), AX)
                    last.then_inc(group_sums, 1)
                    dve.wait_ge(group_rstd, stage.grouped + 1)
                    for t in range(T):
                        o = XN[:, t, :].rearrange("p (h n) -> p h n", h=DIFF_HEADS)
                        r = RSTD[:, t * DIFF_HEADS:(t + 1) * DIFF_HEADS].unsqueeze(2).to_broadcast([P, DIFF_HEADS, P])
                        dve.tensor_tensor(o, o, r, ALU.mult).then_inc(group_normed, 1)

                if stage.kind in ("otrans", "mtrans", "xtrans"):
                    for c in range(1, XH if stage.kind == "xtrans" else KD, 2):
                        n = f0 + c
                        full_wait(dve, n)
                        if stage.kind == "otrans":
                            drained(dve.tensor_scalar(HT[:, c, :], bank(n), SUBG[:, 1:2], None, ALU.mult), n)
                        else:
                            drained(dve.tensor_copy(HT[:, c, :], bank(n)), n)

                if stage.kind in ("attn_out", "mix_out", "x_out"):
                    for t in range(T):
                        for half in range(2):
                            n = f0 + 2 * t + half
                            cols = slice(half * BANK, (half + 1) * BANK)
                            full_wait(dve, n)
                            if stage.kind == "attn_out":
                                gated_y = SCR[:, 5120 + half * BANK:5120 + (half + 1) * BANK]
                                settle(dve.tensor_tensor(gated_y, bank(n), GB[:, 0, cols], ALU.mult))
                                drained(dve.tensor_tensor(X[:, t, cols], X[:, t, cols], gated_y, ALU.add), n)
                            else:
                                drained(dve.tensor_tensor(X[:, t, cols], X[:, t, cols], bank(n), ALU.add), n)

                if stage.kind == "route":
                    def over(name, n, inner=None):
                        v = RT(name).unsqueeze(2)
                        return v.to_broadcast([P, T, n])

                    def first_of(values, top, hot, mark, n):
                        rev = const("rev")[:, 0:n].unsqueeze(1).to_broadcast([P, T, n])
                        settle(dve.tensor_tensor(RT(hot[0]), values, over(top, n), ALU.is_ge))
                        settle(dve.tensor_tensor(RT(hot[0]), RT(hot[0]), rev, ALU.mult))
                        settle(dve.reduce_max(RT(mark), RT(hot[0]), AX))
                        settle(dve.tensor_tensor(RT(hot[1]), RT(hot[0]), over(mark, n), ALU.is_equal))

                    full_wait(dve, f0)
                    logits = RT("logits")
                    drained(dve.tensor_tensor(logits, bank(f0)[:, 0:T * 36].rearrange("p (t n) -> p t n", t=T), RB[:, :].unsqueeze(1).to_broadcast([P, T, 36]), ALU.add), f0)
                    drained_wait(dve, f0)
                    group_logits = logits[:, :, 0:GROUPS]
                    settle(dve.reduce_max(RT("gmax"), group_logits, AX))
                    dve.tensor_tensor(RT("gshift"), group_logits, over("gmax", GROUPS), ALU.subtract).then_inc(group_shift, 1)
                    first_of(group_logits, "gmax", ("gfirst", "group"), "gtop", GROUPS)
                    settle(dve.tensor_tensor(RT("masked"), logits[:, :, GROUPS:].rearrange("p t (g e) -> p t g e", g=GROUPS),
                                             RT("group").unsqueeze(3).to_broadcast([P, T, GROUPS, PER_GROUP]), ALU.mult))
                    settle(dve.reduce_sum(RT("elogits"), RT("masked").rearrange("p t g e -> p t e g"), AX))
                    settle(dve.reduce_max(RT("top1"), RT("elogits"), AX))
                    first_of(RT("elogits"), "top1", ("first1", "hot1"), "mark1", PER_GROUP)
                    settle(dve.scalar_tensor_tensor(RT("rest"), RT("hot1"), NEG, RT("elogits"), ALU.mult, ALU.add))
                    settle(dve.reduce_max(RT("top2"), RT("rest"), AX))
                    first_of(RT("rest"), "top2", ("first2", "hot2"), "mark2", PER_GROUP)
                    dve.tensor_tensor(RT("gap"), RT("top2"), RT("top1"), ALU.subtract).then_inc(pair_diff, 1)
                    for name, hot in (("assign1", "hot1"), ("assign2", "hot2")):
                        settle(dve.tensor_tensor(RT(name).rearrange("p t (g e) -> p t g e", g=GROUPS),
                                                 RT("group").unsqueeze(3).to_broadcast([P, T, GROUPS, PER_GROUP]),
                                                 RT(hot).unsqueeze(2).to_broadcast([P, T, GROUPS, PER_GROUP]), ALU.mult))
                    dve.tensor_tensor(RT("assigned"), RT("assign1"), RT("assign2"), ALU.add).then_inc(assigned, 1)
                    dve.wait_ge(group_exp, layer + 1)
                    settle(dve.reduce_sum(RT("gsum"), RT("gexp"), AX))
                    settle(dve.reciprocal(RT("gweight"), RT("gsum")))
                    dve.wait_ge(pair_exp, layer + 1)
                    settle(dve.tensor_scalar_add(RT("total"), RT("gapexp"), 1.0))
                    settle(dve.reciprocal(RT("share"), RT("total")))
                    settle(dve.tensor_tensor(WTS[:, 0, :], RT("share"), RT("gweight"), ALU.mult))
                    settle(dve.tensor_tensor(WTS[:, 1, :], WTS[:, 0, :], RT("gapexp"), ALU.mult))
                    full_wait(dve, f0 + 1)
                    dve.tensor_copy(RT("rank"), bank(f0 + 1)[:, 0:T * EXPERTS].rearrange("p (t n) -> p t n", t=T))
                    drained(dve.tensor_copy(RT("count"), bank(f0 + 1)[:, T * EXPERTS:(T + 1) * EXPERTS]), f0 + 1)
                    drained_wait(dve, f0 + 1)
                    settle(dve.tensor_scalar(RT("nblocks"), RT("count"), 0.5, None, ALU.is_gt))
                    for m in range(1, T):
                        settle(dve.scalar_tensor_tensor(RT("nblocks"), RT("count"), P * m + 0.5, RT("nblocks"), ALU.is_gt, ALU.add))
                    settle(dve.tensor_tensor_scan(RT("upto"), ones[:, 0:EXPERTS], RT("nblocks"), 0.0, ALU.mult, ALU.add))
                    settle(dve.tensor_tensor(RT("first"), RT("upto"), RT("nblocks"), ALU.subtract))
                    settle(dve.tensor_scalar(RT("over"), RT("rank"), P - 0.5, None, ALU.is_gt))
                    for m in range(2, T):
                        settle(dve.scalar_tensor_tensor(RT("over"), RT("rank"), P * m - 0.5, RT("over"), ALU.is_gt, ALU.add))
                    settle(dve.scalar_tensor_tensor(RT("place"), RT("over"), -float(P), RT("rank"), ALU.mult, ALU.add))
                    settle(dve.tensor_tensor(RT("blockof"), RT("over"), RT("first").unsqueeze(1).to_broadcast([P, T, EXPERTS]), ALU.add))
                    for j in range(2):
                        for of, value in (("places_of", "place"), ("blocks_of", "blockof")):
                            settle(dve.tensor_tensor(RT("picked"), RT(f"assign{j + 1}"), RT(value), ALU.mult))
                            settle(dve.reduce_sum(RT(of)[:, j, :], RT("picked"), AX))
                    for t in range(T):
                        for j in range(2):
                            dve.tensor_scalar(RT("places")[:, 2 * t + j, :], const("iota"), RT("places_of")[:, j, t:t + 1], None, ALU.is_equal)
                            last = dve.tensor_scalar(RT("blocks")[:, 2 * t + j, :], const("iota")[:, 0:TABLE], RT("blocks_of")[:, j, t:t + 1],
                                                     const("row_id")[:, 2 * t + j:2 * t + j + 1], ALU.is_equal, ALU.mult)
                    last.then_inc(one_hots, 1)
                    upto, past = RT("upto")[0:1, :], RT("past")[0:1]
                    settle(dve.tensor_tensor(past, upto.unsqueeze(1).to_broadcast([1, MAX_BLOCKS, EXPERTS]),
                                             const("iota")[0:1, 0:MAX_BLOCKS].unsqueeze(2).to_broadcast([1, MAX_BLOCKS, EXPERTS]), ALU.is_le))
                    settle(dve.reduce_sum(RT("expert")[0:1, :], past, AX))
                    settle(dve.tensor_scalar_min(RT("expert")[0:1, :], RT("expert")[0:1, :], float(EXPERTS - 1)))
                    dve.tensor_copy(CTRL[0:1, 1:1 + MAX_BLOCKS], RT("expert")[0:1, :])
                    settle(dve.tensor_copy(CTRL[0:1, 0:1], upto[:, EXPERTS - 1:EXPERTS]))
                    full_wait(dve, f0 + 2)
                    raw = bank(f0 + 2)[:, 0:TABLE]
                    settle(dve.tensor_scalar(RT("empty"), raw, 0.0, BIG, ALU.is_equal, ALU.mult))
                    drained(dve.scalar_tensor_tensor(RT("target"), raw, -1.0, RT("empty"), ALU.add, ALU.add), f0 + 2)
                    drained_wait(dve, f0 + 2)
                    settle(dve.tensor_scalar(RT("source"), RT("target"), S - 0.5, -float(S), ALU.is_gt, ALU.mult))
                    settle(dve.tensor_tensor(RT("source"), RT("source"), RT("target"), ALU.add))
                    dve.tensor_copy(TABI[:, 0, :], RT("source"))
                    dve.tensor_copy(TABI[:, 1, :], RT("target")).then_inc(blocks_ready, 1)

                if stage.kind == "experts":
                    s = blocks[layer]
                    gain, shift = COLS[:, 3, :], COLS[:, 2, :]

                    def last_chunks():
                        for k in range(KD // 2, KD):
                            last = dve.tensor_scalar(XGT[:, k, :], PS[:, k // 4, (k % 4) * P:(k % 4 + 1) * P], gain[:, k:k + 1], shift[:, k:k + 1], ALU.mult, ALU.add)
                        last.then_inc(s.last_scaled, 1)

                    dve.wait_ge(blocks_ready, layer + 1)
                    n_blocks = dve.value_load(CTRL[0:1, 0:1], min_val=1, max_val=MAX_BLOCKS)
                    dve.sem_inc(s.hidden, 1)
                    dve.sem_inc(s.y_right, 1)
                    dve.wait_ge(s.rows_turned, 1)
                    last_chunks()
                    with dve.Fori(0, n_blocks) as b:
                        dve.wait_ge(s.gate_exp, b + 1)
                        dve.tensor_scalar_add(GE, GE, 1.0).then_inc(s.silu_steps, 1)
                        dve.wait_ge(s.silu_steps, 3 * b + 1)
                        dve.reciprocal(GR, GE).then_inc(s.silu_steps, 1)
                        dve.wait_ge(s.silu_steps, 3 * b + 2)
                        dve.tensor_tensor(GR, GR, PS[:, 2, :], ALU.mult).then_inc(s.silu_steps, 1)
                        dve.wait_ge(s.silu_steps, 3 * b + 3)
                        dve.wait_ge(s.used[3], b + 2)
                        dve.tensor_tensor(HID, GR, PS[:, 3, :], ALU.mult).then_inc(s.hidden, 1)
                        dve.wait_ge(s.rows_turned, b + 2)
                        last_chunks()
                        dve.wait_ge(s.used[5], b + 2)
                        dve.wait_ge(s.y_free, b + 1)
                        dve.tensor_copy(YB[:, BANK:], PS[:, 6, :]).then_inc(s.y_right, 1)

                if stage.kind == "combine":
                    dve.wait_ge(rows_back, 16 * 2 * T * (layer + 1))
                    for t in range(T):
                        y1, y2 = Y2[:, 0, t, :], Y2[:, 1, t, :]
                        settle(dve.tensor_scalar(y1, y1, WTS[:, 0, t:t + 1], None, ALU.mult))
                        settle(dve.scalar_tensor_tensor(y1, y2, WTS[:, 1, t:t + 1], y1, ALU.mult, ALU.add))
                        settle(dve.tensor_tensor(y1, y1, GB[:, 1, :], ALU.mult))
                        dve.tensor_tensor(X[:, t, :], X[:, t, :], y1, ALU.add).then_inc(residual_written, 1)

                if stage.kind == "project":
                    for j, (at, width) in enumerate(IN_CHUNKS):
                        for t in range(1, T, 2):
                            n = f0 + T * j + t
                            full_wait(dve, n)
                            drained(dve.tensor_copy(PR[:, t, at:at + width], bank(n)[:, 0:width]), n)

                if stage.kind == "latent_up":
                    for n in range(f0 - BANKS, f0):
                        drained_wait(dve, n)
                    if stage.turn == 0:
                        pos, turns, wide = SIN_T[0], SIN_T[1], SIN_T[2]
                        settle(dve.tensor_copy(POSF[:, :], POSI[:, :]))
                        settle(dve.tensor_tensor(pos, POSF[:, :].unsqueeze(2).to_broadcast([P, T, ROPE // 2]),
                                                 const("inv_freq").unsqueeze(1).to_broadcast([P, T, ROPE // 2]), ALU.mult))
                        for dst, quarter in ((SIN, 0.0), (COS, 0.25)):
                            settle(dve.tensor_scalar(turns, pos, 1.0 / (2 * math.pi), quarter, ALU.mult, ALU.add))
                            settle(dve.tensor_scalar_add(turns, turns, ROUNDER))
                            settle(dve.tensor_scalar_add(turns, turns, -ROUNDER))
                            settle(dve.scalar_tensor_tensor(wide, turns, -TURN[0], pos, ALU.mult, ALU.add))
                            settle(dve.scalar_tensor_tensor(wide, turns, -TURN[1], wide, ALU.mult, ALU.add))
                            settle(dve.scalar_tensor_tensor(wide, turns, -TURN[2], wide, ALU.mult, ALU.add))
                            if quarter:
                                settle(dve.tensor_scalar_add(wide, wide, math.pi / 2))
                            settle(dve.tensor_scalar(dst[:, :, :], wide, PI_BELOW, -PI_BELOW, ALU.min, ALU.max))
                        dve.drain().then_inc(angles, 1)
                    dve.wait_ge(group_rstd, stage.grouped + 1)
                    for t in range(T):
                        for j, at in enumerate((C_CQ, C_CKV)):
                            last = dve.tensor_scalar(PR[:, t, at:at + RANK], PR[:, t, at:at + RANK], RSTD[:, j * T + t:j * T + t + 1], None, ALU.mult)
                        last.then_inc(group_normed, 1)
                    dve.wait_ge(mixer_in, 96 * (stage.turn + 1))
                    for j in range(4):
                        full_wait(dve, f0 + j)
                        drained(dve.tensor_scalar(HT[:, j, :], bank(f0 + j), RG[:, j // 2, j % 2:j % 2 + 1], None, ALU.mult), f0 + j)
                    for j in range(2 * T):
                        n = f0 + 4 + j
                        t, h = j // 2, 3 * (j % 2)
                        full_wait(dve, n)
                        drained(dve.tensor_copy(QM[:, t, h:h + 3, :], bank(n)[:, 0:3 * MQ].rearrange("p (h n) -> p h n", h=3)), n)
                    for n in range(f0 + 4, f0 + 4 + 4 * T):
                        if n >= f0 + 4 + 4 * T - BANKS or n < f0 + 4 + 2 * T:
                            drained_wait(dve, n)
                    dve.wait_ge(rope_ready, 1)
                    half = ROPE // 2

                    def rotate(dst1, dst2, x1, x2, cos, sin, tmp):
                        for out_ap, a, table in ((tmp[0], x1, cos), (tmp[1], x2, sin), (tmp[2], x2, cos), (tmp[3], x1, sin)):
                            last = dve.tensor_tensor(out_ap, a, table, ALU.mult)
                        settle(last)
                        settle(dve.tensor_tensor(dst1, tmp[0], tmp[1], ALU.subtract))
                        return dve.tensor_tensor(dst2, tmp[2], tmp[3], ALU.add)

                    gb = GB.rearrange("p a n -> p (a n)")
                    for t in range(T):
                        cos = COS[:, t, :].unsqueeze(1).to_broadcast([P, MH, half])
                        sin = SIN[:, t, :].unsqueeze(1).to_broadcast([P, MH, half])
                        q1, q2 = QM[:, t, :, NOPE:NOPE + half], QM[:, t, :, NOPE + half:]
                        tmp = [gb[:, m * 96:(m + 1) * 96].rearrange("p (h n) -> p h n", h=MH) for m in range(4)]
                        settle(rotate(q1, q2, q1, q2, cos, sin, tmp))
                    dve.drain().then_inc(mixer_up, 1)
                    k1, k2 = PR[:, :, C_KR:C_KR + half], PR[:, :, C_KR + half:C_KR + ROPE]
                    tmp = [gb[:, m * 64:(m + 1) * 64].rearrange("p (t n) -> p t n", t=T) for m in range(4)]
                    settle(rotate(k1, k2, k1, k2, COS[:, :, :], SIN[:, :, :], tmp))
                    dve.tensor_copy(KM[:, :, :, NOPE:], PR[:, :, C_KR:C_KR + ROPE].unsqueeze(2).to_broadcast([P, T, MH, ROPE])).then_inc(mixer_up, 1)

                if stage.kind == "xq":
                    for h in range(XH):
                        full_wait(dve, f0 + h)
                        drained(dve.tensor_copy(XQT[:, h, :], bank(f0 + h)), f0 + h)
                if stage.kind == "xkv":
                    for h in range(XH):
                        full_wait(dve, f0 + h)
                        drained(dve.tensor_copy(XKT[:, h, :], bank(f0 + h)[:, 0:MEM]), f0 + h)
                    for t in range(MT):
                        n = f0 + XH + t
                        full_wait(dve, n)
                        drained(dve.tensor_copy(XV[:, t, :], bank(n)), n)

                if stage.kind in ("latent", "xattn"):
                    order, heads, scale, span, dv, o_at = soft_plan(stage)
                    made = {what_s: n for n, what_s in enumerate(order, f0)}
                    steps = heads * T
                    for r in range(steps + AHEAD + 1):
                        if r < steps:
                            L, n = span(r % T), made["scores", r]
                            if stage.kind == "latent" and r % T == 0:
                                h = r // T
                                nk = made["turn_k", r]
                                full_wait(dve, nk)
                                if h >= 2:
                                    full_wait(dve, made["scores", r - T - 1])
                                drained(dve.tensor_copy(LKT(h)[0:MQ, :], bank(nk)[0:MQ, :]), nk)
                            full_wait(dve, n)
                            if r >= 4:
                                drained_wait(dve, made["scores", r - 4])
                            settle(dve.tensor_reduce(RCP[:, r % 4, 0:1], bank(n)[:, 0:L], AX, ALU.max, negate=True))
                            dve.tensor_scalar(MX[:, r % 4, 0:1], RCP[:, r % 4, 0:1], scale, None, ALU.mult).then_inc(negmax_ready, 1)
                        s = r - AHEAD - 1
                        if s >= 0:
                            h, i = divmod(s, T)
                            n = made["values", s]
                            full_wait(dve, n)
                            settle(dve.reciprocal(RCP[:, s % 4, 1:2], SUM[:, s % 4, 0:1]))
                            drained(dve.tensor_scalar(XN[:, i, o_at + h * dv:o_at + (h + 1) * dv], bank(n)[:, 0:dv], RCP[:, s % 4, 1:2], None, ALU.mult), n)

                if stage.kind == "gla":
                    f_z, f_b, f_last = f0 + 1, f0 + 3, f0 + 5
                    for j in range(2):
                        n = f_z + j
                        full_wait(dve, n)
                        z = bank(n)[:, 0:2 * GQK].rearrange("p (t n) -> p t n", t=2)
                        dve.tensor_scalar(SOFT[:, 2 * j:2 * j + 2, :], z, -1.0, 30.0, ALU.mult, ALU.min).then_inc(soft_in, 1)
                    dve.wait_ge(soft_log, stage.turn + 1)
                    for j in range(2):
                        n = f_z + j
                        z = bank(n)[:, 0:2 * GQK].rearrange("p (t n) -> p t n", t=2)
                        soft = SOFT[:, 2 * j:2 * j + 2, :]
                        drained(dve.scalar_tensor_tensor(soft, z, -1.0, soft, ALU.mult, ALU.max), n)
                        drained_wait(dve, n)
                        dve.drain().then_inc(soft_ready, 1)
                    for j in range(2):
                        n = f_last + j
                        full_wait(dve, n)
                        drained_wait(dve, f_b + j)
                        ke = KE[:, 2 * j:2 * j + 2, :]
                        drained(dve.tensor_tensor(ke, bank(n)[:, 0:2 * GQK].rearrange("p (t n) -> p t n", t=2), ke, ALU.subtract), n)
                    drained_wait(dve, f_last)
                    drained_wait(dve, f_last + 1)
                    dve.drain().then_inc(decayed, 1)
                    dve.scalar_tensor_tensor(QD, PR[:, :, C_GQ:C_GQ + GQK], GDK ** -0.5, QD, ALU.mult, ALU.mult)
                    dve.tensor_tensor(KI, PR[:, :, C_GK:C_GK + GQK], KI, ALU.mult).then_inc(decayed, 1)
                    dve.wait_ge(decays_ready, stage.turn + 1)
                    dve.tensor_tensor(KE, PR[:, :, C_GK:C_GK + GQK], KE, ALU.mult).then_inc(decayed, 1)
                    for h in range(GH):
                        n = f0 + 9 + 2 * h
                        full_wait(dve, n)
                        drained(dve.tensor_copy(GKT[0:GDK, h, :], bank(n)[0:GDK, :]), n)
                    dve.wait_ge(gla_clear, 2 * (stage.turn + 1))
                    drained_wait(dve, f0 + 7)
                    for h in range(GH):
                        if h >= 2:
                            full_wait(dve, gla_fill(stage, "outputs", h - 2))
                        st = GST(h)
                        settle(dve.memset(st[0:GDK, 0, :], 0.0))
                        for j in range(7):
                            n = gla_fill(stage, "update", h, j % 2)
                            if j < 2:
                                full_wait(dve, n)
                            step = dve.scalar_tensor_tensor(st[0:GDK, j + 1, :], st[0:GDK, j, :], DEC[0:GDK, h * 8 + j:h * 8 + j + 1],
                                                            bank(n)[0:GDK, (j // 2) * GDV:(j // 2 + 1) * GDV], ALU.mult, ALU.add)
                            if j in (5, 6):
                                drained(step, n)
                                drained_wait(dve, n)
                            else:
                                settle(step)
                        dve.drain().then_inc(state_ready, 1)
                        n = gla_fill(stage, "scores", h)
                        full_wait(dve, n)
                        drained(dve.copy_predicated(GAT(h), const("gla_mask").bitcast(I32).unsqueeze(1).to_broadcast([P, T, P]),
                                                    bank(n).rearrange("p (t n) -> p t n", t=T)), n)
                    dve.wait_ge(squares_ready, squares_before(stage) + 1)
                    dve.reduce_sum(SUMSQ[:, 0:T * GH], SCR[:, 0:T * GV].rearrange("p (g n) -> p g n", n=GDV), AX).then_inc(group_sums, 1)
                    dve.wait_ge(group_rstd, stage.grouped + 1)
                    for t in range(T):
                        o = XN[:, t, 0:GV].rearrange("p (h n) -> p h n", h=GH)
                        settle(dve.tensor_tensor(o, o, RSTD[:, t * GH:(t + 1) * GH].unsqueeze(2).to_broadcast([P, GH, GDV]), ALU.mult))
                        settle(dve.tensor_tensor(o, o, GN[:, :].unsqueeze(1).to_broadcast([P, GH, GDV]), ALU.mult))
                    g = gated(0, stage)
                    dve.tensor_tensor(XN[:, :, 0:GV], XN[:, :, 0:GV], g, ALU.mult).then_inc(mixed, 1)

                if stage.kind == "conv":
                    settle(dve.tensor_tensor(CU2, PR[:, :, C_CC:C_CC + CW], PR[:, :, C_CH:C_CH + CW], ALU.mult))
                    for dst, j in ((CU1, 1), (CU0, 0)):
                        last = dve.tensor_tensor(dst, CU2, CWT[:, j, :].unsqueeze(1).to_broadcast([P, T, CW]), ALU.mult)
                    last.then_inc(conv_in, 1)
                    settle(dve.tensor_tensor(CU2, CU2, CWT[:, 2, :].unsqueeze(1).to_broadcast([P, T, CW]), ALU.mult))
                    for j in range(2):
                        n = f0 + j
                        full_wait(dve, n)
                        drained(dve.tensor_tensor(CU2[:, 2 * j:2 * j + 2, :], CU2[:, 2 * j:2 * j + 2, :], bank(n).rearrange("p (t n) -> p t n", t=2), ALU.add), n)
                        drained_wait(dve, n)
                    settle(dve.tensor_tensor(CU2, CU2, PR[:, :, C_CB:C_CB + CW], ALU.mult))
                    g = gated(1, stage)
                    dve.tensor_tensor(XN[:, :, GV:GV + CW], CU2, g, ALU.mult).then_inc(mixed, 1)
                    g = gated(2, stage)
                    dve.tensor_tensor(XN[:, :, GV + CW:], XN[:, :, GV + CW:], g, ALU.mult).then_inc(mixed, 1)


_INPUTS = ["x", "c", "norm1_g", "norm2_g", "ada_w", "ada_b", "diff_w_in", "diff_w_out", "diff_lambda_q1", "diff_lambda_k1",
           "diff_lambda_q2", "diff_lambda_k2", "diff_subln_g", "sb_w_in", "sb_w_out", "router_group_w", "router_group_b",
           "router_expert_w", "router_expert_b", "expert_w_gate", "expert_w_up", "expert_w_down", "final_norm_g", "mem_2",
           "positions_2", "norm_mix_2", "w_in_2", "gla_w_gate_2", "gla_b_gate_2", "gla_norm_2", "conv_w_2", "mla_q_norm_2",
           "mla_w_uq_2", "mla_kv_norm_2", "mla_w_ukv_2", "w_out_2", "norm_xattn_2", "norm_mem_2", "mem_wq_2", "mem_wk_2",
           "mem_wv_2", "mem_wo_2", "norm_final_2"]


def kernel(**inputs):
    import concourse.bacc as bacc
    from concourse.bass_utils import run_bass_kernel_spmd

    nc = bacc.Bacc("TRN2", target_bir_lowering=False, num_devices=1)
    arrays, args = {}, {}
    given = {name: np.ascontiguousarray(inputs[name]) for name in _INPUTS}
    given["tables"] = shape_constants()[0]
    for name, a in given.items():
        arrays[f"in_{name}"] = a
        args[name] = nc.dram_tensor(f"in_{name}", a.shape, mybir.dt.from_np(a.dtype), kind="ExternalInput").ap()
    out = nc.dram_tensor("out_0", (1, S, D), F32, kind="ExternalOutput").ap()
    build_program(nc, None, out=out, **args)
    result = run_bass_kernel_spmd(nc, [arrays], core_ids=[0])
    return result.results[0]["out_0"]
```

```python
import math
from contextlib import ExitStack

import numpy as np

import concourse.bass as bass
from concourse import mybir

F32 = mybir.dt.float32
F32R = mybir.dt.float32r
I32 = mybir.dt.int32
ALU = mybir.AluOpType
ACT = mybir.ActivationFunctionType
AX = mybir.AxisListType.X

P = 128
D = 1024
S = 512
T = S // P
KD = D // P
DEPTH = 2
BANK = 512
BANKS = 8
SLOTS = 4
SLOT = 4096
NEG = -1e30
BIG = float(1 << 20)

DIFF_HEADS = 8
DIFF_LAMBDA_INIT = 0.8 - 0.6 * math.exp(0.0)
SB_HEADS = 16
HD = 64

GROUPS = 4
PER_GROUP = 8
EXPERTS = GROUPS * PER_GROUP
HIDDEN = 512
KH = HIDDEN // P
MAX_BLOCKS = (2 * S + EXPERTS * P) // P
MIN_BLOCKS = 2 * S // P
TABLE = MAX_BLOCKS + 2

MEM = 256
MT = MEM // P
GH, GDK, GDV, CHUNK = 4, 48, 96, 64
GQK, GV = GH * GDK, GH * GDV
CW = 256
MH, NOPE, ROPE, MV = 6, 64, 32, 64
MQ = NOPE + ROPE
RANK = 256
XH, XD = 4, 128
IN_SPLITS = (GQK, GQK, GV, 16, GV, CW, CW, CW, CW, RANK, RANK, ROPE, MH * MV)
IN_WIDTH = sum(IN_SPLITS)
IN_AT = [sum(IN_SPLITS[:n]) for n in range(len(IN_SPLITS))]
(C_GQ, C_GK, C_GV, C_GLR, C_GGATE, C_CC, C_CB, C_CH, C_CGATE, C_CQ, C_CKV, C_KR, C_MGATE) = IN_AT
IN_CHUNKS = [(n, min(BANK, IN_WIDTH - n)) for n in range(0, IN_WIDTH, BANK)]


UNITS = {("qkv", 0): 3 * D // BANK, ("qkv", 1): 3 * D // BANK, ("attn_out", 0): D // BANK,
         ("project", 0): len(IN_CHUNKS), ("project", 1): len(IN_CHUNKS), ("mix_out", 0): D // BANK, ("mix_out", 1): D // BANK}


def shape_constants():
    p = np.arange(P)[:, None]
    c = np.arange(P)[None, :]
    same = (p // CHUNK) == (c // CHUNK)
    u = np.arange(S)[None, :] - (S - P)
    parts = {
        "ident": (p == c),
        "alibi": np.where(np.floor_divide(u, CHUNK) <= p // CHUNK, -np.abs(p - u), NEG),
        "before": (p < c),
        "neg_ge": -1.0 * (p >= c),
        "ones": np.ones((P, P)),
        "neg_ones": -np.ones((P, P)),
        "gla_cum": -1.0 / 16 * (same & (p <= c)),
        "gla_last": -1.0 / 16 * same,
        "gla_chunk": -1.0 / 16 * ((p // CHUNK) == np.arange(2)[None, :]),
        "shift1": (c == p + 1),
        "shift2": (c == p + 2),
        "carry1": (p == P - 1) & (c == 0),
        "carry2": (c == p + 2 - P),
        "gla_mask": (same & (p <= c)),
        "causal": np.where(c <= p, 0.0, NEG),
        "iota": np.broadcast_to(c, (P, P)),
        "rev": np.broadcast_to(8.0 - np.arange(8)[None, :], (P, 8)),
        "row_id": (np.arange(T)[None, :, None] * P + np.arange(P)[:, None, None]
                   + S * np.arange(2)[None, None, :] + 1).reshape(P, 2 * T),
        "inv_freq": np.broadcast_to((1.0 / (np.float32(10000.0) ** (np.arange(0, ROPE, 2, dtype=np.float32) / np.float32(ROPE)))).astype(np.float32)[None, :], (P, ROPE // 2)),
        "minus_half": np.full((P, 32), -0.5),
    }
    at, n = {}, 0
    for name, a in parts.items():
        at[name] = (n, a.shape[1])
        n += a.shape[1]
    table = np.concatenate([np.asarray(a, np.float32) for a in parts.values()], axis=1)
    return np.ascontiguousarray(table), at


class Stage:

    def __init__(self, kind, arg, fill, load, turn, residual, scaled, grouped, tiles_before, updates):
        self.kind, self.arg, self.fill, self.load, self.turn, self.residual = kind, arg, fill, load, turn, residual
        self.scaled, self.grouped, self.tiles_before = scaled, grouped, tiles_before
        self.updates = updates


def attention_steps(heads, ahead, per_head):
    steps = heads * T
    order = [(what, 0) for what in per_head]
    for s in range(steps + ahead + 1):
        if s < steps:
            order.append(("scores", s))
            if (s + 1) % T == 0 and s + 1 < steps:
                order += [(what, s + 1) for what in per_head]
        if 0 <= s - ahead < steps:
            order.append(("turned", s - ahead))
        if s > ahead:
            order.append(("values", s - ahead - 1))
    return order


def diff_order():
    order = []
    for what, s in attention_steps(DIFF_HEADS, AHEAD, ()):
        if what == "turned" and s < 2 * MOD_CHUNKS:
            order += [("mod_rest" if s % 2 else "mod", s // 2)]
        order += [("map0", s), ("map1", s)] if what == "scores" else [(what, s)]
    return order


def diff_fills():
    numbered = [what_s for what_s in diff_order() if what_s[0] != "mod_rest"]
    return {what_s: n for n, what_s in enumerate(numbered)}


def gla_fill(stage, what, h, part=0):
    first = stage.fill + 16
    if what == "update":
        return first + 4 * h + part - (h > 0)
    if what == "scores":
        return first + 4 * h + 2 - (h > 0)
    return first + 4 * h + 6 - 3 * (h == GH - 1)


ROUNDER = 1.5 * 2.0 ** 23
_T0 = 6.28125
_T1 = float(np.float32(np.floor((2 * math.pi - _T0) * 2 ** 20) / 2 ** 20))
TURN = (_T0, _T1, 2 * math.pi - _T0 - _T1)
PI_BELOW = 3.1415925
AHEAD = 2
MOD_CHUNKS = 6 * D // BANK
N_FIRST = 3
N_LATE = 3 + 4 + 10


def plan_stages():
    kinds = []
    for layer in range(DEPTH):
        kinds += [("mod", layer), ("norm", ("first1", layer)), ("qkv", layer),
                  ("diff" if layer == 0 else "stick", layer)]
        if layer == 0:
            kinds += [("otrans", 0)]
        kinds += [("attn_out", layer), ("norm", ("first2", layer)), ("route", layer), ("experts", layer),
                  ("combine", layer)]
    kinds += [("final", 0)]
    for layer in range(DEPTH):
        kinds += [("norm", ("mix", layer)), ("project", layer), ("latent_up", layer), ("latent", layer),
                  ("gla", layer), ("conv", layer), ("mtrans", layer), ("mix_out", layer),
                  ("norm", ("xattn", layer)), ("xq", layer), ("norm", ("mem", layer)), ("xkv", layer),
                  ("xattn", layer), ("xtrans", layer), ("x_out", layer)]
    kinds += [("final", 1)]
    fills = {
        "mod": 13, "norm": KD, "qkv": 24, "diff": len(diff_fills()), "stick": 0, "otrans": KD,
        "attn_out": 8, "route": 3, "experts": 0, "combine": 0, "final": 0,
        "project": len(IN_CHUNKS) * T, "latent_up": 4 + 4 * T, "latent": MH * (2 + 3 * T),
        "gla": 8 + GH * 6, "conv": 2, "mtrans": KD, "mix_out": 8,
        "xq": XH, "xkv": XH + MT, "xattn": 3 * XH * T, "xtrans": XH, "x_out": 8,
    }
    readers = {
        "mod": list(range(MOD_CHUNKS)), "diff": [diff_fills()["mod", j] for j in range(MOD_CHUNKS)], "attn_out": [6, 7],
        "qkv": [T * j + T - 1 for j in range(3 * D // BANK)],
        "project": [T * j + T - 1 for j in range(len(IN_CHUNKS))], "latent_up": [3 + 2 * T, 3 + 4 * T],
        "mix_out": [6, 7], "xq": [XH - 1], "xkv": [XH - 1, XH + MT - 1], "x_out": [7],
    }
    plan, last_reader, fill, seen, residual, updates, scaled, grouped, tiles = [], [], 0, {}, None, 0, 0, 0, 0
    for kind, arg in kinds:
        plan.append(Stage(kind, arg, fill, len(last_reader), seen.get(kind, 0), residual,
                          scaled, grouped, tiles, updates))
        plan[-1].units = UNITS.get((kind, arg), 0)
        plan[-1].units_before = sum(stage.units for stage in plan[:-1])
        plan[-1].splits_before = KD * sum(stage.units > 0 for stage in plan[:-1])
        scaled += kind in ("norm", "final")
        grouped += kind in ("otrans", "latent_up", "gla")
        if kind == "norm":
            tiles += MT if arg[0] == "mem" else T
        seen[kind] = seen.get(kind, 0) + 1
        if (kind, arg) == ("mod", 1):
            continue
        for r in readers.get(kind, []):
            last_reader += [fill + r] * (2 if (kind, arg) in UNITS else 1)
        if kind in ("attn_out", "mix_out", "x_out"):
            residual = ("fills", fill)
        if kind in ("combine", "final"):
            updates += T
            residual = ("updates", updates)
        fill += fills[kind]
    return plan, last_reader


def build_program(nc, x, c, norm1_g, norm2_g, ada_w, ada_b, diff_w_in, diff_w_out,
                  diff_lambda_q1, diff_lambda_k1, diff_lambda_q2, diff_lambda_k2, diff_subln_g,
                  sb_w_in, sb_w_out, router_group_w, router_group_b, router_expert_w, router_expert_b,
                  expert_w_gate, expert_w_up, expert_w_down, final_norm_g, mem_2, positions_2,
                  norm_mix_2, w_in_2, gla_w_gate_2, gla_b_gate_2, gla_norm_2, conv_w_2, mla_q_norm_2,
                  mla_w_uq_2, mla_kv_norm_2, mla_w_ukv_2, w_out_2, norm_xattn_2, norm_mem_2,
                  mem_wq_2, mem_wk_2, mem_wv_2, mem_wo_2, norm_final_2, tables, out):
    _, table_at = shape_constants()
    TABLE_WIDTH = tables.shape[1]
    plan, last_reader = plan_stages()
    ctx = ExitStack()
    with ctx:
        def sbuf(name, shape, dtype=F32):
            return ctx.enter_context(nc.sbuf_tensor(name, shape, dtype))

        def semaphore(name):
            return ctx.enter_context(nc.semaphore(name))

        def twofold(name, shape):
            with nc.sbuf_tensor(name + "_rounded", [P, math.prod(shape[1:])], F32R) as rounded:
                pass
            return sbuf(name, shape), rounded

        XN, XN_R = twofold("normed_by_token", [P, T, D])
        HT, HT_R = twofold("normed_by_feature", [P, KD, S])
        BIGA, BIGA_R = twofold("projections", [P, T * 3136])
        RING, RING_R = twofold("weight_ring", [P, SLOTS, SLOT])
        X = sbuf("residual", [P, T, D])
        GB = sbuf("gates", [P, 2, D])
        SCR, SCR_R = twofold("scratch", [P, 6144])
        CON = sbuf("constants", [P, TABLE_WIDTH])
        COLS = sbuf("columns", [P, 4, KD])
        GCOL = sbuf("gain_columns", [P, 10, KD])
        PS = ctx.enter_context(nc.psum_tensor("banks", [P, BANKS, BANK], F32))

        QT = BIGA[:, 0:4096].rearrange("p (c s) -> p c s", c=8)
        KT = BIGA[:, 4096:8192].rearrange("p (c s) -> p c s", c=8)
        V = BIGA[:, 8192:12288].rearrange("p (t n) -> p t n", t=T)
        PR = BIGA[:, 0:T * IN_WIDTH].rearrange("p (t n) -> p t n", t=T)

        def const(name):
            a, n = table_at[name]
            return CON[:, a:a + n]

        ident = const("ident")
        ones = const("ones")

        SUMSQ = sbuf("sum_of_squares", [P, 32])
        RSTD = sbuf("reciprocal_rms", [P, 32])
        MX = sbuf("row_max", [P, 4, 2])
        SUM = sbuf("row_sum", [P, 4, 2])
        RCP = sbuf("row_reciprocal", [P, 4, 2])
        LAMV = sbuf("lambda_vectors", [P, 4, HD])
        LAM = sbuf("lambda", [P, 8])
        SUBG = sbuf("subln_gain", [P, 2])
        MODC = sbuf("modulation_columns", [P, 4, KD])
        CCOL = sbuf("condition", [P, 4, KD])

        RW = sbuf("router_weights", [P, KD, GROUPS + EXPERTS])
        RB = sbuf("router_bias", [P, GROUPS + EXPERTS])
        WTS = sbuf("expert_weights", [P, 2, T])
        TABI = sbuf("slot_table", [P, 2, TABLE], I32)
        CTRL = sbuf("block_experts", [1, MAX_BLOCKS + 8], I32)
        ROWS_IN = sbuf("block_rows_in", [P, 1], I32)
        TICK = sbuf("carrier", [P, 1], I32)
        ROWS_OUT = sbuf("block_rows_out", [P, 1], I32)

        COS = sbuf("rope_cos", [P, T, ROPE // 2])
        SIN = sbuf("rope_sin", [P, T, ROPE // 2])
        POSI = sbuf("positions", [P, T], I32)
        POSF = sbuf("positions_float", [P, T])
        ANGLE = sbuf("rope_steps", [P, 3, T, ROPE // 2])
        SIN_T = [ANGLE[:, n] for n in range(3)]
        GW = LAMV[0:32].rearrange("p a n -> p (a n)")[:, 0:GQK]
        GN = RW[:, :, :].rearrange("p k n -> p (k n)")[:, 0:GDV]
        at = table_at["alibi"][0]
        CWT = CON[:, at:at + 3 * CW].rearrange("p (j n) -> p j n", j=3)
        RG = sbuf("rank_gains", [P, 2, 2])

        xn_d = nc.dram_tensor("xn_rows", [S, D], F32, kind="Internal").ap()
        mod_d = nc.dram_tensor("second_modulation", [1, 6 * D], F32, kind="Internal").ap()
        y_d = nc.dram_tensor("y_rows", [2 * S, D], F32, kind="Internal").ap()

        bank_full = [semaphore(f"bank_full{n}") for n in range(BANKS)]
        bank_drained = [semaphore(f"bank_drained{n}") for n in range(BANKS)]
        slot_loaded = [semaphore(f"slot_loaded{n}") for n in range(SLOTS)]
        inputs_in = semaphore("inputs_in")
        dve_done = semaphore("dve_done")
        act_done = semaphore("act_done")
        pool_done = semaphore("pool_done")

        def full_wait(eng, n):
            eng.wait_ge(bank_full[n % BANKS], n // BANKS + 1)

        def drained_wait(eng, n):
            eng.wait_ge(bank_drained[n % BANKS], n // BANKS + 1)

        def free_wait(eng, n):
            if n >= BANKS:
                eng.wait_ge(bank_drained[n % BANKS], n // BANKS)

        def loaded_wait(eng, u):
            eng.wait_ge(slot_loaded[u % SLOTS], 16 * (u // SLOTS + 1))

        def bank(n):
            return PS[:, n % BANKS, :]

        def slot(u, width, k=KD):
            return RING[:, u % SLOTS, 0:k * width].rearrange("p (k n) -> p k n", k=k)

        def residual_wait(eng, stage, t=None):
            if stage.residual is None:
                return
            how, n = stage.residual
            tiles = range(T) if t is None else [t]
            if how == "updates":
                eng.wait_ge(residual_written, n - T + 1 + tiles[-1])
            else:
                for tile in tiles:
                    drained_wait(eng, n + 2 * tile)
                    drained_wait(eng, n + 2 * tile + 1)


        residual_written = semaphore("residual_written")
        act_prepared = semaphore("act_prepared")
        dve_prepared = semaphore("dve_prepared")
        sumsq_ready = semaphore("sumsq_ready")
        rstd_ready = semaphore("rstd_ready")
        xn_ready = semaphore("xn_ready")
        chunk_high = semaphore("chunk_high")
        chunk_low = semaphore("chunk_low")
        unit_low = semaphore("unit_low")
        bias_row_in = [semaphore(f"bias_row_in{n}") for n in range(2)]
        mod_stored = [semaphore(f"mod_stored{n}") for n in range(2)]
        mod_columns_in = semaphore("mod_columns_in")
        mod_gates_in = semaphore("mod_gates_in")
        squares_ready = semaphore("squares_ready")
        group_sums = semaphore("group_sums")
        group_rstd = semaphore("group_rstd")
        group_normed = semaphore("group_normed")
        negmax_ready = semaphore("negmax_ready")
        diff_exp = semaphore("diff_exp")
        diff_ready = semaphore("diff_ready")
        z_full = semaphore("z_full")
        z_clamped = semaphore("z_clamped")
        z_log = semaphore("z_log")
        sp_raw = semaphore("sp_raw")
        sp_ready = semaphore("sp_ready")
        r_full = semaphore("r_full")
        a_raw = semaphore("a_raw")
        a_ready = semaphore("a_ready")
        o_full = semaphore("o_full")
        o_drained = semaphore("o_drained")
        router_in = semaphore("router_in")
        group_shift = semaphore("group_shift")
        group_exp = semaphore("group_exp")
        pair_diff = semaphore("pair_diff")
        pair_exp = semaphore("pair_exp")
        assigned = semaphore("assigned")
        one_hots = semaphore("one_hots")
        blocks_ready = semaphore("blocks_ready")
        xn_stored = semaphore("xn_stored")
        experts_over = semaphore("experts_over")
        rows_back = [semaphore(f"rows_back{t}") for t in range(T)]
        weighted = semaphore("weighted")
        gain_in = semaphore("gain_in")
        mixer_in = semaphore("mixer_in")
        mixer_up = semaphore("mixer_up")
        soft_in = semaphore("soft_in")
        soft_log = semaphore("soft_log")
        soft_ready = semaphore("soft_ready")
        decays_ready = semaphore("decays_ready")
        decayed = semaphore("decayed")
        pool_cleared = semaphore("pool_cleared")
        state_ready = semaphore("state_ready")
        gate_exp = semaphore("gate_exp")
        gate_reciprocal = semaphore("gate_reciprocal")
        conv_in = semaphore("conv_in")
        mixed = semaphore("mixed")
        angles = semaphore("angles")
        rope_ready = semaphore("rope_ready")
        late_inputs_in = semaphore("late_inputs_in")
        stored = semaphore("stored")

        class Blocks:

            def __init__(self, layer):
                def s(name):
                    return semaphore(f"{name}_{layer}")

                self.loaded = [s(f"part_loaded{n}") for n in range(6)]
                self.used = [s(f"part_used{n}") for n in range(6)]
                self.high_ready = s("high_ready")
                self.low_ready = s("low_ready")
                self.late_low_ready = s("late_low_ready")
                self.gathered = s("gathered")
                self.in_listed = s("in_listed")
                self.out_listed = s("out_listed")
                self.carried = s("carried")
                self.scattered = s("scattered")
                self.y_free = s("y_free")
                self.rows_turned = s("rows_turned")
                self.first_scaled = s("first_scaled")
                self.last_scaled = s("last_scaled")
                self.rows_high = s("rows_high")
                self.rows_low = s("rows_low")
                self.gate_exp = s("block_gate_exp")
                self.silu_steps = s("silu_steps")
                self.hidden = s("hidden")
                self.hidden_turned = s("hidden_turned")
                self.hidden_high = s("hidden_high")
                self.hidden_low = s("hidden_low")
                self.y_left = s("y_left")
                self.y_right = s("y_right")

        blocks = [Blocks(layer) for layer in range(DEPTH)]

        XG = BIGA[:, 0:1024]
        XGT = BIGA[:, 1024:2048].rearrange("p (k n) -> p k n", k=KD)
        XGT_HIGH, XGT_LOW = (BIGA_R[:, n:n + 1024].rearrange("p (k n) -> p k n", k=KD) for n in (5120, 6144))
        HID = BIGA[:, 2048:2560]
        HIDT_HIGH, HIDT_LOW = (BIGA_R[:, n:n + 512] for n in (7168, 7680))
        YB = BIGA[:, 3072:4096]
        GE = BIGA[:, 4096:4608]
        GR = BIGA[:, 4608:5120]
        Y2 = BIGA[:, 0:8192].rearrange("p (j t n) -> p j t n", j=2, t=T)
        W_GATE = RING[:, 0, :].rearrange("p (k n) -> p k n", k=KD)
        W_UP = RING[:, 1, :].rearrange("p (k n) -> p k n", k=KD)
        W_DOWN = RING[:, 2, :].rearrange("p (h k n) -> p h k n", h=2, k=KH)
        PART = SLOT // 2
        PARTS = 6
        LOADED = [RING[:, n // 2, PART * (n % 2):PART * (n % 2 + 1)] for n in range(PARTS)]
        LOW = [RING_R[:, PART * n:PART * (n + 1)] for n in range(PARTS)]
        HIGH = [(RING_R[:, 3 * SLOT:], HT_R, XN_R)[n // 2][:, PART * (n % 2):PART * (n % 2 + 1)] for n in range(PARTS)]
        MODROW = HT[0:1, :, :].rearrange("p (q a) n -> p q (a n)", a=2)
        ADAB = BIGA[0:1, 6144:12288]
        MOD_ROW = [SCR[0:1, 4096 + BANK * n:4096 + BANK * (n + 1)] for n in range(2)]
        BIAS_ROW = [SCR[0:1, 5120 + BANK * n:5120 + BANK * (n + 1)] for n in range(2)]
        CB = BIGA[:, 0:1024].rearrange("p (k n) -> p k n", k=KD)
        MEMT = BIGA[:, 4096:6144].rearrange("p (t n) -> p t n", t=MT)
        QM = SCR[:, 0:2304].rearrange("p (t h n) -> p t h n", t=T, h=MH)
        KM = SCR[:, 2304:4608].rearrange("p (t h n) -> p t h n", t=T, h=MH)
        VM = SCR[:, 4608:6144].rearrange("p (t h n) -> p t h n", t=T, h=MH)
        XQT = BIGA[:, 0:2048].rearrange("p (h s) -> p h s", h=XH)
        XKT = BIGA[:, 2048:3072].rearrange("p (h s) -> p h s", h=XH)
        XV = BIGA[:, 3072:4096].rearrange("p (t n) -> p t n", t=MT)

        def SA(s):
            return SCR[:, 1024 * (s % 3):1024 * (s % 3 + 1)].rearrange("p (m n) -> p m n", m=2)

        def AT(s):
            return SCR[:, 3072 + BANK * (s % 2):3072 + BANK * (s % 2 + 1)]

        def SP1(stage, s):
            return GB.rearrange("p a n -> p (a n)")[:, BANK * (s % 3):BANK * (s % 3 + 1)]

        def AT1(stage, s):
            return HT[:, s % 2, :] if stage.kind == "latent" else SCR[:, BANK * (s % 2):BANK * (s % 2 + 1)]

        def LQT(h):
            return HT[:, 4 + h % 2, :]

        def LKT(h):
            return HT[:, 6 + h % 2, :]

        SOFT = SCR[:, 0:768].rearrange("p (t n) -> p t n", t=T)
        QD = SCR[:, 768:1536].rearrange("p (t n) -> p t n", t=T)
        KI = SCR[:, 1536:2304].rearrange("p (t n) -> p t n", t=T)
        KE = SCR[:, 2304:3072].rearrange("p (t n) -> p t n", t=T)
        GLA_SQUARES = SCR[:, 1536:1536 + T * GV]
        GLT = SCR[:, 3072:3584]
        DEC = SCR[:, 3584:3616]
        GQT = HT[:, 0:4, :]
        GKT = HT[:, 4:8, :]
        CU2 = XN[:, :, GV:GV + CW]
        CU1 = SCR[:, 4640:4640 + T * CW].rearrange("p (t n) -> p t n", t=T)
        CU0 = SCR[:, 0:T * CW].rearrange("p (t n) -> p t n", t=T)

        def GAT(h):
            return SCR[:, 3616 + BANK * (h % 2):3616 + BANK * (h % 2 + 1)].rearrange("p (t n) -> p t n", t=T)

        def GST(h):
            return GB.rearrange("p a n -> p (a n)")[:, 768 * (h % 2):768 * (h % 2 + 1)].rearrange("p (j n) -> p j n", j=8)

        GATES = ((C_GGATE, GV), (C_CGATE, CW), (C_MGATE, MH * MV))
        PIECES = len(GATES) * T * 2

        def gate_piece(n):
            j, t, half = n // (2 * T), n // 2 % T, n % 2
            at, width = GATES[j]
            width //= 2
            first = (GV if j == 1 else 0) + half * width
            return j, t, slice(half * width, (half + 1) * width), PR[:, t, at + half * width:at + (half + 1) * width], XN[:, t, first:first + width]

        def normed_after(stage):
            return T if stage.kind == "otrans" else T * (2 + stage.turn)

        def squares_before(stage):
            return T + 2 * stage.turn + (stage.kind == "gla")

        def soft_base(stage):
            return DIFF_HEADS * T + stage.turn * (MH + XH) * T + (MH * T if stage.kind == "xattn" else 0)

        ROUTE = {}
        at = 0
        for name, dims in (("logits", (T, 36)), ("gmax", (T,)), ("gshift", (T, 4)), ("gexp", (T, 4)), ("gsum", (T,)),
                           ("gweight", (T,)), ("gfirst", (T, 4)), ("gtop", (T,)), ("group", (T, 4)),
                           ("masked", (T, 4, 8)), ("elogits", (T, 8)), ("top1", (T,)), ("first1", (T, 8)), ("mark1", (T,)),
                           ("hot1", (T, 8)), ("rest", (T, 8)), ("top2", (T,)), ("first2", (T, 8)), ("mark2", (T,)),
                           ("hot2", (T, 8)), ("gap", (T,)), ("gapexp", (T,)), ("total", (T,)), ("share", (T,)),
                           ("assign1", (T, 32)), ("assign2", (T, 32)), ("assigned", (T, 32)), ("rank", (T, 32)),
                           ("count", (32,)), ("nblocks", (32,)), ("upto", (32,)), ("first", (32,)), ("over", (T, 32)),
                           ("place", (T, 32)), ("blockof", (T, 32)), ("picked", (T, 32)), ("places_of", (2, T)),
                           ("blocks_of", (2, T)), ("places", (2 * T, P)), ("blocks", (2 * T, TABLE)), ("empty", (TABLE,)),
                           ("target", (TABLE,)), ("source", (TABLE,)), ("past", (MAX_BLOCKS, 32)), ("expert", (MAX_BLOCKS,))):
            size = math.prod(dims)
            v = SCR[:, at:at + size]
            if len(dims) == 2:
                v = v.rearrange("p (a b) -> p a b", a=dims[0])
            if len(dims) == 3:
                v = v.rearrange("p (a b c) -> p a b c", a=dims[0], b=dims[1])
            ROUTE[name] = v
            at += size
        assert at <= 6144

        def RT(name):
            return ROUTE[name]

        def gains(stage):
            which, layer = stage.arg
            if which == "first1":
                return X, T, COLS[:, 1, :], COLS[:, 0, :]
            if which == "first2":
                return X, T, COLS[:, 3, :], COLS[:, 2, :]
            if which == "mem":
                return MEMT, MT, GCOL[:, 8 + layer, :], None
            return X, T, GCOL[:, {"mix": 4, "xattn": 6}[which] + layer, :], None

        def stick_view(g):
            b = 3 * (g % 2)
            return PS[:, b:b + 3, :].rearrange("p b n -> p (b n)")

        STICK_AT = [0, 512, 1024, 896]
        STICK_N = [S - P * kt for kt in range(T)]
        STICK_W = 1280
        E_BUF = [SCR[:, n * STICK_W:(n + 1) * STICK_W] for n in range(2)]
        A_BUF = [SCR[:, (2 + n) * STICK_W:(3 + n) * STICK_W] for n in range(2)]

        def soft_plan(stage):
            if stage.kind == "latent":
                order = attention_steps(MH, AHEAD, ("turn_q", "turn_k"))
                return order, MH, float(MQ) ** -0.5, lambda i: P * (i + 1), MV, GV + CW
            order = attention_steps(XH, AHEAD, ())
            return order, XH, float(XD) ** -0.5, lambda i: MEM, XD, 0

        def by_row(w, n0, n1):
            return w[:, n0:n1].rearrange("(p k) n -> p k n", p=P)

        def by_chunk(w, n0, n1):
            return w[:, n0:n1].rearrange("(k p) n -> p k n", p=P)

        def weight_loads(stage):
            loads = whole_loads(stage)
            return [load for unit in loads for load in (unit, None)] if stage.units else loads

        def whole_loads(stage):
            layer = stage.arg
            if (stage.kind, layer) == ("mod", 0) or stage.kind == "diff":
                w = ada_w[1 if stage.kind == "diff" else 0]
                return [(BANK, KD, by_row(w, n * BANK, (n + 1) * BANK)) for n in range(MOD_CHUNKS)]
            if stage.kind == "qkv":
                w = diff_w_in[0] if layer == 0 else sb_w_in[0]
                return [(BANK, KD, by_row(w, n * BANK, (n + 1) * BANK)) for n in range(6)]
            if stage.kind == "attn_out":
                w = diff_w_out[0] if layer == 0 else sb_w_out[0]
                return [(BANK, KD, by_chunk(w, n * BANK, (n + 1) * BANK)) for n in range(2)]
            if stage.kind == "project":
                return [(w, KD, by_row(w_in_2[layer], n, n + w)) for n, w in IN_CHUNKS]
            if stage.kind == "latent_up":
                return [(MH * MQ, 2, by_row(mla_w_uq_2[layer], 0, MH * MQ)),
                        (MH * (NOPE + MV), 2, by_row(mla_w_ukv_2[layer], 0, MH * (NOPE + MV)))]
            if stage.kind == "mix_out":
                return [(BANK, KD, by_chunk(w_out_2[layer], n * BANK, (n + 1) * BANK)) for n in range(2)]
            if stage.kind == "xq":
                return [(BANK, KD, by_row(mem_wq_2[layer], 0, BANK))]
            if stage.kind == "xkv":
                return [(BANK, KD, by_row(mem_wk_2[layer], 0, BANK)), (BANK, KD, by_row(mem_wv_2[layer], 0, BANK))]
            if stage.kind == "x_out":
                return [(D, XH, by_chunk(mem_wo_2[layer], 0, D))]
            return []

        HT_HIGH = SCR_R[:, 0:KD * S].rearrange("p (k s) -> p k s", k=KD)
        HT_LOW = HT_R.rearrange("p (k s) -> p k s", k=KD)

        def unit_width(stage, i):
            return IN_CHUNKS[i][1] if stage.kind == "project" else BANK

        def rounded_slot(u, width):
            return RING_R[:, (u % SLOTS) * SLOT:(u % SLOTS) * SLOT + KD * width].rearrange("p (k n) -> p k n", k=KD)

        def product_after(stage, steps=1):
            after = plan[plan.index(stage) + steps]
            return after if after.units else None

        block = ctx.enter_context(nc.Block())

        @block.sync
        def _(sp):
            first = [(CCOL[:, 0, :], c[0].rearrange("(p k) -> p k", p=P)), (ADAB, ada_b[0:1, :]), (CON[:, :], tables)]
            late = [
                (X[:, :, :], x[0].rearrange("(t p) n -> p t n", p=P)),
                (SUBG[:, 0:1], diff_subln_g[0].rearrange("(p k) -> p k", p=P)),
                (POSI[:, :], positions_2[0].rearrange("(t p) -> p t", p=P)),
            ]
            for n, v in enumerate((diff_lambda_q1, diff_lambda_k1, diff_lambda_q2, diff_lambda_k2)):
                late.append((LAMV[:, n, :], v[0].partition_broadcast(P)))
            for n, g in enumerate((norm1_g, norm2_g, norm_mix_2, norm_xattn_2, norm_mem_2)):
                for layer in range(DEPTH):
                    late.append((GCOL[:, 2 * n + layer, :], g[layer].rearrange("(p k) -> p k", p=P)))
            assert (len(first), len(late)) == (N_FIRST, N_LATE)
            for dst, src in first:
                sp.dma_start(dst, src).then_inc(inputs_in, 16)
            for stage in plan:
                layer = stage.arg
                if stage.kind == "mod" and layer == 1:
                    for stored_rows in mod_stored:
                        sp.wait_ge(stored_rows, 16 * MOD_CHUNKS // 2)
                    for q, part in enumerate((0, 1, 3, 4)):
                        sp.dma_start(MODC[:, q, :], mod_d[0, part * D:(part + 1) * D].rearrange("(p k) -> p k", p=P)).then_inc(mod_columns_in, 16)
                    residual_wait(sp, stage)
                    for which, part in enumerate((2, 5)):
                        sp.dma_start(GB[:, which, :], mod_d[0, part * D:(part + 1) * D].partition_broadcast(P)).then_inc(mod_gates_in, 16)
                if stage.kind == "route":
                    if stage.turn:
                        full_wait(sp, plan[[p.kind for p in plan].index("route")].fill)
                        residual_wait(sp, stage)
                    with nc.allow_non_contiguous_dma(reason="narrow router weights"):
                        sp.dma_start(RW[:, :, 0:GROUPS], router_group_w[layer].rearrange("(p k) n -> p k n", p=P)).then_inc(router_in, 16)
                        sp.dma_start(RW[:, :, GROUPS:], router_expert_w[layer].rearrange("(p k) n -> p k n", p=P)).then_inc(router_in, 16)
                    sp.dma_start(RB[:, 0:GROUPS], router_group_b[layer].partition_broadcast(P)).then_inc(router_in, 16)
                    sp.dma_start(RB[:, GROUPS:], router_expert_b[layer].rearrange("g e -> (g e)").partition_broadcast(P)).then_inc(router_in, 16)
                if stage.kind == "final":
                    residual_wait(sp, stage)
                    g = final_norm_g if stage.arg == 0 else norm_final_2
                    sp.dma_start(GB[:, 0, :], g.partition_broadcast(P)).then_inc(gain_in, 16)
                    if stage.arg == 1:
                        for t in range(T):
                            sp.wait_ge(residual_written, stage.updates + t + 1)
                            sp.dma_start(out[0].rearrange("(t p) n -> p t n", p=P)[:, t, :], X[:, t, :]).then_inc(stored, 16)
                        sp.wait_ge(stored, 16 * T)
                if stage.kind == "project":
                    if stage.turn:
                        residual_wait(sp, stage)
                    sp.dma_start(GW[0:16, :], gla_w_gate_2[layer]).then_inc(mixer_in, 16)
                    sp.dma_start(GW[16:17, :], gla_b_gate_2[layer:layer + 1, :]).then_inc(mixer_in, 16)
                    sp.dma_start(GN[:, :], gla_norm_2[layer].partition_broadcast(P)).then_inc(mixer_in, 16)
                    sp.dma_start(CWT[:, :, :], conv_w_2[layer].partition_broadcast(P)).then_inc(mixer_in, 16)
                    sp.dma_start(RG[:, 0, :], mla_q_norm_2[layer].rearrange("(p k) -> p k", p=P)).then_inc(mixer_in, 16)
                    sp.dma_start(RG[:, 1, :], mla_kv_norm_2[layer].rearrange("(p k) -> p k", p=P)).then_inc(mixer_in, 16)
                for n, load in enumerate(weight_loads(stage)):
                    if load is None:
                        continue
                    width, k, src = load
                    u = stage.load + n
                    if u == SLOTS:
                        with nc.allow_non_contiguous_dma(reason="a few positions"):
                            for late_dst, late_src in late:
                                sp.dma_start(late_dst, late_src).then_inc(late_inputs_in, 16)
                    if stage.kind == "diff":
                        if n >= 2:
                            drained_wait(sp, stage.fill + diff_fills()["mod", n - 2])
                        sp.dma_start(BIAS_ROW[n % 2], ada_b[1:2, n * BANK:(n + 1) * BANK]).then_inc(bias_row_in[n % 2], 16)
                    if u >= SLOTS:
                        full_wait(sp, last_reader[u - SLOTS])
                    sp.dma_start(slot(u, width, k), src).then_inc(slot_loaded[u % SLOTS], 16)
                if stage.kind == "xq":
                    sp.wait_ge(mixed, 3 * (stage.turn + 1))
                    sp.dma_start(MEMT, mem_2[0].rearrange("(t p) n -> p t n", p=P)).then_inc(late_inputs_in, 16)
                if stage.kind == "experts":
                    s = blocks[layer]
                    for u in range(stage.load - SLOTS, stage.load):
                        full_wait(sp, last_reader[u])
                    sp.wait_ge(blocks_ready, layer + 1)
                    n_blocks = sp.value_load(CTRL[0:1, 0:1], min_val=MIN_BLOCKS, max_val=MAX_BLOCKS)
                    with sp.Fori(0, n_blocks) as b:
                        e = sp.value_load(CTRL[0:1, bass.ds(b + 1, 1)], min_val=0, max_val=EXPERTS - 1)
                        gate = expert_w_gate[layer, bass.ds(e, 1)].rearrange("a (p k) n -> p (a k) n", p=P)
                        up = expert_w_up[layer, bass.ds(e, 1)].rearrange("a (p k) n -> p (a k) n", p=P)
                        down = expert_w_down[layer, bass.ds(e, 1)].rearrange("a (p k) n -> p (a k) n", p=P)
                        half = KD // 2
                        for n, (dst, src) in enumerate((
                                (W_GATE[:, 0:half, :], gate[:, 0:half, :]), (W_GATE[:, half:, :], gate[:, half:, :]),
                                (W_UP[:, 0:half, :], up[:, 0:half, :]), (W_UP[:, half:, :], up[:, half:, :]),
                                (W_DOWN[:, 0], down[:, :, 0:BANK]), (W_DOWN[:, 1], down[:, :, BANK:]))):
                            sp.wait_ge(s.used[n], b + 1)
                            sp.dma_start(dst, src).then_inc(s.loaded[n], 16)
                    sp.wait_ge(experts_over, 3 * (layer + 1))

        @block.tensor
        def _(pe):
            def fill_done(last, n):
                last.then_inc(bank_full[n % BANKS], 1)

            pe.wait_ge(inputs_in, 16 * N_FIRST)
            for stage in plan:
                f0, u0, layer = stage.fill, stage.load, stage.arg

                if stage.kind == "mod" and layer == 0:
                    pe.wait_ge(dve_prepared, 1)
                    for n in range(12):
                        free_wait(pe, f0 + n)
                        loaded_wait(pe, u0 + n)
                        w = slot(u0 + n, BANK)
                        for k in range(KD):
                            pe.matmul(bank(f0 + n), CB[:, k, :], w[:, k, :], start=k == 0, stop=False)
                        fill_done(pe.matmul(bank(f0 + n), ones[0:1, :], ADAB[:, n * BANK:(n + 1) * BANK], start=False, stop=True), f0 + n)
                    fc = f0 + 12
                    free_wait(pe, fc)
                    for q, part in enumerate((0, 1, 3, 4)):
                        drained_wait(pe, f0 + 2 * part)
                        drained_wait(pe, f0 + 2 * part + 1)
                        for k in range(KD):
                            last = pe.matmul(bank(fc)[:, q * KD + k:q * KD + k + 1], MODROW[0:1, q, k::KD], ones[0:1, 0:1], start=True, stop=True)
                    fill_done(last, fc)

                if stage.kind == "norm":
                    _, tiles, _, _ = gains(stage)
                    for k in range(KD):
                        n = f0 + k
                        free_wait(pe, n)
                        for t in range(tiles):
                            if k == 0:
                                pe.wait_ge(xn_ready, stage.tiles_before + t + 1)
                            last = pe.transpose(bank(n)[:, t * P:(t + 1) * P], XN[:, t, k::KD], ident)
                        fill_done(last, n)

                def unit_ready(i):
                    loaded_wait(pe, u0 + 2 * i + 1)
                    pe.wait_ge(unit_low, stage.units_before + i + 1)
                    return rounded_slot(u0 + 2 * i + 1, unit_width(stage, i)), rounded_slot(u0 + 2 * i, unit_width(stage, i))

                def chunk_ready(k):
                    pe.wait_ge(chunk_high, stage.splits_before + k + 1)
                    pe.wait_ge(chunk_low, stage.splits_before + k + 1)

                def split_fill(n, out_ap, left, right):
                    free_wait(pe, n)
                    for k in range(KD):
                        if n == f0:
                            chunk_ready(k)
                        (left_high, left_low), (right_high, right_low) = left(k), right(k)
                        pe.matmul(out_ap, left_high, right_high, start=k == 0, stop=False)
                        pe.matmul(out_ap, left_low, right_high, start=False, stop=False)
                        last = pe.matmul(out_ap, left_high, right_low, start=False, stop=k == KD - 1)
                    fill_done(last, n)

                if stage.kind == "qkv":
                    for j in range(24):
                        if j % 4 == 0:
                            w_high, w_low = unit_ready(j // 4)
                        cols = slice((j % 4) * P, (j % 4 + 1) * P)
                        if j < 16:
                            split_fill(f0 + j, bank(f0 + j), lambda k: (w_high[:, k, cols], w_low[:, k, cols]),
                                       lambda k: (HT_HIGH[:, k, :], HT_LOW[:, k, :]))
                        else:
                            split_fill(f0 + j, bank(f0 + j), lambda k: (HT_HIGH[:, k, cols], HT_LOW[:, k, cols]),
                                       lambda k: (w_high[:, k, :], w_low[:, k, :]))

                if stage.kind in ("xq", "xkv"):
                    norm_fill = f0 - KD
                    if stage.kind == "xq":
                        cols, v_tiles = S, 0
                    else:
                        cols, v_tiles = MEM, MT
                    w = slot(u0, BANK)
                    loaded_wait(pe, u0)
                    for j in range(XH):
                        n = f0 + j
                        free_wait(pe, n)
                        for k in range(KD):
                            if j == 0:
                                drained_wait(pe, norm_fill + k)
                            last = pe.matmul(bank(n)[:, 0:cols], w[:, k, j * P:(j + 1) * P], HT[:, k, 0:cols], start=k == 0, stop=k == KD - 1)
                        fill_done(last, n)
                    for t in range(v_tiles):
                        n = f0 + XH + t
                        if t == 0:
                            loaded_wait(pe, u0 + 1)
                            w = slot(u0 + 1, BANK)
                        free_wait(pe, n)
                        for k in range(KD):
                            last = pe.matmul(bank(n), HT[:, k, t * P:(t + 1) * P], w[:, k, :], start=k == 0, stop=k == KD - 1)
                        fill_done(last, n)

                if stage.kind == "diff":
                    for n in range(f0 - BANKS, f0):
                        drained_wait(pe, n)
                    made = {what_s: f0 + n for what_s, n in diff_fills().items()}
                    for what, s in diff_order():
                        if what in ("mod", "mod_rest"):
                            n, u = made["mod", s], u0 + s
                            if what == "mod":
                                free_wait(pe, n)
                                loaded_wait(pe, u)
                            for k in range(0, KD // 2) if what == "mod" else range(KD // 2, KD):
                                last = pe.matmul(bank(n)[0:1, :], CCOL[:, 2, k:k + 1], slot(u, BANK)[:, k, :], start=k == 0, stop=k == KD - 1)
                            if what == "mod_rest":
                                fill_done(last, n)
                            continue
                        n = made[what, s]
                        h, i = divmod(s, T)
                        rows = slice(i * P, (i + 1) * P)
                        free_wait(pe, n)
                        if what in ("map0", "map1"):
                            m = HD * (what == "map1")
                            last = pe.matmul(bank(n)[:, 0:(i + 1) * P], QT[m:m + HD, h, rows], KT[m:m + HD, h, 0:(i + 1) * P], start=True, stop=True)
                        if what == "turned":
                            pe.wait_ge(diff_ready, s + 1)
                            for kt in range(i + 1):
                                last = pe.transpose(bank(n)[:, kt * P:(kt + 1) * P], SA(s)[:, 0, kt * P:(kt + 1) * P], ident)
                        if what == "values":
                            drained_wait(pe, made["turned", s])
                            for kt in range(i + 1):
                                last = pe.matmul(bank(n)[:, 0:P], AT(s)[:, kt * P:(kt + 1) * P], V[:, kt, h * P:(h + 1) * P], start=kt == 0, stop=kt == i)
                        fill_done(last, n)

                if stage.kind == "stick":
                    for n in range(f0 - BANKS, f0):
                        drained_wait(pe, n)

                    def head_rows(g):
                        return slice(HD * (g % 2), HD * (g % 2) + HD)

                    def scores(g):
                        if g >= 2:
                            pe.wait_ge(a_raw, g - 1)
                        rows, c, z = head_rows(g), g // 2, stick_view(g)
                        for kt in (0, 1, 3, 2):
                            last = pe.matmul(z[:, STICK_AT[kt]:STICK_AT[kt] + STICK_N[kt]], KT[rows, c, kt * P:(kt + 1) * P],
                                             QT[rows, c, kt * P:], start=kt != 3, stop=True, skip_group_check=True)
                        last.then_inc(z_full, 1)

                    def sums(g):
                        pe.wait_ge(sp_ready, g + 1)
                        z, sp_rows = stick_view(g), E_BUF[g % 2]
                        for kt in range(T):
                            for jt in range(kt, T):
                                at = STICK_AT[kt] + P * (jt - kt)
                                last = pe.matmul(z[:, at:at + STICK_N[jt]], const("neg_ge" if jt == kt else "neg_ones"),
                                                 sp_rows[:, STICK_AT[jt]:STICK_AT[jt] + STICK_N[jt]], start=False, stop=True, skip_group_check=True)
                        last.then_inc(r_full, 1)

                    def values(g):
                        pe.wait_ge(a_ready, g + 1)
                        if g % 2 == 0 and g >= 4:
                            pe.wait_ge(o_drained, g // 2 - 1)
                        rows, a = head_rows(g), A_BUF[g % 2]
                        for kt in range(T):
                            last = pe.matmul(PS[rows, 6 + (g // 2) % 2, kt * P:], V[:, kt, g * HD:(g + 1) * HD],
                                             a[:, STICK_AT[kt]:STICK_AT[kt] + STICK_N[kt]], start=kt == 0, stop=True, skip_group_check=True)
                        last.then_inc(o_full, 1)

                    scores(0)
                    for g in range(SB_HEADS):
                        if g + 1 < SB_HEADS:
                            scores(g + 1)
                        sums(g)
                        if g:
                            values(g - 1)
                    values(SB_HEADS - 1)

                if stage.kind in ("otrans", "mtrans", "xtrans"):
                    if stage.kind == "otrans":
                        pe.wait_ge(group_normed, normed_after(stage))
                    elif stage.kind == "mtrans":
                        pe.wait_ge(mixed, 3 * (stage.turn + 1))
                    else:
                        for n in range(f0 - BANKS, f0):
                            drained_wait(pe, n)
                    for c in range(XH if stage.kind == "xtrans" else KD):
                        n = f0 + c
                        free_wait(pe, n)
                        for t in range(T):
                            last = pe.transpose(bank(n)[:, t * P:(t + 1) * P], XN[:, t, c * P:(c + 1) * P], ident)
                        fill_done(last, n)

                if stage.kind in ("attn_out", "mix_out") and stage.units:
                    units = [unit_ready(0)]
                    for t in range(T):
                        cols = slice(t * P, (t + 1) * P)
                        for half in range(2):
                            if (t, half) == (0, 1):
                                units.append(unit_ready(1))
                            w_high, w_low = units[half]
                            n = f0 + 2 * t + half
                            split_fill(n, bank(n), lambda k: (HT_HIGH[:, k, cols], HT_LOW[:, k, cols]), lambda k: (w_high[:, k, :], w_low[:, k, :]))
                elif stage.kind in ("attn_out", "mix_out", "x_out"):
                    chunks = XH if stage.kind == "x_out" else KD
                    w = [slot(u0, D, XH)[:, :, h * BANK:(h + 1) * BANK] if stage.kind == "x_out" else slot(u0 + h, BANK) for h in range(2)]
                    for t in range(T):
                        for half in range(2):
                            n = f0 + 2 * t + half
                            free_wait(pe, n)
                            if t == 0:
                                loaded_wait(pe, u0 + (0 if stage.kind == "x_out" else half))
                            for k in range(chunks):
                                if n == f0:
                                    if stage.kind == "attn_out" and layer == 1:
                                        pe.wait_ge(o_drained, k + 1)
                                    else:
                                        drained_wait(pe, f0 - chunks + k)
                                last = pe.matmul(bank(n), HT[:, k, t * P:(t + 1) * P], w[half][:, k, :], start=k == 0, stop=k == chunks - 1)
                            fill_done(last, n)

                if stage.kind == "route":
                    free_wait(pe, f0)
                    pe.wait_ge(router_in, 64 * (layer + 1))
                    for k in range(KD):
                        drained_wait(pe, f0 - KD + k)
                    for t in range(T):
                        for k in range(KD):
                            last = pe.matmul(bank(f0)[:, t * 36:t * 36 + 36], HT[:, k, t * P:(t + 1) * P], RW[:, k, :], start=k == 0, stop=k == KD - 1)
                    fill_done(last, f0)
                    free_wait(pe, f0 + 1)
                    pe.wait_ge(assigned, layer + 1)
                    a = RT("assigned")
                    for t in range(T):
                        for j in range(t + 1):
                            pe.matmul(bank(f0 + 1)[:, t * EXPERTS:(t + 1) * EXPERTS], const("before") if j == t else ones, a[:, j, :], start=j == 0, stop=j == t)
                    for t in range(T):
                        last = pe.matmul(bank(f0 + 1)[:, T * EXPERTS:(T + 1) * EXPERTS], ones, a[:, t, :], start=t == 0, stop=t == T - 1)
                    fill_done(last, f0 + 1)
                    free_wait(pe, f0 + 2)
                    pe.wait_ge(one_hots, layer + 1)
                    for j in range(2 * T):
                        last = pe.matmul(bank(f0 + 2)[:, 0:TABLE], RT("places")[:, j, :], RT("blocks")[:, j, :], start=j == 0, stop=j == 2 * T - 1)
                    fill_done(last, f0 + 2)

                if stage.kind == "experts":
                    s = blocks[layer]

                    def rows_by_feature(half):
                        for k in range(4 * half, 4 * half + 4):
                            last = pe.transpose(PS[:, half, (k % 4) * P:(k % 4 + 1) * P], XG[:, k::KD], ident)
                        last.then_inc(s.rows_turned, 1)

                    def part_product(b, n, bk, high, low, low_ready, first, final):
                        pe.wait_ge(s.high_ready, PARTS * b + n + 1)
                        if n < 4:
                            pe.wait_ge(s.low_ready, 4 * b + n + 1)
                        else:
                            pe.wait_ge(s.late_low_ready, 2 * b + n - 3)
                        w_high, w_low = (w[n].rearrange("p (k n) -> p k n", k=4) for w in (HIGH, LOW))
                        for k in range(4):
                            pe.matmul(PS[:, bk, :], high(k), w_high[:, k, :], start=first and k == 0, stop=False)
                            pe.matmul(PS[:, bk, :], high(k), w_low[:, k, :], start=False, stop=False)
                        low_ready()
                        for k in range(4):
                            last = pe.matmul(PS[:, bk, :], low(k), w_high[:, k, :], start=False, stop=final and k == 3)
                        last.then_inc(s.used[n], 1)

                    for n in range(max(0, f0 - BANKS), f0):
                        drained_wait(pe, n)
                    pe.wait_ge(blocks_ready, layer + 1)
                    n_blocks = pe.value_load(CTRL[0:1, 0:1], min_val=MIN_BLOCKS, max_val=MAX_BLOCKS)
                    for used in s.used:
                        pe.sem_inc(used, 1)
                    pe.wait_ge(s.gathered, 16)
                    rows_by_feature(0)
                    rows_by_feature(1)
                    with pe.Fori(0, n_blocks) as b:
                        pe.wait_ge(s.hidden, b + 1)
                        for n in range(4):
                            half = n % 2
                            if n < 2:
                                pe.wait_ge(s.rows_high, 2 * b + half + 1)
                            part_product(b, n, 2 + n // 2, lambda k: XGT_HIGH[:, 4 * half + k, :], lambda k: XGT_LOW[:, 4 * half + k, :],
                                         lambda: n < 2 and pe.wait_ge(s.rows_low, 2 * b + half + 1), half == 0, half == 1)
                        pe.wait_ge(s.gathered, 16 * b + 32)
                        rows_by_feature(0)
                        pe.wait_ge(s.hidden, b + 2)
                        for k in range(KH):
                            last = pe.transpose(PS[:, 4, k * P:(k + 1) * P], HID[:, k::KH], ident)
                        last.then_inc(s.hidden_turned, 1)
                        rows_by_feature(1)
                        pe.wait_ge(s.hidden_high, b + 1)
                        for half, read in enumerate((s.y_left, s.y_right)):
                            pe.wait_ge(read, b + 1)
                            part_product(b, 4 + half, 5 + half, lambda k: HIDT_HIGH[:, k * P:(k + 1) * P], lambda k: HIDT_LOW[:, k * P:(k + 1) * P],
                                         lambda: half or pe.wait_ge(s.hidden_low, b + 1), True, True)
                    pe.wait_ge(experts_over, 3 * (layer + 1))

                if stage.kind == "project":
                    for j, (_, width) in enumerate(IN_CHUNKS):
                        w_high, w_low = unit_ready(j)
                        for t in range(T):
                            n, cols = f0 + T * j + t, slice(t * P, (t + 1) * P)
                            split_fill(n, bank(n)[:, 0:width], lambda k: (HT_HIGH[:, k, cols], HT_LOW[:, k, cols]),
                                       lambda k: (w_high[:, k, :], w_low[:, k, :]))

                if stage.kind == "latent_up":
                    pe.wait_ge(group_normed, normed_after(stage))
                    for j in range(4):
                        n = f0 + j
                        at = (C_CQ, C_CKV)[j // 2] + j % 2
                        free_wait(pe, n)
                        for t in range(T):
                            last = pe.transpose(bank(n)[:, t * P:(t + 1) * P], PR[:, t, at:at + RANK - j % 2:2], ident)
                        fill_done(last, n)
                    for j, width in enumerate((MH * MQ, MH * (NOPE + MV))):
                        loaded_wait(pe, u0 + j)
                        w = slot(u0 + j, width, 2)
                        for t in range(T):
                            for half in range(2):
                                n = f0 + 4 + 2 * T * j + 2 * t + half
                                free_wait(pe, n)
                                for k in range(2):
                                    if t == 0 and half == 0:
                                        drained_wait(pe, f0 + 2 * j + k)
                                    last = pe.matmul(bank(n)[:, 0:width // 2], HT[:, 2 * j + k, t * P:(t + 1) * P],
                                                     w[:, k, half * width // 2:(half + 1) * width // 2], start=k == 0, stop=k == 1)
                                fill_done(last, n)

                if stage.kind in ("latent", "xattn"):
                    order, heads, _, span, dv, _ = soft_plan(stage)
                    latent = stage.kind == "latent"
                    for n in range(f0 - BANKS, f0):
                        drained_wait(pe, n)
                    if latent:
                        pe.wait_ge(mixer_up, 2 * (stage.turn + 1))
                    made = {what_s: n for n, what_s in enumerate(order, f0)}
                    for (what, s), n in made.items():
                        h, i = divmod(s, T)
                        free_wait(pe, n)
                        if what in ("turn_q", "turn_k"):
                            src = QM if what == "turn_q" else KM
                            for t in range(T):
                                last = pe.transpose(bank(n)[0:MQ, t * P:(t + 1) * P], src[:, t, h, :], ident)
                        if what == "scores":
                            L = span(i)
                            if latent:
                                if i == 0:
                                    drained_wait(pe, made["turn_q", s])
                                    drained_wait(pe, made["turn_k", s])
                                pe.matmul(bank(n)[:, 0:L], LQT(h)[0:MQ, i * P:(i + 1) * P], LKT(h)[0:MQ, 0:L], start=True, stop=False, skip_group_check=True)
                                last = pe.matmul(bank(n)[:, L - P:L], ident, const("causal"), start=False, stop=True, skip_group_check=True)
                            else:
                                last = pe.matmul(bank(n)[:, 0:L], XQT[:, h, i * P:(i + 1) * P], XKT[:, h, :], start=True, stop=True)
                        if what == "turned":
                            drained_wait(pe, made["scores", s])
                            for kt in range(span(i) // P):
                                last = pe.transpose(bank(n)[:, kt * P:(kt + 1) * P], SP1(stage, s)[:, kt * P:(kt + 1) * P], ident)
                        if what == "values":
                            drained_wait(pe, made["turned", s])
                            for kt in range(span(i) // P):
                                v = VM[:, kt, h, :] if latent else XV[:, kt, h * P:(h + 1) * P]
                                last = pe.matmul(bank(n)[:, 0:dv], AT1(stage, s)[:, kt * P:(kt + 1) * P], v, start=kt == 0, stop=kt == span(i) // P - 1)
                        fill_done(last, n)

                if stage.kind == "gla":
                    f_glr, f_z, f_b, f_last, f_dec = f0, f0 + 1, f0 + 3, f0 + 5, f0 + 7
                    free_wait(pe, f_glr)
                    for t in range(T):
                        last = pe.transpose(bank(f_glr)[0:16, t * P:(t + 1) * P], PR[:, t, C_GLR:C_GLR + 16], ident)
                    fill_done(last, f_glr)
                    drained_wait(pe, f_glr)
                    pe.wait_ge(mixer_in, 96 * (stage.turn + 1))
                    for t in range(T):
                        n = f_z + t // 2
                        if t % 2 == 0:
                            free_wait(pe, n)
                        last = pe.matmul(bank(n)[:, (t % 2) * GQK:(t % 2 + 1) * GQK], GLT[0:17, t * P:(t + 1) * P], GW[0:17, :], start=True, stop=True)
                        if t % 2:
                            fill_done(last, n)
                    pe.wait_ge(soft_ready, 2 * (stage.turn + 1))
                    for first, table in ((f_b, "gla_cum"), (f_last, "gla_last")):
                        for j in range(2):
                            free_wait(pe, first + j)
                            fill_done(pe.matmul(bank(first + j)[:, 0:2 * GQK], const(table), SOFT[:, 2 * j:2 * j + 2, :].rearrange("p t n -> p (t n)"), start=True, stop=True), first + j)
                    free_wait(pe, f_dec)
                    for h in range(GH):
                        for t in range(T):
                            last = pe.matmul(bank(f_dec)[0:GDK, h * 8 + 2 * t:h * 8 + 2 * t + 2], SOFT[:, t, h * GDK:(h + 1) * GDK], const("gla_chunk"), start=True, stop=True)
                    fill_done(last, f_dec)
                    f = f0 + 8
                    pe.wait_ge(decayed, 3 * (stage.turn + 1))
                    for h in range(GH):
                        for src in (QD, KI):
                            free_wait(pe, f)
                            for t in range(T):
                                last = pe.transpose(bank(f)[0:GDK, t * P:(t + 1) * P], src[:, t, h * GDK:(h + 1) * GDK], ident)
                            fill_done(last, f)
                            f += 1

                    def outputs(h, n):
                        free_wait(pe, n)
                        drained_wait(pe, gla_fill(stage, "scores", h))
                        pe.wait_ge(state_ready, GH * stage.turn + h + 1)
                        for t in range(T):
                            cols = slice(t * GDV, (t + 1) * GDV)
                            last = pe.matmul(bank(n)[:, cols], GAT(h)[:, t, :], PR[:, t, C_GV + h * GDV:C_GV + (h + 1) * GDV], start=True, stop=False, skip_group_check=True)
                            for half in range(2):
                                if 2 * t + half:
                                    rows = slice(CHUNK * half, CHUNK * (half + 1))
                                    last = pe.matmul(bank(n)[rows, cols], GQT[0:GDK, h, t * P + CHUNK * half:t * P + CHUNK * (half + 1)],
                                                     GST(h)[0:GDK, 2 * t + half, :], start=False, stop=True, skip_group_check=True)
                        fill_done(last, n)

                    for h in range(GH):
                        for part in range(2):
                            n = gla_fill(stage, "update", h, part)
                            free_wait(pe, n)
                            for j in range(part, 7, 2):
                                rows = slice(CHUNK * part, CHUNK * (part + 1))
                                last = pe.matmul(bank(n)[0:GDK, (j // 2) * GDV:(j // 2 + 1) * GDV], KE[rows, j // 2, h * GDK:(h + 1) * GDK],
                                                 PR[rows, j // 2, C_GV + h * GDV:C_GV + (h + 1) * GDV], start=True, stop=True)
                            fill_done(last, n)
                        n = gla_fill(stage, "scores", h)
                        free_wait(pe, n)
                        drained_wait(pe, f0 + 8 + 2 * h)
                        drained_wait(pe, f0 + 9 + 2 * h)
                        for t in range(T):
                            cols = slice(t * P, (t + 1) * P)
                            last = pe.matmul(bank(n)[:, cols], GKT[0:GDK, h, cols], GQT[0:GDK, h, cols], start=True, stop=True)
                        fill_done(last, n)
                        if h:
                            outputs(h - 1, gla_fill(stage, "outputs", h - 1))
                    outputs(GH - 1, gla_fill(stage, "outputs", GH - 1))

                if stage.kind == "conv":
                    pe.wait_ge(conv_in, stage.turn + 1)
                    for t in range(T):
                        n = f0 + t // 2
                        if t % 2 == 0:
                            free_wait(pe, n)
                        pieces = [("shift1", CU1[:, t, :]), ("shift2", CU0[:, t, :])]
                        if t:
                            pieces += [("carry1", CU1[:, t - 1, :]), ("carry2", CU0[:, t - 1, :])]
                        for j, (table, u) in enumerate(pieces):
                            last = pe.matmul(bank(n)[:, (t % 2) * CW:(t % 2 + 1) * CW], const(table), u, start=j == 0, stop=j == len(pieces) - 1)
                        if t % 2:
                            fill_done(last, n)

        @block.scalar
        def _(act):
            own = [0]

            def settle(instruction):
                own[0] += 1
                instruction.then_inc(act_done, 1)
                act.wait_ge(act_done, own[0])

            def drained(instruction, n):
                instruction.then_inc(bank_drained[n % BANKS], 1)

            def unit_high(stage, i):
                if i == stage.units:
                    return
                u, width = stage.load + 2 * i, unit_width(stage, i)
                loaded_wait(act, u)
                full_wait(act, last_reader[u + 1 - SLOTS])
                act.copy(rounded_slot(u + 1, width), slot(u, width)).then_inc(slot_loaded[(u + 1) % SLOTS], 16)

            act.wait_ge(inputs_in, 16 * N_FIRST)
            act.activation(CCOL[:, 1, :], CCOL[:, 0, :], ACT.Exp, scale=-1.0).then_inc(act_prepared, 1)
            for stage in plan:
                f0, layer = stage.fill, stage.arg

                if stage.kind == "mod" and layer == 0:
                    for q, part in enumerate((0, 1, 3, 4)):
                        for half in range(2):
                            n = f0 + 2 * part + half
                            full_wait(act, n)
                            drained(act.copy(MODROW[:, q, half * BANK:(half + 1) * BANK], bank(n)[0:1, :]), n)
                    act.wait_ge(late_inputs_in, 16 * N_LATE)
                    act.wait_ge(dve_prepared, 2)
                    act.activation(LAM[:, 2:4], LAM[:, 0:2], ACT.Exp).then_inc(act_prepared, 1)

                if stage.kind in ("norm", "final"):
                    src, tiles = (X, T) if stage.kind == "final" else gains(stage)[0:2]
                    if src is not X:
                        act.wait_ge(late_inputs_in, 16 * (N_LATE + stage.arg[1] + 1))
                        full_wait(act, f0 - XH - 1)
                    for t in range(tiles):
                        if src is X:
                            residual_wait(act, stage, t)
                        last = act.activation(XN[:, t, :], src[:, t, :], ACT.Square, accum_out=SUMSQ[:, t:t + 1])
                    last.then_inc(sumsq_ready, 1)
                if stage.kind == "norm":
                    _, tiles, gain, shift = gains(stage)
                    if stage.arg[0] == "first2":
                        for t in range(T):
                            act.wait_ge(xn_ready, stage.tiles_before + t + 1)
                            act.dma_start(xn_d[t * P:(t + 1) * P, :], XN[:, t, :]).then_inc(xn_stored, 16)
                    if product_after(stage):
                        unit_high(product_after(stage), 0)
                    for k in range(KD):
                        n = f0 + k
                        if k % 2 == 0:
                            full_wait(act, n)
                            bias = 0.0 if shift is None else shift[:, k:k + 1]
                            drained(act.activation(HT[:, k, 0:tiles * P], bank(n)[:, 0:tiles * P], ACT.Identity, bias=bias, scale=gain[:, k:k + 1]), n)
                        if product_after(stage):
                            drained_wait(act, n)
                            act.copy(HT_HIGH[:, k, :], HT[:, k, :]).then_inc(chunk_high, 1)

                if stage.kind == "qkv":
                    for j in range(8):
                        if j % T == 0:
                            unit_high(stage, j // T + 1)
                        full_wait(act, f0 + j)
                        drained(act.mul(QT[:, j, :], bank(f0 + j), HD ** -0.5), f0 + j)
                    unit_high(stage, 3)
                    unit_high(stage, 4)
                    for j in range(0, 8, 2):
                        n = f0 + 16 + j
                        if j % T == 0:
                            unit_high(stage, 5 + j // T)
                        full_wait(act, n)
                        drained(act.copy(V[:, j % T, (j // T) * BANK:(j // T + 1) * BANK], bank(n)), n)

                if stage.kind == "diff":
                    made = {what_s: f0 + n for what_s, n in diff_fills().items()}
                    steps = DIFF_HEADS * T
                    for r in range(steps + AHEAD + 1):
                        s = r - AHEAD
                        if 0 <= s < steps:
                            L, n = P * (s % T + 1), made["turned", s]
                            full_wait(act, n)
                            if s >= 2:
                                full_wait(act, made["values", s - 2])
                            drained(act.copy(AT(s)[:, 0:L], bank(n)[:, 0:L]), n)
                        if r < steps:
                            L = P * (r % T + 1)
                            act.wait_ge(negmax_ready, r + 1)
                            for m in range(2):
                                act.activation(SA(r)[:, m, 0:L], SA(r)[:, m, 0:L], ACT.Exp, bias=MX[:, r % 3, m:m + 1],
                                               accum_out=SUM[:, r % 3, m:m + 1]).then_inc(diff_exp, 1)
                        s = r - AHEAD - 1
                        if s >= 0:
                            h, i = divmod(s, T)
                            n = made["values", s]
                            full_wait(act, n)
                            drained(act.copy(XN[:, i, h * P:(h + 1) * P], bank(n)[:, 0:P]), n)

                if stage.kind == "stick":
                    def logs(g):
                        act.wait_ge(z_clamped, g + 1)
                        e = E_BUF[g % 2]
                        settle(act.activation(e, e, ACT.Exp))
                        act.activation(e, e, ACT.Ln, bias=1.0).then_inc(z_log, 1)

                    logs(0)
                    for g in range(SB_HEADS):
                        if g + 1 < SB_HEADS:
                            logs(g + 1)
                        act.wait_ge(r_full, g + 1)
                        if g >= 2:
                            act.wait_ge(o_full, g - 1)
                        act.activation(A_BUF[g % 2], stick_view(g)[:, 0:STICK_W], ACT.Exp).then_inc(a_raw, 1)

                if stage.kind == "otrans":
                    for n in range(f0 - BANKS, f0):
                        drained_wait(act, n)
                    for t in range(T):
                        act.activation(HT[:, 2 * t:2 * t + 2, :].rearrange("p a n -> p (a n)"), XN[:, t, :], ACT.Square).then_inc(squares_ready, 1)
                    for i in range(2):
                        unit_high(product_after(stage), i)
                if stage.kind == "latent_up":
                    for n in range(f0 - BANKS, f0):
                        drained_wait(act, n)
                    for j, at in enumerate((C_CQ, C_CKV)):
                        for t in range(T):
                            last = act.activation(SCR[:, (j * T + t) * RANK:(j * T + t + 1) * RANK], PR[:, t, at:at + RANK], ACT.Square, accum_out=SUMSQ[:, j * T + t:j * T + t + 1])
                    last.then_inc(squares_ready, 1)
                    for j in range(2 * T):
                        n = f0 + 4 + 2 * T + j
                        t, h = j // 2, 3 * (j % 2)
                        full_wait(act, n)
                        kv = bank(n)[:, 0:3 * (NOPE + MV)].rearrange("p (h n) -> p h n", h=3)
                        act.copy(KM[:, t, h:h + 3, 0:NOPE], kv[:, :, 0:NOPE])
                        drained(act.copy(VM[:, t, h:h + 3, :], kv[:, :, NOPE:]), n)
                    if stage.turn == 0:
                        act.wait_ge(angles, 1)
                        act.activation(SIN[:, :, :], SIN[:, :, :], ACT.Sin)
                        act.activation(COS[:, :, :], COS[:, :, :], ACT.Sin).then_inc(rope_ready, 1)

                if stage.kind in ("otrans", "mtrans", "xtrans"):
                    for c in range(XH if stage.kind == "xtrans" else KD):
                        n = f0 + c
                        if c % 2 == 0:
                            full_wait(act, n)
                            scale = SUBG[:, 1:2] if stage.kind == "otrans" else 1.0
                            drained(act.activation(HT[:, c, :], bank(n), ACT.Identity, scale=scale), n)
                        if product_after(stage):
                            drained_wait(act, n)
                            act.copy(HT_HIGH[:, c, :], HT[:, c, :]).then_inc(chunk_high, 1)

                if stage.kind == "route":
                    act.wait_ge(group_shift, layer + 1)
                    act.activation(RT("gexp"), RT("gshift"), ACT.Exp).then_inc(group_exp, 1)
                    act.wait_ge(pair_diff, layer + 1)
                    act.activation(RT("gapexp"), RT("gap"), ACT.Exp).then_inc(pair_exp, 1)

                if stage.kind == "experts":
                    s = blocks[layer]
                    gain, shift = COLS[:, 3, :], COLS[:, 2, :]

                    def first_chunks():
                        for k in range(KD // 2):
                            last = act.activation(XGT[:, k, :], PS[:, k // 4, (k % 4) * P:(k % 4 + 1) * P], ACT.Identity, bias=shift[:, k:k + 1], scale=gain[:, k:k + 1])
                        last.then_inc(s.first_scaled, 1)

                    def high(b, n):
                        act.wait_ge(s.loaded[n], 16 * b + 16)
                        act.copy(HIGH[n], LOADED[n]).then_inc(s.high_ready, 1)

                    def rows_high(b, half, scaled):
                        act.wait_ge(scaled, b + 1)
                        act.copy(XGT_HIGH[:, 4 * half:4 * half + 4, :], XGT[:, 4 * half:4 * half + 4, :]).then_inc(s.rows_high, 1)

                    act.wait_ge(blocks_ready, layer + 1)
                    act.wait_ge(xn_stored, 16 * T * (layer + 1))
                    last_block = act.value_load(CTRL[0:1, MAX_BLOCKS + 1:MAX_BLOCKS + 2], min_val=MIN_BLOCKS - 1, max_val=MAX_BLOCKS - 1)
                    act.sem_inc(s.y_left, 1)
                    act.sem_inc(s.y_right, 1)
                    act.wait_ge(s.rows_turned, 1)
                    first_chunks()
                    rows_high(0, 0, s.first_scaled)
                    rows_high(0, 1, s.last_scaled)
                    for n in range(4):
                        high(0, n)
                    def one_block(b, more):
                        high(b, 4)
                        act.wait_ge(s.used[1], b + 2)
                        act.activation(GE, PS[:, 2, :], ACT.Exp, scale=-1.0).then_inc(s.gate_exp, 1)
                        high(b, 5)
                        act.wait_ge(s.rows_low, 2 * b + 2)
                        act.wait_ge(s.rows_turned, 2 * b + 3)
                        first_chunks()
                        act.wait_ge(s.hidden_turned, b + 1)
                        act.copy(HIDT_HIGH, PS[:, 4, :]).then_inc(s.hidden_high, 1)
                        rows_high(b + 1, 0, s.first_scaled)
                        rows_high(b + 1, 1, s.last_scaled)
                        for n in (0, 1, 2) if more else ():
                            high(b + 1, n)
                        act.wait_ge(s.used[4], b + 2)
                        act.wait_ge(s.y_free, b + 1)
                        act.copy(YB[:, 0:BANK], PS[:, 5, :]).then_inc(s.y_left, 1)
                        if more:
                            high(b + 1, 3)
                        act.wait_ge(s.used[5], b + 2)
                        act.copy(YB[:, BANK:], PS[:, 6, :]).then_inc(s.y_right, 1)

                    with act.Fori(0, last_block) as b:
                        one_block(b, True)
                    one_block(last_block, False)
                    act.drain().then_inc(experts_over, 1)

                if stage.kind == "combine":
                    act.wait_ge(experts_over, 3 * (layer + 1))
                    for t in range(T):
                        for j in range(2):
                            act.dma_start(Y2[:, j, t, :], y_d[j * S + t * P:j * S + (t + 1) * P, :]).then_inc(rows_back[t], 16)
                    for t in range(T):
                        act.wait_ge(rows_back[t], 32 * (layer + 1))
                        act.mul(Y2[:, 0, t, :], Y2[:, 0, t, :], WTS[:, 0, t:t + 1]).then_inc(weighted, 1)

                if stage.kind == "project":
                    for j, (at, width) in enumerate(IN_CHUNKS):
                        unit_high(stage, j + 1)
                        for t in range(0, T, 2):
                            n = f0 + T * j + t
                            full_wait(act, n)
                            drained(act.copy(PR[:, t, at:at + width], bank(n)[:, 0:width]), n)

                if stage.kind in ("latent", "xattn"):
                    order, heads, scale, span, dv, _ = soft_plan(stage)
                    made = {what_s: n for n, what_s in enumerate(order, f0)}
                    base = soft_base(stage)
                    steps = heads * T
                    def turned_q(r):
                        if stage.kind == "latent" and r % T == 0 and r < steps:
                            nq = made["turn_q", r]
                            full_wait(act, nq)
                            if r >= 2 * T:
                                full_wait(act, made["scores", r - T - 1])
                            drained(act.copy(LQT(r // T)[0:MQ, :], bank(nq)[0:MQ, :]), nq)

                    turned_q(0)
                    for r in range(steps + AHEAD):
                        turned_q(r + 1)
                        s = r - AHEAD
                        if s >= 0:
                            L, n = span(s % T), made["turned", s]
                            full_wait(act, n)
                            if s >= 2:
                                full_wait(act, made["values", s - 2])
                            drained(act.copy(AT1(stage, s)[:, 0:L], bank(n)[:, 0:L]), n)
                        if r < steps:
                            L, n = span(r % T), made["scores", r]
                            act.wait_ge(negmax_ready, base + r + 1)
                            if r >= 3:
                                full_wait(act, made["turned", r - 3])
                            drained(act.activation(SP1(stage, r)[:, 0:L], bank(n)[:, 0:L], ACT.Exp, bias=MX[:, r % 4, 0:1], scale=scale,
                                                   accum_out=SUM[:, r % 4, 0:1]), n)
                        if stage.kind == "latent" and r < PIECES:
                            gate, room = gate_piece(r)[3:]
                            if r == 4 * T:
                                act.wait_ge(pool_cleared, 3 * stage.turn + 1)
                            settle(act.activation(room, gate, ACT.Exp, scale=-1.0))
                            act.activation(room, room, ACT.Identity, bias=1.0).then_inc(gate_exp, 1)

                if stage.kind == "gla":
                    f_z, f_b, f_last, f_dec = f0 + 1, f0 + 3, f0 + 5, f0 + 7
                    full_wait(act, f0)
                    act.wait_ge(pool_cleared, 3 * stage.turn + 2)
                    drained(act.copy(GLT[0:16, :], bank(f0)[0:16, :]), f0)
                    act.wait_ge(soft_in, 2 * (stage.turn + 1))
                    soft = SOFT.rearrange("p t n -> p (t n)")
                    settle(act.activation(soft, soft, ACT.Exp))
                    act.activation(soft, soft, ACT.Ln, bias=1.0).then_inc(soft_log, 1)
                    for j in range(2):
                        n = f_b + j
                        full_wait(act, n)
                        b = bank(n)[:, 0:2 * GQK]
                        act.activation(QD[:, 2 * j:2 * j + 2, :].rearrange("p t n -> p (t n)"), b, ACT.Exp)
                        act.activation(KI[:, 2 * j:2 * j + 2, :].rearrange("p t n -> p (t n)"), b, ACT.Exp, scale=-1.0)
                        drained(act.copy(KE[:, 2 * j:2 * j + 2, :].rearrange("p t n -> p (t n)"), b), n)
                    full_wait(act, f_dec)
                    drained(act.activation(DEC[0:GDK, :], bank(f_dec)[0:GDK, 0:32], ACT.Exp), f_dec)
                    act.wait_ge(decayed, 3 * stage.turn + 1)
                    act.activation(KE.rearrange("p t n -> p (t n)"), KE.rearrange("p t n -> p (t n)"), ACT.Exp).then_inc(decays_ready, 1)
                    for h in range(GH):
                        n = f0 + 8 + 2 * h
                        full_wait(act, n)
                        drained(act.copy(GQT[0:GDK, h, :], bank(n)[0:GDK, :]), n)
                    for h in range(GH):
                        n = gla_fill(stage, "outputs", h)
                        full_wait(act, n)
                        drained(act.copy(XN[:, :, h * GDV:(h + 1) * GDV], bank(n)[:, 0:T * GDV].rearrange("p (t n) -> p t n", t=T)), n)
                    for h in range(GH):
                        drained_wait(act, gla_fill(stage, "outputs", h))
                    act.activation(GLA_SQUARES.rearrange("p (t n) -> p t n", t=T), XN[:, :, 0:GV], ACT.Square).then_inc(squares_ready, 1)
                    for i in range(2):
                        unit_high(product_after(stage, 3), i)

        @block.gpsimd
        def _(pool):
            own = [0]

            def settle(instruction):
                own[0] += 1
                instruction.then_inc(pool_done, 1)
                pool.wait_ge(pool_done, own[0])

            def rstd(n, width, eps, ready):
                settle(pool.tensor_scalar(RSTD[:, 0:n], SUMSQ[:, 0:n], 1.0 / width, eps, ALU.mult, ALU.add))
                pool.tensor_tensor(RSTD[:, 0:n], RSTD[:, 0:n], const("minus_half")[:, 0:n], ALU.pow).then_inc(ready, 1)

            def silu_piece(stage, n):
                j, t, cols, gate, room = gate_piece(n)
                pool.wait_ge(gate_reciprocal, PIECES * stage.turn + n + 1)
                settle(pool.tensor_tensor(gate, gate, room, ALU.mult))
                if j == 0:
                    by_head = gate.rearrange("p (h n) -> p h n", h=GH // 2)
                    settle(pool.tensor_tensor(by_head, by_head, GN[:, :].unsqueeze(1).to_broadcast([P, GH // 2, GDV]), ALU.mult))
                if j == 1:
                    settle(pool.tensor_tensor(gate, gate, PR[:, t, C_CB + cols.start:C_CB + cols.stop], ALU.mult))

            def past_only(buf, done):
                for at in STICK_AT:
                    diagonal = buf[:, at:at + P]
                    last = pool.affine_select(out=diagonal, in_=diagonal, compare_op=ALU.is_gt, fill=0.0, base=0, pattern=[[1, P]], channel_multiplier=-1)
                last.then_inc(done, 1)

            pool.wait_ge(inputs_in, 16 * N_FIRST)
            for stage in plan:
                layer = stage.arg
                if stage.kind in ("norm", "final"):
                    pool.wait_ge(sumsq_ready, stage.scaled + 1)
                    rstd(T if stage.kind == "final" else gains(stage)[1], D, 1e-6, rstd_ready)
                if stage.kind == "diff":
                    for j in range(MOD_CHUNKS):
                        drained_wait(pool, stage.fill + diff_fills()["mod", j])
                        pool.dma_start(mod_d[0:1, j * BANK:(j + 1) * BANK], MOD_ROW[j % 2]).then_inc(mod_stored[j % 2], 16)
                if stage.kind == "otrans":
                    pool.wait_ge(group_sums, 1)
                    rstd(T * DIFF_HEADS, P, 1e-5, group_rstd)
                if stage.kind == "latent_up":
                    pool.wait_ge(squares_ready, squares_before(stage) + 1)
                    rstd(2 * T, RANK, 1e-6, group_rstd)
                if stage.kind == "latent":
                    pool.wait_ge(mixer_in, 96 * (stage.turn + 1))
                    for n in range(PIECES):
                        silu_piece(stage, n)
                        if n == 2 * T - 1:
                            pool.sem_inc(pool_cleared, 1)
                if stage.kind == "gla":
                    for n in range(stage.fill - BANKS, stage.fill):
                        drained_wait(pool, n)
                    pool.memset(GLT[0:32, :], 1.0).then_inc(pool_cleared, 1)
                    pool.memset(SCR[:, 3616:3616 + 2 * BANK], 0.0).then_inc(pool_cleared, 1)
                    pool.wait_ge(group_sums, 2 + stage.turn)
                    rstd(T * GH, GDV, 1e-6, group_rstd)
                if stage.kind == "stick":
                    for g in range(SB_HEADS + 1):
                        if g < SB_HEADS:
                            pool.wait_ge(sp_raw, g + 1)
                            past_only(E_BUF[g % 2], sp_ready)
                        if g:
                            pool.wait_ge(a_raw, g)
                            past_only(A_BUF[(g - 1) % 2], a_ready)
                if stage.kind == "experts":
                    s = blocks[layer]
                    pool.wait_ge(blocks_ready, layer + 1)
                    pool.wait_ge(xn_stored, 16 * T * (layer + 1))
                    n_blocks = pool.value_load(CTRL[0:1, 0:1], min_val=MIN_BLOCKS, max_val=MAX_BLOCKS)
                    settle(pool.memset(XG, 0.0))

                    def gather(list_ready):
                        list_ready()
                        pool.indirect_dma_start(out=XG, out_offset=None, in_=xn_d, in_offset=bass.IndirectOffsetOnAxis(ap=ROWS_IN[:, 0:1], axis=0),
                                                bounds_check=S - 1, oob_is_err=False).then_inc(s.gathered, 16)

                    def rows_low(b, half):
                        chunks = slice(4 * half, 4 * half + 4)
                        pool.wait_ge(s.rows_high, 2 * b + half + 1)
                        pool.tensor_tensor(XGT_LOW[:, chunks, :], XGT[:, chunks, :], XGT_HIGH[:, chunks, :].bitcast(F32), ALU.subtract).then_inc(s.rows_low, 1)

                    def late_low(b, n):
                        pool.wait_ge(s.high_ready, PARTS * b + n + 1)
                        pool.tensor_tensor(LOW[n], LOADED[n], HIGH[n].bitcast(F32), ALU.subtract).then_inc(s.late_low_ready, 1)

                    pool.tensor_copy(ROWS_IN[:, :], TABI[:, 0, 0:1]).then_inc(s.in_listed, 1)
                    gather(lambda: pool.wait_ge(s.in_listed, 1))
                    rows_low(0, 0)
                    rows_low(0, 1)
                    pool.wait_ge(s.gathered, 16)
                    pool.wait_ge(s.rows_turned, 2)
                    pool.tensor_copy(ROWS_IN[:, :], TABI[:, 0, 1:2]).then_inc(s.in_listed, 1)
                    gather(lambda: pool.wait_ge(s.in_listed, 2))
                    pool.dma_start(TICK[:, :], TABI[:, 0, 0:1]).then_inc(s.scattered, 16)
                    pool.wait_ge(s.scattered, 16)
                    pool.tensor_copy(TICK[:, :], TABI[:, 0, 0:1]).then_inc(s.carried, 1)
                    with pool.Fori(0, n_blocks) as b:
                        late_low(b, 4)
                        pool.wait_ge(s.scattered, 16 * b + 16)
                        pool.tensor_copy(ROWS_OUT[:, :], TABI[:, 1, bass.ds(b, 1)]).then_inc(s.out_listed, 1)
                        pool.sem_inc(s.y_free, 1)
                        late_low(b, 5)
                        pool.wait_ge(s.gathered, 16 * b + 32)
                        pool.tensor_copy(ROWS_IN[:, :], TABI[:, 0, bass.ds(b + 2, 1)]).then_inc(s.in_listed, 1)
                        rows_low(b + 1, 0)
                        rows_low(b + 1, 1)
                        pool.wait_ge(s.rows_turned, 2 * b + 4)
                        pool.wait_ge(s.in_listed, b + 3)
                        pool.wait_ge(s.carried, 2 * b + 1)
                        pool.tensor_copy(TICK[:, :], TABI[:, 0, bass.ds(b, 1)]).then_inc(s.carried, 1)
                        gather(lambda: None)
                        pool.wait_ge(s.y_left, b + 2)
                        pool.wait_ge(s.y_right, b + 2)
                        pool.wait_ge(s.out_listed, b + 1)
                        pool.wait_ge(s.carried, 2 * b + 2)
                        pool.tensor_copy(TICK[:, :], TABI[:, 1, bass.ds(b + 1, 1)]).then_inc(s.carried, 1)
                        pool.indirect_dma_start(out=y_d, out_offset=bass.IndirectOffsetOnAxis(ap=ROWS_OUT[:, 0:1], axis=0), in_=YB, in_offset=None,
                                                bounds_check=2 * S - 1, oob_is_err=False).then_inc(s.scattered, 16)
                    pool.wait_ge(s.scattered, 16 * n_blocks + 16)
                    pool.wait_ge(s.gathered, 16 * n_blocks + 32)
                    pool.wait_ge(s.carried, 2 * n_blocks + 1)
                    pool.tensor_copy(TICK[:, :], TABI[:, 0, bass.ds(n_blocks, 1)]).then_inc(experts_over, 1)

        @block.vector
        def _(dve):
            own = [0]

            def settle(instruction):
                own[0] += 1
                instruction.then_inc(dve_done, 1)
                dve.wait_ge(dve_done, own[0])

            def drained(instruction, n):
                instruction.then_inc(bank_drained[n % BANKS], 1)

            def unit_low_half(stage, i):
                if i == stage.units:
                    return
                u, width = stage.load + 2 * i, unit_width(stage, i)
                loaded_wait(dve, u + 1)
                dve.tensor_tensor(rounded_slot(u, width), slot(u, width), rounded_slot(u + 1, width).bitcast(F32), ALU.subtract).then_inc(unit_low, 1)

            def chunk_low_half(product, k):
                dve.wait_ge(chunk_high, product.splits_before + k + 1)
                dve.tensor_tensor(HT_LOW[:, k, :], HT[:, k, :], HT_HIGH[:, k, :].bitcast(F32), ALU.subtract).then_inc(chunk_low, 1)

            dve.wait_ge(inputs_in, 16 * N_FIRST)
            dve.wait_ge(act_prepared, 1)
            settle(dve.tensor_scalar_add(CCOL[:, 2, :], CCOL[:, 1, :], 1.0))
            settle(dve.reciprocal(CCOL[:, 3, :], CCOL[:, 2, :]))
            settle(dve.tensor_tensor(CCOL[:, 2, :], CCOL[:, 3, :], CCOL[:, 0, :], ALU.mult))
            dve.tensor_copy(CB, CCOL[:, 2, :].unsqueeze(2).to_broadcast([P, KD, P])).then_inc(dve_prepared, 1)
            dve.wait_ge(late_inputs_in, 16 * N_LATE)
            settle(dve.tensor_tensor(LAMV[:, 0, :], LAMV[:, 0, :], LAMV[:, 1, :], ALU.mult))
            settle(dve.tensor_tensor(LAMV[:, 2, :], LAMV[:, 2, :], LAMV[:, 3, :], ALU.mult))
            dve.reduce_sum(LAM[:, 0:1], LAMV[:, 0, :], AX)
            dve.reduce_sum(LAM[:, 1:2], LAMV[:, 2, :], AX).then_inc(dve_prepared, 1)
            settle(dve.tensor_scalar(SUBG[:, 1:2], SUBG[:, 0:1], 1.0 - DIFF_LAMBDA_INIT, None, ALU.mult))

            for stage in plan:
                f0, layer = stage.fill, stage.arg

                if stage.kind == "mod" and layer == 0:
                    for which, part in enumerate((2, 5)):
                        for half in range(2):
                            n = f0 + 2 * part + half
                            full_wait(dve, n)
                            drained(dve.tensor_copy(GB[:, which, half * BANK:(half + 1) * BANK], bank(n)), n)
                    dve.wait_ge(act_prepared, 2)
                    settle(dve.tensor_tensor(LAM[:, 4:5], LAM[:, 3:4], LAM[:, 2:3], ALU.subtract))
                    settle(dve.tensor_scalar_add(LAM[:, 5:6], LAM[:, 4:5], -DIFF_LAMBDA_INIT))
                    full_wait(dve, f0 + 12)
                if stage.kind == "mod":
                    cols = bank(f0 + 12)[:, 0:4 * KD].rearrange("p (q k) -> p q k", q=4)
                    if layer == 1:
                        dve.wait_ge(mod_columns_in, 64)
                        cols = MODC
                    dve.tensor_copy(COLS[:, 0, :], cols[:, 0, :])
                    dve.tensor_copy(COLS[:, 2, :], cols[:, 2, :])
                    dve.scalar_tensor_tensor(COLS[:, 1, :], cols[:, 1, :], 1.0, GCOL[:, layer, :], ALU.add, ALU.mult)
                    last = dve.scalar_tensor_tensor(COLS[:, 3, :], cols[:, 3, :], 1.0, GCOL[:, 2 + layer, :], ALU.add, ALU.mult)
                    if layer == 0:
                        drained(last, f0 + 12)
                        drained_wait(dve, f0 + 12)
                    else:
                        settle(last)

                if stage.kind == "norm":
                    src, tiles, gain, shift = gains(stage)
                    dve.wait_ge(rstd_ready, stage.scaled + 1)
                    for t in range(tiles):
                        dve.tensor_scalar(XN[:, t, :], src[:, t, :], RSTD[:, t:t + 1], None, ALU.mult).then_inc(xn_ready, 1)
                    product = product_after(stage)
                    if product:
                        unit_low_half(product, 0)
                    for k in range(1, KD, 2):
                        n = f0 + k
                        full_wait(dve, n)
                        src_ap, dst = bank(n)[:, 0:tiles * P], HT[:, k, 0:tiles * P]
                        if shift is None:
                            drained(dve.tensor_scalar(dst, src_ap, gain[:, k:k + 1], None, ALU.mult), n)
                        else:
                            drained(dve.tensor_scalar(dst, src_ap, gain[:, k:k + 1], shift[:, k:k + 1], ALU.mult, ALU.add), n)
                        if product:
                            chunk_low_half(product, k - 1)
                            chunk_low_half(product, k)

                if stage.kind == "final":
                    dve.wait_ge(rstd_ready, stage.scaled + 1)
                    dve.wait_ge(gain_in, 16 * (stage.turn + 1))
                    for t in range(T):
                        dve.scalar_tensor_tensor(X[:, t, :], X[:, t, :], RSTD[:, t:t + 1], GB[:, 0, :], ALU.mult, ALU.mult).then_inc(residual_written, 1)

                if stage.kind == "qkv":
                    unit_low_half(stage, 1)
                    unit_low_half(stage, 2)
                    for j in range(8):
                        if j % T == 0:
                            unit_low_half(stage, 3 + j // T)
                        full_wait(dve, f0 + 8 + j)
                        drained(dve.tensor_copy(KT[:, j, :], bank(f0 + 8 + j)), f0 + 8 + j)
                    unit_low_half(stage, 5)
                    for j in range(1, 8, 2):
                        n = f0 + 16 + j
                        full_wait(dve, n)
                        drained(dve.tensor_copy(V[:, j % T, (j // T) * BANK:(j // T + 1) * BANK], bank(n)), n)

                if stage.kind == "diff":
                    made = {what_s: f0 + n for what_s, n in diff_fills().items()}
                    steps = DIFF_HEADS * T
                    for r in range(steps + 1):
                        j = (r - AHEAD - 2) // 2
                        if r % 2 == 0 and 0 <= j < MOD_CHUNKS:
                            n = made["mod", j]
                            full_wait(dve, n)
                            dve.wait_ge(bias_row_in[j % 2], 16 * (j // 2 + 1))
                            if j >= 2:
                                dve.wait_ge(mod_stored[j % 2], 16 * (j // 2))
                            drained(dve.tensor_tensor(MOD_ROW[j % 2], bank(n)[0:1, :], BIAS_ROW[j % 2], ALU.add), n)
                        if r < steps:
                            h, i = divmod(r, T)
                            L, slope = P * (i + 1), 2.0 ** (-8.0 * (h + 1) / DIFF_HEADS)
                            if r >= 3:
                                full_wait(dve, made["turned", r - 3])
                            for m in range(2):
                                n = made[f"map{m}", r]
                                full_wait(dve, n)
                                drained(dve.scalar_tensor_tensor(SA(r)[:, m, 0:L], const("alibi")[:, S - L:S], slope, bank(n)[:, 0:L], ALU.mult, ALU.add), n)
                            for m in range(2):
                                drained_wait(dve, made[f"map{m}", r])
                            dve.tensor_reduce(MX[:, r % 3, :], SA(r)[:, :, 0:L], AX, ALU.max, negate=True).then_inc(negmax_ready, 1)
                        s = r - 1
                        if s >= 0:
                            L = P * (s % T + 1)
                            dve.wait_ge(diff_exp, 2 * (s + 1))
                            settle(dve.reciprocal(RCP[:, s % 3, :], SUM[:, s % 3, :]))
                            settle(dve.tensor_tensor(RCP[:, s % 3, 1:2], RCP[:, s % 3, 1:2], LAM[:, 5:6], ALU.mult))
                            settle(dve.tensor_scalar(SA(s)[:, 0, 0:L], SA(s)[:, 0, 0:L], RCP[:, s % 3, 0:1], None, ALU.mult))
                            dve.scalar_tensor_tensor(SA(s)[:, 0, 0:L], SA(s)[:, 1, 0:L], RCP[:, s % 3, 1:2], SA(s)[:, 0, 0:L], ALU.mult, ALU.add).then_inc(diff_ready, 1)

                if stage.kind == "otrans":
                    for stored_rows in mod_stored:
                        dve.wait_ge(stored_rows, 16 * MOD_CHUNKS // 2)

                if stage.kind == "stick":
                    def clamp(g):
                        dve.wait_ge(z_full, g + 1)
                        if g >= 2:
                            dve.wait_ge(r_full, g - 1)
                        dve.tensor_scalar(E_BUF[g % 2], stick_view(g)[:, 0:STICK_W], 30.0, None, ALU.min).then_inc(z_clamped, 1)

                    clamp(0)
                    for g in range(SB_HEADS):
                        dve.wait_ge(z_log, g + 1)
                        dve.tensor_tensor(E_BUF[g % 2], E_BUF[g % 2], stick_view(g)[:, 0:STICK_W], ALU.max).then_inc(sp_raw, 1)
                        if g + 1 < SB_HEADS:
                            clamp(g + 1)
                        if g % 2 and g >= 3:
                            c = g // 2 - 1
                            dve.wait_ge(o_full, 2 * c + 2)
                            dve.tensor_copy(HT[:, c, :], PS[:, 6 + c % 2, :]).then_inc(o_drained, 1)
                    c = SB_HEADS // 2 - 1
                    dve.wait_ge(o_full, SB_HEADS)
                    dve.tensor_copy(HT[:, c, :], PS[:, 6 + c % 2, :]).then_inc(o_drained, 1)

                if stage.kind == "otrans":
                    for t in range(T):
                        dve.wait_ge(squares_ready, t + 1)
                        last = dve.reduce_sum(SUMSQ[:, t * DIFF_HEADS:(t + 1) * DIFF_HEADS], HT[:, 2 * t:2 * t + 2, :].rearrange("p a (h n) -> p (a h) n", h=4), AX)
                    last.then_inc(group_sums, 1)
                    unit_low_half(product_after(stage), 0)
                    dve.wait_ge(group_rstd, stage.grouped + 1)
                    for t in range(T):
                        o = XN[:, t, :].rearrange("p (h n) -> p h n", h=DIFF_HEADS)
                        r = RSTD[:, t * DIFF_HEADS:(t + 1) * DIFF_HEADS].unsqueeze(2).to_broadcast([P, DIFF_HEADS, P])
                        dve.tensor_tensor(o, o, r, ALU.mult).then_inc(group_normed, 1)

                if stage.kind in ("otrans", "mtrans", "xtrans"):
                    for c in range(1, XH if stage.kind == "xtrans" else KD, 2):
                        n = f0 + c
                        full_wait(dve, n)
                        if stage.kind == "otrans":
                            drained(dve.tensor_scalar(HT[:, c, :], bank(n), SUBG[:, 1:2], None, ALU.mult), n)
                        else:
                            drained(dve.tensor_copy(HT[:, c, :], bank(n)), n)
                        if product_after(stage):
                            chunk_low_half(product_after(stage), c - 1)
                            chunk_low_half(product_after(stage), c)
                    if product_after(stage):
                        unit_low_half(product_after(stage), 1)

                if stage.kind in ("attn_out", "mix_out", "x_out"):
                    if stage.kind == "attn_out" and layer == 1:
                        dve.wait_ge(mod_gates_in, 32)
                    for t in range(T):
                        for half in range(2):
                            n = f0 + 2 * t + half
                            cols = slice(half * BANK, (half + 1) * BANK)
                            full_wait(dve, n)
                            if stage.kind == "attn_out":
                                gated_y = SCR[:, 5120 + half * BANK:5120 + (half + 1) * BANK]
                                settle(dve.tensor_tensor(gated_y, bank(n), GB[:, 0, cols], ALU.mult))
                                drained(dve.tensor_tensor(X[:, t, cols], X[:, t, cols], gated_y, ALU.add), n)
                            else:
                                drained(dve.tensor_tensor(X[:, t, cols], X[:, t, cols], bank(n), ALU.add), n)

                if stage.kind == "route":
                    def over(name, n, inner=None):
                        v = RT(name).unsqueeze(2)
                        return v.to_broadcast([P, T, n])

                    def first_of(values, top, hot, mark, n):
                        rev = const("rev")[:, 0:n].unsqueeze(1).to_broadcast([P, T, n])
                        settle(dve.tensor_tensor(RT(hot[0]), values, over(top, n), ALU.is_ge))
                        settle(dve.tensor_tensor(RT(hot[0]), RT(hot[0]), rev, ALU.mult))
                        settle(dve.reduce_max(RT(mark), RT(hot[0]), AX))
                        settle(dve.tensor_tensor(RT(hot[1]), RT(hot[0]), over(mark, n), ALU.is_equal))

                    full_wait(dve, f0)
                    logits = RT("logits")
                    drained(dve.tensor_tensor(logits, bank(f0)[:, 0:T * 36].rearrange("p (t n) -> p t n", t=T), RB[:, :].unsqueeze(1).to_broadcast([P, T, 36]), ALU.add), f0)
                    drained_wait(dve, f0)
                    group_logits = logits[:, :, 0:GROUPS]
                    settle(dve.reduce_max(RT("gmax"), group_logits, AX))
                    dve.tensor_tensor(RT("gshift"), group_logits, over("gmax", GROUPS), ALU.subtract).then_inc(group_shift, 1)
                    first_of(group_logits, "gmax", ("gfirst", "group"), "gtop", GROUPS)
                    settle(dve.tensor_tensor(RT("masked"), logits[:, :, GROUPS:].rearrange("p t (g e) -> p t g e", g=GROUPS),
                                             RT("group").unsqueeze(3).to_broadcast([P, T, GROUPS, PER_GROUP]), ALU.mult))
                    settle(dve.reduce_sum(RT("elogits"), RT("masked").rearrange("p t g e -> p t e g"), AX))
                    settle(dve.reduce_max(RT("top1"), RT("elogits"), AX))
                    first_of(RT("elogits"), "top1", ("first1", "hot1"), "mark1", PER_GROUP)
                    settle(dve.scalar_tensor_tensor(RT("rest"), RT("hot1"), NEG, RT("elogits"), ALU.mult, ALU.add))
                    settle(dve.reduce_max(RT("top2"), RT("rest"), AX))
                    first_of(RT("rest"), "top2", ("first2", "hot2"), "mark2", PER_GROUP)
                    dve.tensor_tensor(RT("gap"), RT("top2"), RT("top1"), ALU.subtract).then_inc(pair_diff, 1)
                    for name, hot in (("assign1", "hot1"), ("assign2", "hot2")):
                        settle(dve.tensor_tensor(RT(name).rearrange("p t (g e) -> p t g e", g=GROUPS),
                                                 RT("group").unsqueeze(3).to_broadcast([P, T, GROUPS, PER_GROUP]),
                                                 RT(hot).unsqueeze(2).to_broadcast([P, T, GROUPS, PER_GROUP]), ALU.mult))
                    dve.tensor_tensor(RT("assigned"), RT("assign1"), RT("assign2"), ALU.add).then_inc(assigned, 1)
                    dve.wait_ge(group_exp, layer + 1)
                    settle(dve.reduce_sum(RT("gsum"), RT("gexp"), AX))
                    settle(dve.reciprocal(RT("gweight"), RT("gsum")))
                    dve.wait_ge(pair_exp, layer + 1)
                    settle(dve.tensor_scalar_add(RT("total"), RT("gapexp"), 1.0))
                    settle(dve.reciprocal(RT("share"), RT("total")))
                    settle(dve.tensor_tensor(WTS[:, 0, :], RT("share"), RT("gweight"), ALU.mult))
                    settle(dve.tensor_tensor(WTS[:, 1, :], WTS[:, 0, :], RT("gapexp"), ALU.mult))
                    full_wait(dve, f0 + 1)
                    dve.tensor_copy(RT("rank"), bank(f0 + 1)[:, 0:T * EXPERTS].rearrange("p (t n) -> p t n", t=T))
                    drained(dve.tensor_copy(RT("count"), bank(f0 + 1)[:, T * EXPERTS:(T + 1) * EXPERTS]), f0 + 1)
                    drained_wait(dve, f0 + 1)
                    settle(dve.tensor_scalar(RT("nblocks"), RT("count"), 0.5, None, ALU.is_gt))
                    for m in range(1, T):
                        settle(dve.scalar_tensor_tensor(RT("nblocks"), RT("count"), P * m + 0.5, RT("nblocks"), ALU.is_gt, ALU.add))
                    settle(dve.tensor_tensor_scan(RT("upto"), ones[:, 0:EXPERTS], RT("nblocks"), 0.0, ALU.mult, ALU.add))
                    settle(dve.tensor_tensor(RT("first"), RT("upto"), RT("nblocks"), ALU.subtract))
                    settle(dve.tensor_scalar(RT("over"), RT("rank"), P - 0.5, None, ALU.is_gt))
                    for m in range(2, T):
                        settle(dve.scalar_tensor_tensor(RT("over"), RT("rank"), P * m - 0.5, RT("over"), ALU.is_gt, ALU.add))
                    settle(dve.scalar_tensor_tensor(RT("place"), RT("over"), -float(P), RT("rank"), ALU.mult, ALU.add))
                    settle(dve.tensor_tensor(RT("blockof"), RT("over"), RT("first").unsqueeze(1).to_broadcast([P, T, EXPERTS]), ALU.add))
                    for j in range(2):
                        for of, value in (("places_of", "place"), ("blocks_of", "blockof")):
                            settle(dve.tensor_tensor(RT("picked"), RT(f"assign{j + 1}"), RT(value), ALU.mult))
                            settle(dve.reduce_sum(RT(of)[:, j, :], RT("picked"), AX))
                    for t in range(T):
                        for j in range(2):
                            dve.tensor_scalar(RT("places")[:, 2 * t + j, :], const("iota"), RT("places_of")[:, j, t:t + 1], None, ALU.is_equal)
                            last = dve.tensor_scalar(RT("blocks")[:, 2 * t + j, :], const("iota")[:, 0:TABLE], RT("blocks_of")[:, j, t:t + 1],
                                                     const("row_id")[:, 2 * t + j:2 * t + j + 1], ALU.is_equal, ALU.mult)
                    last.then_inc(one_hots, 1)
                    upto, past = RT("upto")[0:1, :], RT("past")[0:1]
                    settle(dve.tensor_tensor(past, upto.unsqueeze(1).to_broadcast([1, MAX_BLOCKS, EXPERTS]),
                                             const("iota")[0:1, 0:MAX_BLOCKS].unsqueeze(2).to_broadcast([1, MAX_BLOCKS, EXPERTS]), ALU.is_le))
                    settle(dve.reduce_sum(RT("expert")[0:1, :], past, AX))
                    settle(dve.tensor_scalar_min(RT("expert")[0:1, :], RT("expert")[0:1, :], float(EXPERTS - 1)))
                    dve.tensor_copy(CTRL[0:1, 1:1 + MAX_BLOCKS], RT("expert")[0:1, :])
                    dve.tensor_scalar_add(CTRL[0:1, MAX_BLOCKS + 1:MAX_BLOCKS + 2], upto[:, EXPERTS - 1:EXPERTS], -1.0)
                    settle(dve.tensor_copy(CTRL[0:1, 0:1], upto[:, EXPERTS - 1:EXPERTS]))
                    full_wait(dve, f0 + 2)
                    raw = bank(f0 + 2)[:, 0:TABLE]
                    settle(dve.tensor_scalar(RT("empty"), raw, 0.0, BIG, ALU.is_equal, ALU.mult))
                    drained(dve.scalar_tensor_tensor(RT("target"), raw, -1.0, RT("empty"), ALU.add, ALU.add), f0 + 2)
                    drained_wait(dve, f0 + 2)
                    settle(dve.tensor_scalar(RT("source"), RT("target"), S - 0.5, -float(S), ALU.is_gt, ALU.mult))
                    settle(dve.tensor_tensor(RT("source"), RT("source"), RT("target"), ALU.add))
                    dve.tensor_copy(TABI[:, 0, :], RT("source"))
                    dve.tensor_copy(TABI[:, 1, :], RT("target")).then_inc(blocks_ready, 1)

                if stage.kind == "experts":
                    s = blocks[layer]
                    gain, shift = COLS[:, 3, :], COLS[:, 2, :]

                    def last_chunks():
                        for k in range(KD // 2, KD):
                            last = dve.tensor_scalar(XGT[:, k, :], PS[:, k // 4, (k % 4) * P:(k % 4 + 1) * P], gain[:, k:k + 1], shift[:, k:k + 1], ALU.mult, ALU.add)
                        last.then_inc(s.last_scaled, 1)

                    def low(b, n):
                        dve.wait_ge(s.high_ready, PARTS * b + n + 1)
                        dve.tensor_tensor(LOW[n], LOADED[n], HIGH[n].bitcast(F32), ALU.subtract).then_inc(s.low_ready, 1)

                    dve.wait_ge(blocks_ready, layer + 1)
                    last_block = dve.value_load(CTRL[0:1, MAX_BLOCKS + 1:MAX_BLOCKS + 2], min_val=MIN_BLOCKS - 1, max_val=MAX_BLOCKS - 1)
                    dve.sem_inc(s.hidden, 1)
                    dve.wait_ge(s.rows_turned, 2)
                    last_chunks()
                    for n in range(4):
                        low(0, n)
                    def one_block(b, more):
                        dve.wait_ge(s.gate_exp, b + 1)
                        dve.tensor_scalar_add(GE, GE, 1.0).then_inc(s.silu_steps, 1)
                        dve.wait_ge(s.silu_steps, 3 * b + 1)
                        dve.reciprocal(GR, GE).then_inc(s.silu_steps, 1)
                        dve.wait_ge(s.silu_steps, 3 * b + 2)
                        dve.tensor_tensor(GR, GR, PS[:, 2, :], ALU.mult).then_inc(s.silu_steps, 1)
                        dve.wait_ge(s.silu_steps, 3 * b + 3)
                        dve.wait_ge(s.used[3], b + 2)
                        dve.tensor_tensor(HID, GR, PS[:, 3, :], ALU.mult).then_inc(s.hidden, 1)
                        dve.wait_ge(s.hidden_high, b + 1)
                        dve.tensor_tensor(HIDT_LOW, PS[:, 4, :], HIDT_HIGH.bitcast(F32), ALU.subtract).then_inc(s.hidden_low, 1)
                        dve.wait_ge(s.rows_low, 2 * b + 2)
                        dve.wait_ge(s.rows_turned, 2 * b + 4)
                        last_chunks()
                        for n in range(4) if more else ():
                            low(b + 1, n)

                    with dve.Fori(0, last_block) as b:
                        one_block(b, True)
                    one_block(last_block, False)
                    dve.drain().then_inc(experts_over, 1)

                if stage.kind == "combine":
                    for t in range(T):
                        dve.wait_ge(rows_back[t], 32 * (layer + 1))
                        dve.wait_ge(weighted, T * layer + t + 1)
                        y1, y2 = Y2[:, 0, t, :], Y2[:, 1, t, :]
                        settle(dve.scalar_tensor_tensor(y1, y2, WTS[:, 1, t:t + 1], y1, ALU.mult, ALU.add))
                        settle(dve.tensor_tensor(y1, y1, GB[:, 1, :], ALU.mult))
                        dve.tensor_tensor(X[:, t, :], X[:, t, :], y1, ALU.add).then_inc(residual_written, 1)

                if stage.kind == "project":
                    for j, (at, width) in enumerate(IN_CHUNKS):
                        unit_low_half(stage, j + 1)
                        for t in range(1, T, 2):
                            n = f0 + T * j + t
                            full_wait(dve, n)
                            drained(dve.tensor_copy(PR[:, t, at:at + width], bank(n)[:, 0:width]), n)

                if stage.kind == "latent_up":
                    for n in range(f0 - BANKS, f0):
                        drained_wait(dve, n)
                    if stage.turn == 0:
                        pos, turns, wide = SIN_T[0], SIN_T[1], SIN_T[2]
                        settle(dve.tensor_copy(POSF[:, :], POSI[:, :]))
                        settle(dve.tensor_tensor(pos, POSF[:, :].unsqueeze(2).to_broadcast([P, T, ROPE // 2]),
                                                 const("inv_freq").unsqueeze(1).to_broadcast([P, T, ROPE // 2]), ALU.mult))
                        for dst, quarter in ((SIN, 0.0), (COS, 0.25)):
                            settle(dve.tensor_scalar(turns, pos, 1.0 / (2 * math.pi), quarter, ALU.mult, ALU.add))
                            settle(dve.tensor_scalar_add(turns, turns, ROUNDER))
                            settle(dve.tensor_scalar_add(turns, turns, -ROUNDER))
                            settle(dve.scalar_tensor_tensor(wide, turns, -TURN[0], pos, ALU.mult, ALU.add))
                            settle(dve.scalar_tensor_tensor(wide, turns, -TURN[1], wide, ALU.mult, ALU.add))
                            settle(dve.scalar_tensor_tensor(wide, turns, -TURN[2], wide, ALU.mult, ALU.add))
                            if quarter:
                                settle(dve.tensor_scalar_add(wide, wide, math.pi / 2))
                            settle(dve.tensor_scalar(dst[:, :, :], wide, PI_BELOW, -PI_BELOW, ALU.min, ALU.max))
                        dve.drain().then_inc(angles, 1)
                    dve.wait_ge(group_rstd, stage.grouped + 1)
                    for t in range(T):
                        for j, at in enumerate((C_CQ, C_CKV)):
                            last = dve.tensor_scalar(PR[:, t, at:at + RANK], PR[:, t, at:at + RANK], RSTD[:, j * T + t:j * T + t + 1], None, ALU.mult)
                        last.then_inc(group_normed, 1)
                    dve.wait_ge(mixer_in, 96 * (stage.turn + 1))
                    for j in range(4):
                        full_wait(dve, f0 + j)
                        drained(dve.tensor_scalar(HT[:, j, :], bank(f0 + j), RG[:, j // 2, j % 2:j % 2 + 1], None, ALU.mult), f0 + j)
                    for j in range(2 * T):
                        n = f0 + 4 + j
                        t, h = j // 2, 3 * (j % 2)
                        full_wait(dve, n)
                        drained(dve.tensor_copy(QM[:, t, h:h + 3, :], bank(n)[:, 0:3 * MQ].rearrange("p (h n) -> p h n", h=3)), n)
                    for n in range(f0 + 4, f0 + 4 + 4 * T):
                        if n >= f0 + 4 + 4 * T - BANKS or n < f0 + 4 + 2 * T:
                            drained_wait(dve, n)
                    dve.wait_ge(rope_ready, 1)
                    half = ROPE // 2

                    def rotate(dst1, dst2, x1, x2, cos, sin, tmp):
                        for out_ap, a, table in ((tmp[0], x1, cos), (tmp[1], x2, sin), (tmp[2], x2, cos), (tmp[3], x1, sin)):
                            last = dve.tensor_tensor(out_ap, a, table, ALU.mult)
                        settle(last)
                        settle(dve.tensor_tensor(dst1, tmp[0], tmp[1], ALU.subtract))
                        return dve.tensor_tensor(dst2, tmp[2], tmp[3], ALU.add)

                    gb = GB.rearrange("p a n -> p (a n)")
                    for t in range(T):
                        cos = COS[:, t, :].unsqueeze(1).to_broadcast([P, MH, half])
                        sin = SIN[:, t, :].unsqueeze(1).to_broadcast([P, MH, half])
                        q1, q2 = QM[:, t, :, NOPE:NOPE + half], QM[:, t, :, NOPE + half:]
                        tmp = [gb[:, m * 96:(m + 1) * 96].rearrange("p (h n) -> p h n", h=MH) for m in range(4)]
                        settle(rotate(q1, q2, q1, q2, cos, sin, tmp))
                    dve.drain().then_inc(mixer_up, 1)
                    k1, k2 = PR[:, :, C_KR:C_KR + half], PR[:, :, C_KR + half:C_KR + ROPE]
                    tmp = [gb[:, m * 64:(m + 1) * 64].rearrange("p (t n) -> p t n", t=T) for m in range(4)]
                    settle(rotate(k1, k2, k1, k2, COS[:, :, :], SIN[:, :, :], tmp))
                    dve.tensor_copy(KM[:, :, :, NOPE:], PR[:, :, C_KR:C_KR + ROPE].unsqueeze(2).to_broadcast([P, T, MH, ROPE])).then_inc(mixer_up, 1)

                if stage.kind == "xq":
                    for h in range(XH):
                        full_wait(dve, f0 + h)
                        drained(dve.tensor_copy(XQT[:, h, :], bank(f0 + h)), f0 + h)
                if stage.kind == "xkv":
                    for h in range(XH):
                        full_wait(dve, f0 + h)
                        drained(dve.tensor_copy(XKT[:, h, :], bank(f0 + h)[:, 0:MEM]), f0 + h)
                    for t in range(MT):
                        n = f0 + XH + t
                        full_wait(dve, n)
                        drained(dve.tensor_copy(XV[:, t, :], bank(n)), n)

                if stage.kind in ("latent", "xattn"):
                    order, heads, scale, span, dv, o_at = soft_plan(stage)
                    made = {what_s: n for n, what_s in enumerate(order, f0)}
                    steps = heads * T

                    def turned_k(r):
                        if stage.kind == "latent" and r % T == 0 and r < steps:
                            nk = made["turn_k", r]
                            full_wait(dve, nk)
                            if r >= 2 * T:
                                full_wait(dve, made["scores", r - T - 1])
                            drained(dve.tensor_copy(LKT(r // T)[0:MQ, :], bank(nk)[0:MQ, :]), nk)

                    turned_k(0)
                    for r in range(steps + AHEAD + 1):
                        if r < steps:
                            L, n = span(r % T), made["scores", r]
                            full_wait(dve, n)
                            if r >= 4:
                                drained_wait(dve, made["scores", r - 4])
                            settle(dve.tensor_reduce(RCP[:, r % 4, 0:1], bank(n)[:, 0:L], AX, ALU.max, negate=True))
                            dve.tensor_scalar(MX[:, r % 4, 0:1], RCP[:, r % 4, 0:1], scale, None, ALU.mult).then_inc(negmax_ready, 1)
                        turned_k(r + 1)
                        s = r - AHEAD - 1
                        if s >= 0:
                            h, i = divmod(s, T)
                            n = made["values", s]
                            full_wait(dve, n)
                            settle(dve.reciprocal(RCP[:, s % 4, 1:2], SUM[:, s % 4, 0:1]))
                            drained(dve.tensor_scalar(XN[:, i, o_at + h * dv:o_at + (h + 1) * dv], bank(n)[:, 0:dv], RCP[:, s % 4, 1:2], None, ALU.mult), n)
                        if stage.kind == "latent" and 1 <= r <= PIECES:
                            room = gate_piece(r - 1)[4]
                            dve.wait_ge(gate_exp, PIECES * stage.turn + r)
                            dve.reciprocal(room, room).then_inc(gate_reciprocal, 1)

                if stage.kind == "gla":
                    f_z, f_b, f_last = f0 + 1, f0 + 3, f0 + 5
                    for j in range(2):
                        n = f_z + j
                        full_wait(dve, n)
                        z = bank(n)[:, 0:2 * GQK].rearrange("p (t n) -> p t n", t=2)
                        dve.tensor_scalar(SOFT[:, 2 * j:2 * j + 2, :], z, -1.0, 30.0, ALU.mult, ALU.min).then_inc(soft_in, 1)
                    dve.wait_ge(soft_log, stage.turn + 1)
                    for j in range(2):
                        n = f_z + j
                        z = bank(n)[:, 0:2 * GQK].rearrange("p (t n) -> p t n", t=2)
                        soft = SOFT[:, 2 * j:2 * j + 2, :]
                        drained(dve.scalar_tensor_tensor(soft, z, -1.0, soft, ALU.mult, ALU.max), n)
                        drained_wait(dve, n)
                        dve.drain().then_inc(soft_ready, 1)
                    for j in range(2):
                        n = f_last + j
                        full_wait(dve, n)
                        drained_wait(dve, f_b + j)
                        ke = KE[:, 2 * j:2 * j + 2, :]
                        drained(dve.tensor_tensor(ke, bank(n)[:, 0:2 * GQK].rearrange("p (t n) -> p t n", t=2), ke, ALU.subtract), n)
                    drained_wait(dve, f_last)
                    drained_wait(dve, f_last + 1)
                    dve.drain().then_inc(decayed, 1)
                    dve.scalar_tensor_tensor(QD, PR[:, :, C_GQ:C_GQ + GQK], GDK ** -0.5, QD, ALU.mult, ALU.mult)
                    dve.tensor_tensor(KI, PR[:, :, C_GK:C_GK + GQK], KI, ALU.mult).then_inc(decayed, 1)
                    dve.wait_ge(decays_ready, stage.turn + 1)
                    dve.tensor_tensor(KE, PR[:, :, C_GK:C_GK + GQK], KE, ALU.mult).then_inc(decayed, 1)
                    for h in range(GH):
                        n = f0 + 9 + 2 * h
                        full_wait(dve, n)
                        drained(dve.tensor_copy(GKT[0:GDK, h, :], bank(n)[0:GDK, :]), n)
                    dve.wait_ge(pool_cleared, 3 * (stage.turn + 1))
                    drained_wait(dve, f0 + 7)
                    for h in range(GH):
                        if h >= 2:
                            full_wait(dve, gla_fill(stage, "outputs", h - 2))
                        st = GST(h)
                        settle(dve.memset(st[0:GDK, 0, :], 0.0))
                        for j in range(7):
                            n = gla_fill(stage, "update", h, j % 2)
                            if j < 2:
                                full_wait(dve, n)
                            step = dve.scalar_tensor_tensor(st[0:GDK, j + 1, :], st[0:GDK, j, :], DEC[0:GDK, h * 8 + j:h * 8 + j + 1],
                                                            bank(n)[0:GDK, (j // 2) * GDV:(j // 2 + 1) * GDV], ALU.mult, ALU.add)
                            if j in (5, 6):
                                drained(step, n)
                                drained_wait(dve, n)
                            else:
                                settle(step)
                        dve.drain().then_inc(state_ready, 1)
                        n = gla_fill(stage, "scores", h)
                        full_wait(dve, n)
                        drained(dve.copy_predicated(GAT(h), const("gla_mask").bitcast(I32).unsqueeze(1).to_broadcast([P, T, P]),
                                                    bank(n).rearrange("p (t n) -> p t n", t=T)), n)
                    settle(dve.tensor_tensor(CU2, PR[:, :, C_CC:C_CC + CW], PR[:, :, C_CH:C_CH + CW], ALU.mult))
                    for dst, j in ((CU1, 1), (CU0, 0)):
                        last = dve.tensor_tensor(dst, CU2, CWT[:, j, :].unsqueeze(1).to_broadcast([P, T, CW]), ALU.mult)
                    last.then_inc(conv_in, 1)
                    settle(dve.tensor_tensor(CU2, CU2, CWT[:, 2, :].unsqueeze(1).to_broadcast([P, T, CW]), ALU.mult))
                    dve.wait_ge(squares_ready, squares_before(stage) + 1)
                    dve.reduce_sum(SUMSQ[:, 0:T * GH], GLA_SQUARES.rearrange("p (g n) -> p g n", n=GDV), AX).then_inc(group_sums, 1)
                    unit_low_half(product_after(stage, 3), 0)
                    dve.wait_ge(group_rstd, stage.grouped + 1)
                    latent = XN[:, :, GV + CW:]
                    dve.tensor_tensor(latent, latent, PR[:, :, C_MGATE:C_MGATE + MH * MV], ALU.mult).then_inc(mixed, 1)
                    for t in range(T):
                        o = XN[:, t, 0:GV].rearrange("p (h n) -> p h n", h=GH)
                        settle(dve.tensor_tensor(o, o, RSTD[:, t * GH:(t + 1) * GH].unsqueeze(2).to_broadcast([P, GH, GDV]), ALU.mult))
                    dve.tensor_tensor(XN[:, :, 0:GV], XN[:, :, 0:GV], PR[:, :, C_GGATE:C_GGATE + GV], ALU.mult).then_inc(mixed, 1)

                if stage.kind == "conv":
                    for j in range(2):
                        n = f0 + j
                        full_wait(dve, n)
                        part = CU2[:, 2 * j:2 * j + 2, :]
                        drained(dve.tensor_tensor(part, part, bank(n).rearrange("p (t n) -> p t n", t=2), ALU.add), n)
                        drained_wait(dve, n)
                    dve.tensor_tensor(CU2, CU2, PR[:, :, C_CGATE:C_CGATE + CW], ALU.mult).then_inc(mixed, 1)


_INPUTS = ["x", "c", "norm1_g", "norm2_g", "ada_w", "ada_b", "diff_w_in", "diff_w_out", "diff_lambda_q1", "diff_lambda_k1",
           "diff_lambda_q2", "diff_lambda_k2", "diff_subln_g", "sb_w_in", "sb_w_out", "router_group_w", "router_group_b",
           "router_expert_w", "router_expert_b", "expert_w_gate", "expert_w_up", "expert_w_down", "final_norm_g", "mem_2",
           "positions_2", "norm_mix_2", "w_in_2", "gla_w_gate_2", "gla_b_gate_2", "gla_norm_2", "conv_w_2", "mla_q_norm_2",
           "mla_w_uq_2", "mla_kv_norm_2", "mla_w_ukv_2", "w_out_2", "norm_xattn_2", "norm_mem_2", "mem_wq_2", "mem_wk_2",
           "mem_wv_2", "mem_wo_2", "norm_final_2"]


def kernel(**inputs):
    import concourse.bacc as bacc
    from concourse.bass_utils import run_bass_kernel_spmd

    nc = bacc.Bacc("TRN2", target_bir_lowering=False, num_devices=1)
    arrays, args = {}, {}
    given = {name: np.ascontiguousarray(inputs[name]) for name in _INPUTS}
    given["tables"] = shape_constants()[0]
    for name, a in given.items():
        arrays[f"in_{name}"] = a
        args[name] = nc.dram_tensor(f"in_{name}", a.shape, mybir.dt.from_np(a.dtype), kind="ExternalInput").ap()
    out = nc.dram_tensor("out_0", (1, S, D), F32, kind="ExternalOutput").ap()
    build_program(nc, out=out, **args)
    result = run_bass_kernel_spmd(nc, [arrays], core_ids=[0])
    return result.results[0]["out_0"]
```
